# Optimizing a Trainium2 kernel written in Bass

```python
import math
import jax, jax.numpy as jnp
from jax import lax
import numpy as np

D_MODEL = 2048
BATCH = 1
SEQ = 256
DEPTH = 1

N_MEM = 256
N_MIXERS = 2
EXPAND = 2
INNER = EXPAND * D_MODEL
XA_HEADS = 4
XA_WIDTH = INNER // 4
XA_DIM = XA_WIDTH // XA_HEADS
MIX_WIDTH = INNER - XA_WIDTH
DN_HEAD_DIM = 128
DN_V_HEADS = MIX_WIDTH // DN_HEAD_DIM
DN_QK_HEADS = DN_V_HEADS // 2
DN_QK_WIDTH = DN_QK_HEADS * DN_HEAD_DIM
DN_CONV = 4
DN_CHUNK = 64
DN_MIX_COLS = 2 * DN_QK_WIDTH + MIX_WIDTH + 2 * DN_V_HEADS
DN_PROJ = DN_MIX_COLS + XA_WIDTH + INNER
SB_HEAD_DIM = 128
SB_HEADS = MIX_WIDTH // SB_HEAD_DIM
SB_BLOCK = 128
SB_MIX_COLS = 3 * MIX_WIDTH
SB_PROJ = SB_MIX_COLS + XA_WIDTH + INNER
EPS = 1e-6


def rms_norm(x, g):
    xf = x.astype(jnp.float32)
    y = xf * lax.rsqrt(jnp.mean(xf * xf, axis=-1, keepdims=True) + EPS)
    return (y * g.astype(jnp.float32)).astype(x.dtype)

def l2_norm(x):
    xf = x.astype(jnp.float32)
    return (xf * lax.rsqrt(jnp.sum(xf * xf, axis=-1, keepdims=True) + EPS)).astype(x.dtype)

def causal_depthwise_conv(x, w):
    c = x.shape[-1]
    return lax.conv_general_dilated(
        x, w[:, None, :].astype(x.dtype), window_strides=(1,),
        padding=((w.shape[0] - 1, 0),), dimension_numbers=("NWC", "WIO", "NWC"),
        feature_group_count=c)

def gated_delta_rule(q, k, v, g, beta):
    f32 = jnp.float32
    B, H, S, dk = q.shape
    dv = v.shape[-1]
    C, N = DN_CHUNK, S // DN_CHUNK
    q, k, v = (t.astype(f32).reshape(B, H, N, C, t.shape[-1]) for t in (q, k, v))
    g = g.astype(f32).reshape(B, H, N, C)
    beta = beta.astype(f32).reshape(B, H, N, C)
    gc = jnp.cumsum(g, axis=-1)
    idx = jnp.arange(C)
    incl = idx[:, None] >= idx[None, :]
    strict = idx[:, None] > idx[None, :]
    decay = jnp.exp(jnp.where(incl, gc[..., :, None] - gc[..., None, :], -jnp.inf))
    kk = jnp.einsum("bhncd,bhnjd->bhncj", k, k)
    m = jnp.where(strict, beta[..., :, None] * kk * decay, 0.0) + jnp.eye(C, dtype=f32)
    rhs = jnp.concatenate([v * beta[..., None], k * (beta * jnp.exp(gc))[..., None]], axis=-1)
    sol = lax.linalg.triangular_solve(m, rhs, left_side=True, lower=True, unit_diagonal=True)
    u0, w = sol[..., :dv], sol[..., dv:]
    qk = jnp.einsum("bhncd,bhnjd->bhncj", q, k) * decay
    q_dec = q * jnp.exp(gc)[..., None]
    k_dec = k * jnp.exp(gc[..., -1:] - gc)[..., None]
    chunk_decay = jnp.exp(gc[..., -1])

    def step(state, inp):
        u0_c, w_c, qk_c, qd_c, kd_c, cd_c = inp
        u = u0_c - jnp.einsum("bhcd,bhde->bhce", w_c, state)
        o = jnp.einsum("bhcd,bhde->bhce", qd_c, state) + jnp.einsum("bhcj,bhje->bhce", qk_c, u)
        state = cd_c[..., None, None] * state + jnp.einsum("bhcd,bhce->bhde", kd_c, u)
        return state, o

    xs = tuple(jnp.moveaxis(t, 2, 0) for t in (u0, w, qk, q_dec, k_dec, chunk_decay))
    _, o = lax.scan(step, jnp.zeros((B, H, dk, dv), f32), xs)
    return jnp.moveaxis(o, 0, 2).reshape(B, H, S, dv)

def deltanet_branch(p, conv_w, a_log, dt_bias, out_g):
    B, S, _ = p.shape
    c_qkv = 2 * DN_QK_WIDTH + MIX_WIDTH
    qkv = jax.nn.silu(causal_depthwise_conv(p[..., :c_qkv], conv_w))
    q = qkv[..., :DN_QK_WIDTH].reshape(B, S, DN_QK_HEADS, DN_HEAD_DIM)
    k = qkv[..., DN_QK_WIDTH:2 * DN_QK_WIDTH].reshape(B, S, DN_QK_HEADS, DN_HEAD_DIM)
    v = qkv[..., 2 * DN_QK_WIDTH:].reshape(B, S, DN_V_HEADS, DN_HEAD_DIM)
    a = p[..., c_qkv:c_qkv + DN_V_HEADS].astype(jnp.float32)
    b = p[..., c_qkv + DN_V_HEADS:].astype(jnp.float32)
    rep = DN_V_HEADS // DN_QK_HEADS
    q = jnp.repeat(l2_norm(q), rep, axis=2) * DN_HEAD_DIM ** -0.5
    k = jnp.repeat(l2_norm(k), rep, axis=2)
    g = -jnp.exp(a_log.astype(jnp.float32)) * jax.nn.softplus(a + dt_bias.astype(jnp.float32))
    beta = jax.nn.sigmoid(b)
    o = gated_delta_rule(q.transpose(0, 2, 1, 3), k.transpose(0, 2, 1, 3), v.transpose(0, 2, 1, 3),
                         g.transpose(0, 2, 1), beta.transpose(0, 2, 1))
    o = rms_norm(o.astype(p.dtype), out_g)
    return o.transpose(0, 2, 1, 3).reshape(B, S, MIX_WIDTH)

def stick_breaking_attention(q, k, v):
    B, H, S, d = q.shape
    scale = d ** -0.5
    outs = []
    for blk in range(S // SB_BLOCK):
        q0 = blk * SB_BLOCK
        kv_len = q0 + SB_BLOCK
        qb = q[:, :, q0:kv_len]
        kb, vb = k[:, :, :kv_len], v[:, :, :kv_len]
        z = jnp.einsum("bhtd,bhsd->bhts", qb, kb).astype(jnp.float32) * scale
        t_pos = q0 + jnp.arange(SB_BLOCK)
        s_pos = jnp.arange(kv_len)
        mask = s_pos[None, :] < t_pos[:, None]
        log_rest = jnp.where(mask, jax.nn.log_sigmoid(-z), 0.0)
        later = lax.cumsum(log_rest, axis=3, reverse=True) - log_rest
        wts = jnp.where(mask, jnp.exp(jax.nn.log_sigmoid(z) + later), 0.0)
        outs.append(jnp.einsum("bhts,bhsd->bhtd", wts.astype(v.dtype), vb))
    return jnp.concatenate(outs, axis=2)

def stick_breaking_branch(p, qn_g, kn_g):
    B, S, _ = p.shape
    q, k, v = (t.reshape(B, S, SB_HEADS, SB_HEAD_DIM) for t in jnp.split(p, 3, axis=-1))
    q, k = rms_norm(q, qn_g), rms_norm(k, kn_g)
    o = stick_breaking_attention(q.transpose(0, 2, 1, 3), k.transpose(0, 2, 1, 3), v.transpose(0, 2, 1, 3))
    return o.transpose(0, 2, 1, 3).reshape(B, S, MIX_WIDTH)

def memory_cross_attention(xq, mem_n, w_kv, qn_g, kn_g):
    B, S, _ = xq.shape
    q = rms_norm(xq.reshape(B, S, XA_HEADS, XA_DIM), qn_g)
    kv = jnp.einsum("bmd,de->bme", mem_n, w_kv)
    k = rms_norm(kv[..., :XA_WIDTH].reshape(B, -1, XA_HEADS, XA_DIM), kn_g)
    v = kv[..., XA_WIDTH:].reshape(B, -1, XA_HEADS, XA_DIM)
    s = jnp.einsum("bthd,bmhd->bhtm", q, k).astype(jnp.float32) * XA_DIM ** -0.5
    p = jax.nn.softmax(s, axis=-1).astype(v.dtype)
    return jnp.einsum("bhtm,bmhd->bthd", p, v).reshape(B, S, XA_WIDTH)

def first_inputs(seed: int = 0) -> dict:
    key = jax.random.key(seed)
    ks = jax.random.split(key, 20)
    f32 = jnp.float32
    n_dn = (DEPTH + N_MIXERS - 1) // N_MIXERS
    n_sb = DEPTH // N_MIXERS

    def dense(k, shape, fan_in):
        return jax.random.normal(k, shape, f32) * fan_in ** -0.5

    def gain(k, shape):
        return 1.0 + 0.02 * jax.random.normal(k, shape, f32)

    dt = jnp.exp(jax.random.uniform(ks[10], (n_dn, DN_V_HEADS), f32,
                                    minval=math.log(1e-3), maxval=math.log(1e-1)))
    return {
        "x": jax.random.normal(ks[0], (BATCH, SEQ, D_MODEL), f32),
        "mem": jax.random.normal(ks[1], (BATCH, N_MEM, D_MODEL), f32),
        "norm_g": gain(ks[2], (DEPTH, D_MODEL)),
        "mem_norm_g": gain(ks[3], (D_MODEL,)),
        "mem_w_kv": dense(ks[4], (DEPTH, D_MODEL, 2 * XA_WIDTH), D_MODEL),
        "xa_q_norm_g": gain(ks[5], (DEPTH, XA_DIM)),
        "xa_k_norm_g": gain(ks[6], (DEPTH, XA_DIM)),
        "w_out": dense(ks[7], (DEPTH, INNER, D_MODEL), INNER),
        "dn_w_in": dense(ks[8], (n_dn, D_MODEL, DN_PROJ), D_MODEL),
        "dn_conv_w": dense(ks[9], (n_dn, DN_CONV, 2 * DN_QK_WIDTH + MIX_WIDTH), DN_CONV),
        "dn_a_log": jnp.log(jax.random.uniform(ks[11], (n_dn, DN_V_HEADS), f32, minval=1.0, maxval=16.0)),
        "dn_dt_bias": dt + jnp.log(-jnp.expm1(-dt)),
        "dn_out_norm_g": gain(ks[12], (n_dn, DN_HEAD_DIM)),
        "sb_w_in": dense(ks[13], (n_sb, D_MODEL, SB_PROJ), D_MODEL),
        "sb_q_norm_g": gain(ks[14], (n_sb, SB_HEAD_DIM)),
        "sb_k_norm_g": gain(ks[15], (n_sb, SB_HEAD_DIM)),
    }

def first_block(x, mem, norm_g, mem_norm_g, mem_w_kv, xa_q_norm_g, xa_k_norm_g, w_out,
              dn_w_in, dn_conv_w, dn_a_log, dn_dt_bias, dn_out_norm_g,
              sb_w_in, sb_q_norm_g, sb_k_norm_g):
    mem_n = rms_norm(mem, mem_norm_g)
    for i in range(DEPTH):
        h = rms_norm(x, norm_g[i])
        j = i // N_MIXERS
        if i % N_MIXERS == 0:
            proj = jnp.einsum("bsd,de->bse", h, dn_w_in[j])
            mix = deltanet_branch(proj[..., :DN_MIX_COLS], dn_conv_w[j], dn_a_log[j],
                                  dn_dt_bias[j], dn_out_norm_g[j])
        else:
            proj = jnp.einsum("bsd,de->bse", h, sb_w_in[j])
            mix = stick_breaking_branch(proj[..., :SB_MIX_COLS], sb_q_norm_g[j], sb_k_norm_g[j])
        xq = proj[..., -(XA_WIDTH + INNER):-INNER]
        z = proj[..., -INNER:]
        xa = memory_cross_attention(xq, mem_n, mem_w_kv[i], xa_q_norm_g[i], xa_k_norm_g[i])
        y = jnp.concatenate([mix, xa], axis=-1) * jax.nn.silu(z)
        x = x + jnp.einsum("bse,ed->bsd", y, w_out[i])
    return x


D_MIX = D_MODEL
D_POOL = D_MIX // 2
POOL_WINDOWS = (2, 4, 8, 16)
N_POOL_GROUPS = len(POOL_WINDOWS)
POOL_GROUP = D_POOL // N_POOL_GROUPS
D_ATTN = D_MIX - D_POOL
N_HEADS = 8
HEAD_DIM = D_ATTN // N_HEADS
IDX_HEADS = 16
IDX_DIM = 64
INDEXER_SCALE = (IDX_HEADS * IDX_DIM) ** -0.5
MAX_TOPK = 256
Q_BLOCK = 128
N_BUCKETS = 32
MAX_DISTANCE = 128
PEER_HEADS = 8
PEER_KEYS = 128
N_EXPERTS = PEER_KEYS * PEER_KEYS
PEER_QDIM = 256
PEER_HALF = PEER_QDIM // 2
PEER_TOPK = 16
PEER_CHUNK = 128
ALPHA = (2 * DEPTH) ** 0.25
BETA = (8 * DEPTH) ** -0.25
LN_EPS = 1e-5
NEG_INF = -1e30

SPLIT_SIZES = (D_POOL, D_ATTN, D_ATTN, D_ATTN, IDX_HEADS * IDX_DIM, IDX_DIM, IDX_HEADS)
D_IN = sum(SPLIT_SIZES)


def layer_norm(x, g, b):
    xf = x.astype(jnp.float32)
    mu = jnp.mean(xf, axis=-1, keepdims=True)
    var = jnp.mean(jnp.square(xf - mu), axis=-1, keepdims=True)
    y = (xf - mu) * lax.rsqrt(var + LN_EPS)
    return (y * g.astype(jnp.float32) + b.astype(jnp.float32)).astype(x.dtype)

def split_columns(proj):
    parts, start = [], 0
    for size in SPLIT_SIZES:
        parts.append(proj[..., start:start + size])
        start += size
    return parts

def pool_mixer(v, pool_w, pool_scale):
    B, S, _ = v.shape
    vg = v.reshape(B, S, N_POOL_GROUPS, POOL_GROUP)
    c = jnp.cumsum(vg.astype(jnp.float32), axis=1)
    c = jnp.pad(c, ((0, 0), (1, 0), (0, 0), (0, 0)))
    pos = jnp.arange(S)
    means = []
    for g, w in enumerate(POOL_WINDOWS):
        cg = c[:, :, g]
        hi = cg[:, 1:]
        lo = cg[:, jnp.maximum(pos + 1 - w, 0)]
        cnt = jnp.minimum(pos + 1, w).astype(jnp.float32)[None, :, None]
        means.append((hi - lo) / cnt)
    pooled = jnp.stack(means, axis=2).astype(v.dtype) - vg
    mixed = jnp.einsum('bsgc,gcd->bsgd', pooled, pool_w)
    return mixed.reshape(B, S, D_POOL) * pool_scale

def t5_bucket(dist):
    max_exact = N_BUCKETS // 2
    d = jnp.maximum(dist, 1).astype(jnp.float32)
    large = max_exact + (jnp.log(d / max_exact) / math.log(MAX_DISTANCE / max_exact)
                         * (N_BUCKETS - max_exact)).astype(jnp.int32)
    large = jnp.minimum(large, N_BUCKETS - 1)
    return jnp.where(dist < max_exact, dist, large)

def sparse_attention(q, k, v, q_idx, k_idx, w_idx, rel_bias):
    B, S = q.shape[:2]
    top_k = min(MAX_TOPK, S // 4)
    n_blocks = S // Q_BLOCK
    b_ix = jnp.arange(B)[:, None, None]
    key_pos = jnp.arange(S)

    def block(i):
        start = i * Q_BLOCK
        qi = lax.dynamic_slice_in_dim(q_idx, start, Q_BLOCK, axis=1)
        wi = lax.dynamic_slice_in_dim(w_idx, start, Q_BLOCK, axis=1)
        qa = lax.dynamic_slice_in_dim(q, start, Q_BLOCK, axis=1)
        q_pos = start + jnp.arange(Q_BLOCK)
        rel = jax.nn.relu(jnp.einsum('bqhd,bsd->bqhs', qi, k_idx))
        score = jnp.einsum('bqh,bqhs->bqs', wi, rel).astype(jnp.float32) * INDEXER_SCALE
        causal = key_pos[None, :] <= q_pos[:, None]
        score = jnp.where(causal[None], score, NEG_INF)
        _, sel = lax.top_k(score, top_k)
        k_sel = k[b_ix, sel]
        v_sel = v[b_ix, sel]
        logits = jnp.einsum('bqhd,bqkhd->bhqk', qa, k_sel).astype(jnp.float32) * HEAD_DIM ** -0.5
        dist = q_pos[None, :, None] - sel
        bias = rel_bias[t5_bucket(jnp.maximum(dist, 0))]
        logits = logits + jnp.transpose(bias, (0, 3, 1, 2)).astype(jnp.float32)
        logits = jnp.where((dist >= 0)[:, None], logits, NEG_INF)
        p = jax.nn.softmax(logits, axis=-1).astype(v.dtype)
        return jnp.einsum('bhqk,bqkhd->bqhd', p, v_sel)

    out = lax.map(block, jnp.arange(n_blocks))
    return jnp.transpose(out, (1, 0, 2, 3, 4)).reshape(B, S, N_HEADS * HEAD_DIM)

def peer_ffn(x, wq, sub_keys, u, v):
    B, S, D = x.shape
    xt = x.reshape(-1, PEER_CHUNK, D)

    def chunk(xc):
        qh = (xc @ wq).reshape(PEER_CHUNK, PEER_HEADS, 2, PEER_HALF)
        s1 = jnp.einsum('thd,kd->thk', qh[:, :, 0], sub_keys[0]).astype(jnp.float32)
        s2 = jnp.einsum('thd,kd->thk', qh[:, :, 1], sub_keys[1]).astype(jnp.float32)
        v1, i1 = lax.top_k(s1, PEER_TOPK)
        v2, i2 = lax.top_k(s2, PEER_TOPK)
        cand = (v1[..., :, None] + v2[..., None, :]).reshape(PEER_CHUNK, PEER_HEADS, PEER_TOPK * PEER_TOPK)
        cidx = (i1[..., :, None] * PEER_KEYS + i2[..., None, :]).reshape(PEER_CHUNK, PEER_HEADS, PEER_TOPK * PEER_TOPK)
        best, pos = lax.top_k(cand, PEER_TOPK)
        expert = jnp.take_along_axis(cidx, pos, axis=-1)
        gate = jax.nn.softmax(best, axis=-1)
        u_sel = u[expert]
        v_sel = v[expert]
        act = jax.nn.gelu(jnp.einsum('td,thkd->thk', xc, u_sel).astype(jnp.float32), approximate=False)
        return jnp.einsum('thk,thkd->td', (gate * act).astype(x.dtype), v_sel)

    return lax.map(chunk, xt).reshape(B, S, D)

def second_inputs(seed: int = 0) -> dict:
    key = jax.random.key(seed)
    ks = jax.random.split(key, 16)
    f32 = jnp.float32
    L = DEPTH
    x = jax.random.normal(ks[0], (BATCH, SEQ, D_MODEL), f32)
    w_in = jax.random.normal(ks[1], (L, D_MODEL, D_IN), f32) * D_MODEL ** -0.5
    pool_w = jax.random.normal(ks[2], (L, N_POOL_GROUPS, POOL_GROUP, POOL_GROUP), f32) * POOL_GROUP ** -0.5
    pool_scale = 1.0 + 0.1 * jax.random.normal(ks[3], (L, D_POOL), f32)
    rel_bias = 0.5 * jax.random.normal(ks[4], (N_BUCKETS, N_HEADS), f32)
    w_out = jax.random.normal(ks[5], (L, D_MIX, D_MODEL), f32) * (D_MIX ** -0.5 * BETA)
    ln1_g = 1.0 + 0.05 * jax.random.normal(ks[6], (L, D_MODEL), f32)
    ln1_b = 0.02 * jax.random.normal(ks[7], (L, D_MODEL), f32)
    peer_wq = jax.random.normal(ks[8], (L, D_MODEL, PEER_HEADS * PEER_QDIM), f32) * D_MODEL ** -0.5
    peer_subkeys = jax.random.normal(ks[9], (L, 2, PEER_KEYS, PEER_HALF), f32) * PEER_HALF ** -0.5
    peer_u = jax.random.normal(ks[10], (L, N_EXPERTS, D_MODEL), f32) * D_MODEL ** -0.5
    peer_v = jax.random.normal(ks[11], (L, N_EXPERTS, D_MODEL), f32) * (BETA * PEER_HEADS ** -0.5)
    ln2_g = 1.0 + 0.05 * jax.random.normal(ks[12], (L, D_MODEL), f32)
    ln2_b = 0.02 * jax.random.normal(ks[13], (L, D_MODEL), f32)
    return {"x": x, "w_in": w_in, "pool_w": pool_w, "pool_scale": pool_scale,
            "rel_bias": rel_bias, "w_out": w_out, "ln1_g": ln1_g, "ln1_b": ln1_b,
            "peer_wq": peer_wq, "peer_subkeys": peer_subkeys, "peer_u": peer_u,
            "peer_v": peer_v, "ln2_g": ln2_g, "ln2_b": ln2_b}

def second_block(x, w_in, pool_w, pool_scale, rel_bias, w_out, ln1_g, ln1_b,
              peer_wq, peer_subkeys, peer_u, peer_v, ln2_g, ln2_b):
    B, S, _ = x.shape
    h = x
    for l in range(DEPTH):
        proj = h @ w_in[l]
        p_pool, p_q, p_k, p_v, p_qi, p_ki, p_wi = split_columns(proj)
        out_pool = pool_mixer(p_pool, pool_w[l], pool_scale[l])
        out_attn = sparse_attention(
            p_q.reshape(B, S, N_HEADS, HEAD_DIM),
            p_k.reshape(B, S, N_HEADS, HEAD_DIM),
            p_v.reshape(B, S, N_HEADS, HEAD_DIM),
            p_qi.reshape(B, S, IDX_HEADS, IDX_DIM), p_ki, p_wi, rel_bias)
        mix = jnp.concatenate([out_pool, out_attn], axis=-1) @ w_out[l]
        h = layer_norm(ALPHA * h + mix, ln1_g[l], ln1_b[l])
        ffn = peer_ffn(h, peer_wq[l], peer_subkeys[l], peer_u[l], peer_v[l])
        h = layer_norm(ALPHA * h + ffn, ln2_g[l], ln2_b[l])
    return h


def setup_inputs(seed=0):
    out = dict(first_inputs(seed))
    for name, value in second_inputs(seed + 1).items():
        if name != "x":
            out[name + "_2"] = value
    return out


def reference(
    x, mem, norm_g, mem_norm_g, mem_w_kv, xa_q_norm_g, xa_k_norm_g, w_out, dn_w_in, dn_conv_w,
    dn_a_log, dn_dt_bias, dn_out_norm_g, sb_w_in, sb_q_norm_g, sb_k_norm_g, w_in_2, pool_w_2,
    pool_scale_2, rel_bias_2, w_out_2, ln1_g_2, ln1_b_2, peer_wq_2, peer_subkeys_2, peer_u_2,
    peer_v_2, ln2_g_2, ln2_b_2,
):
    x = first_block(
        x, mem, norm_g, mem_norm_g, mem_w_kv, xa_q_norm_g, xa_k_norm_g, w_out, dn_w_in,
        dn_conv_w, dn_a_log, dn_dt_bias, dn_out_norm_g, sb_w_in, sb_q_norm_g, sb_k_norm_g,
    )
    return second_block(
        x, w_in_2, pool_w_2, pool_scale_2, rel_bias_2, w_out_2, ln1_g_2, ln1_b_2, peer_wq_2,
        peer_subkeys_2, peer_u_2, peer_v_2, ln2_g_2, ln2_b_2,
    )


_drawn_inputs = setup_inputs


def setup_inputs(seed=0):
    import zlib

    import numpy as np

    out = dict(_drawn_inputs(seed))
    spreads = {}
    factors = {'mem_norm_g': 8.0,
     'xa_q_norm_g': 8.0,
     'xa_k_norm_g': 8.0,
     'dn_out_norm_g': 3.756,
     'ln2_b_2': 2.79}
    for name, (base, spread) in spreads.items():
        noise = np.random.default_rng([zlib.crc32(name.encode()), seed]).standard_normal(out[name].shape)
        drawn = base * np.exp(spread * noise) if base else spread * noise
        out[name] = __import__('jax').numpy.asarray(drawn.astype(out[name].dtype))
    for name, factor in factors.items():
        out[name] = (out[name] * factor).astype(out[name].dtype)
    return out
```

```python
import math
from contextlib import ExitStack

import numpy as np
import concourse.bass as bass
from concourse import mybir

F = mybir.dt.float32
R = mybir.dt.float32r
U32 = mybir.dt.uint32
ALU = mybir.AluOpType
ACT = mybir.ActivationFunctionType
AX = mybir.AxisListType

KB = 256
NRAW = 3
ALPHA = 2.0 ** 0.25
BIG = 1e30
LEVELS = (2, 4, 8, 16, 32)

CON = {}
_off = 0
for _n, _w in (("ident", 128), ("tri", 128), ("blk", 128), ("mt", 128), ("ms", 128), ("nm1", 128),
               ("nmt1", 128), ("mt2", 128), ("mt4", 128), ("mt8", 128), ("mt16", 128), ("mt32", 128),
               ("flip", 128), ("ones", 128), ("iota", 128), ("causal", 128), ("chunk", 2), ("iota16", 16),
               ("eps6", 1), ("eps5", 1)):
    CON[_n] = (_off, _w)
    _off += _w
NCON = _off

VEC = {}
_off = 0
for _n, _w in (("norm_g", 16), ("mem_g", 16), ("conv", 192), ("ln1g", 16), ("ln1b", 16), ("xaq", 2), ("xak", 2),
               ("outg", 1), ("pools", 8), ("alog", 24), ("dtb", 24)):
    VEC[_n] = (_off, _w)
    _off += _w
NVEC = _off


def constants():
    c = np.zeros((128, NCON), np.float32)
    p = np.arange(128)[:, None]
    x = np.arange(128)[None, :]
    same = (p // 64) == (x // 64)

    def put(name, a):
        o, w = CON[name]
        c[:, o:o + w] = a

    put("ident", p == x)
    put("tri", (p <= x) & same)
    put("blk", same)
    put("mt", np.where((p <= x) & same, 0.0, -BIG))
    put("ms", np.where((x < p) & same, 0.0, BIG))

    def low(s):
        return ((p // (2 * s)) == (x // (2 * s))) & ((p // s) % 2 == 1) & ((x // s) % 2 == 0)

    put("nm1", -1.0 * low(1))
    put("nmt1", -1.0 * low(1).T)
    for s in LEVELS:
        put(f"mt{s}", low(s).T)
    put("flip", (p + x) == 127)
    put("ones", 1.0)
    put("iota", x + 0 * p)
    put("causal", np.where(x <= p, 0.0, -BIG))
    put("chunk", (p // 64) == np.arange(2)[None, :])
    put("iota16", np.arange(16)[None, :] + 0 * p)
    put("eps6", 1e-6)
    put("eps5", 1e-5)
    inv = np.stack([1.0 / np.minimum(np.arange(256) + 1, w) for w in (2, 4, 8, 16)]).astype(np.float32)
    inv = np.ascontiguousarray(np.broadcast_to(inv.reshape(1, 1024), (128, 1024)))
    dist = np.maximum(255 - np.arange(384), 0)
    d = np.maximum(dist, 1).astype(np.float32)
    large = 16 + (np.log(d / np.float32(16)) / np.float32(math.log(8.0)) * np.float32(16)).astype(np.int32)
    bucket = np.where(dist < 16, dist, np.minimum(large, 31))
    hot = (np.arange(32)[:, None] == bucket[None, :]).astype(np.float32)
    return c, inv, hot


class Queue:

    def __init__(self, sem):
        self.sem, self.items, self.n, self.seen = sem, [], 0, {}

    def wait(self, tok):
        if tok is None:
            return
        sem, value = tok
        key = sem.name
        if self.seen.get(key, 0) < value:
            self.seen[key] = value
            self.items.append(lambda e: e.wait_ge(sem, value))

    def do(self, fn, *waits, sig=True):
        for w in waits:
            self.wait(w)
        if not sig:
            self.items.append(fn)
            return None
        self.n += 1
        self.items.append(lambda e: fn(e).then_inc(self.sem, 1))
        return (self.sem, self.n)

    def dma(self, fn, sem, value, *waits):
        for w in waits:
            self.wait(w)
        self.items.append(lambda e: fn(e).then_inc(sem, 16))
        return (sem, value)


def build(nc, D, out, scratch, stage=99, dbg=None):
    ctx = ExitStack()
    with ctx:
        def sb(name, shape, dt):
            return ctx.enter_context(nc.sbuf_tensor(name, shape, dt))

        def semaphore(name):
            return ctx.enter_context(nc.semaphore(name))

        con = sb("cons", [128, NCON], F)
        vec = sb("vecs", [128, NVEC], F)
        keep = sb("keep", [128, 352], F)
        raw = sb("raw", [128, NRAW, 2048], F)
        WH = sb("WH", [128, 4, 1024], R)
        WL = sb("WL", [128, 4, 1024], R)
        PS = ctx.enter_context(nc.psum_tensor("PS", [128, 8, 512], F))

        PE = Queue(semaphore("pe"))
        V = Queue(semaphore("dve"))
        A = Queue(semaphore("act"))
        G = Queue(semaphore("pool"))
        SP = Queue(semaphore("sp"))

        views = {}

        def view(kb, n, dt):
            o = int(kb * KB)
            key = (o, n, dt)
            if key not in views:
                name = f"m{o}_{n}" + ("r" if dt == R else "")
                if o:
                    with nc.sbuf_tensor("pad_" + name, [128, o], F):
                        with nc.sbuf_tensor(name, [128, n], dt) as t:
                            pass
                else:
                    with nc.sbuf_tensor(name, [128, n], dt) as t:
                        pass
                views[key] = t[:, :]
            return views[key]

        def f(kb, n):
            return view(kb, n, F)

        def r(kb, n):
            return view(kb, n, R)

        def C(name):
            o, w = CON[name]
            return con[:, o:o + w]

        def vc(name, i=0, n=1):
            o, _ = VEC[name]
            return vec[:, o + i:o + i + n]

        def finish():
            for tok in last_store:
                SP.wait(tok)
            for tok in raw_in.values():
                SP.wait(tok)

            block = ctx.enter_context(nc.Block())

            def play(q):
                def body(e):
                    for item in q.items:
                        item(e)
                return body

            block.sync(play(SP))
            block.tensor(play(PE))
            block.vector(play(V))
            block.scalar(play(A))
            block.gpsimd(play(G))

        nload = [0]
        last_store = []

        def load(q, dst, src, *waits, store=False):
            nload[0] += 1
            s = semaphore(f"ld{nload[0]}")
            tok = q.dma(lambda e: e.dma_start(dst, src), s, 16, *waits)
            if store:
                last_store.append(tok)
            return tok

        def mm(o, l, x, start, stop, *waits, sig=False):
            return PE.do(lambda e: e.matmul(o, l, x, start=start, stop=stop), *waits, sig=sig)

        def tr(o, i, *waits, sig=False):
            return PE.do(lambda e: e.transpose(o, i, C("ident")), *waits, sig=sig)

        def tt(q, o, a, b, op, *waits):
            return q.do(lambda e: e.tensor_tensor(o, a, b, op), *waits)

        def ts(q, o, a, s1, s2, op0, op1, *waits):
            if op1 is None:
                return q.do(lambda e: e.tensor_scalar(o, a, s1, None, op0), *waits)
            return q.do(lambda e: e.tensor_scalar(o, a, s1, s2, op0, op1), *waits)

        def stt(o, a, s, b, op0, op1, *waits):
            return V.do(lambda e: e.scalar_tensor_tensor(out=o, in0=a, scalar=s, in1=b, op0=op0, op1=op1), *waits)

        def act(o, i, fn, *waits, scale=1.0, bias=0.0, acc=None):
            if acc is None:
                return A.do(lambda e: e.activation(o, i, fn, scale=scale, bias=bias), *waits)
            return A.do(lambda e: e.activation(o, i, fn, scale=scale, bias=bias, accum_out=acc), *waits)

        def acopy(o, i, *waits):
            return A.do(lambda e: e.copy(o, i), *waits)

        def vcopy(o, i, *waits):
            return V.do(lambda e: e.tensor_copy(o, i), *waits)

        def recip(o, i, *waits):
            return V.do(lambda e: e.reciprocal(o, i), *waits)

        def bc(ap, n, axis=1):
            w = ap.shape[1]
            return ap.unsqueeze(1).broadcast_to([128, n, w]) if axis == 1 else ap.unsqueeze(2).broadcast_to([128, w, n])

        units = []
        for i in range(16):
            units.append(D["w_kv"][i])
        for i in range(8):
            units.append(D["w_xq"][i])
        for i in range(12):
            units.append(D["w_qkv"][12 + i])
            units.append(D["w_qkv"][i])
        units.append(D["w_ab"][0])
        for i in range(24):
            units.append(D["w_qkv"][24 + i])
        for i in range(32):
            units.append(D["w_z"][i])
        for i in range(32):
            units.append(D["w_o"][i])
        units.append(D["w2_kiwi"][0])
        for g in (4, 2, 1, 3, 0):
            for i in range(8):
                units.append(D["w2"][8 * g + i])
        for i in range(16):
            units.append(D["w_o2"][i])
        for i in range(16):
            units.append(D["w_q2"][i])
        vv = D["pv"].rearrange("(i j) d -> j i d", j=128)
        for half in range(2):
            for j in range(64):
                units.append(D["pu"][64 * half + j])
            for j in range(64):
                units.append(vv[64 * half + j])
        raw_sem = [semaphore(f"raw{i}") for i in range(NRAW)]
        raw_in = {}
        ready = {}
        used = {}

        def issue(n, *waits):
            if n < len(units):
                raw_in[n] = SP.dma(lambda e: e.dma_start(raw[:, n % NRAW, :], units[n]),
                                   raw_sem[n % NRAW], 16 * (n // NRAW + 1), *waits)

        def prep(n, h):
            if (n, h) in ready or n >= len(units):
                return
            k = (n % 2) * 2 + h
            src = raw[:, n % NRAW, h * 1024:h * 1024 + 1024]
            free = used.get((n - 2, h))
            hi = acopy(WH[:, k, :], src, raw_in[n], free)
            lo = tt(V, WL[:, k, :], src, WH[:, k, :].bitcast(F), ALU.subtract, raw_in[n], hi, free)
            ready[(n, h)] = lo
            if h == 1:
                issue(n + NRAW, ready[(n, 0)], lo)

        def prep_ahead(n, h):
            for q in range(2 * n + h, 2 * n + h + 4):
                prep(q // 2, q % 2)

        for n in range(NRAW):
            issue(n)
        un = [0]

        def unit(XH, XL, bank, *waits, start=True, stop=True, per=12):
            n = un[0]
            un[0] += 1
            for h in range(2):
                prep_ahead(n, h)
                k = (n % 2) * 2 + h
                cnt = 0
                for kt in range(8):
                    x = 8 * h + kt
                    wh = WH[:, k, kt * 128:kt * 128 + 128]
                    wl = WL[:, k, kt * 128:kt * 128 + 128]
                    first = start and h == 0 and kt == 0
                    last = stop and h == 1 and kt == 7
                    mm(PS[:, bank, 0:256], wh, XH[:, x, :], first, False, ready[(n, h)], *waits)
                    mm(PS[:, bank, 0:256], wh, XL[:, x, :], False, False)
                    t = mm(PS[:, bank, 0:256], wl, XH[:, x, :], False, last, sig=(kt == 7))
                    cnt += 3
                    if kt == 7:
                        used[(n, h)] = t
                    if cnt % per == 0:
                        yield t
            unit_done[0] = t

        unit_done = [None]

        def drain(g):
            for _ in g:
                pass

        def together(a, b):
            for _ in a:
                next(b, None)
            drain(b)

        t_con = load(A, con[:, :], D["con"])
        t_vec = load(A, vec[:, :], D["vec"])
        XT, TMP, MT_ = f(64, 4096), f(80, 4096), f(96, 4096)
        t_mem = load(A, MT_, D["memT"])
        t_x = load(A, XT, D["xT"])
        for q in (PE, V, A, G):
            q.wait(t_con)
            q.wait(t_vec)

        def k3(ap):
            return ap.rearrange("p (k t) -> p k t", t=256)

        def norm_T(src, t_src, gain, XH, XL, bank, free):
            sq = []
            for c in range(4):
                sq.append(act(TMP[:, c * 1024:c * 1024 + 1024], src[:, c * 1024:c * 1024 + 1024], ACT.Square, t_src, free))
            for kt in range(16):
                t = mm(PS[:, bank, 0:256], C("ones"), TMP[:, kt * 256:kt * 256 + 256], kt == 0, kt == 15,
                       sq[kt // 4], sig=(kt == 15))
            rt = f(128, 256)
            a = act(rt, PS[:, bank, 0:256], ACT.Sqrt, t, scale=1.0 / 2048, bias=C("eps6"))
            b = recip(rt, rt, a)
            m = tt(V, k3(TMP), k3(src), bc(rt, 16), ALU.mult, b)
            for kt in range(16):
                hi = act(XH[:, kt * 256:kt * 256 + 256], TMP[:, kt * 256:kt * 256 + 256], ACT.Identity, m,
                         scale=vc(gain, kt))
                lo = stt(XL[:, kt * 256:kt * 256 + 256], TMP[:, kt * 256:kt * 256 + 256], vc(gain, kt),
                         XH[:, kt * 256:kt * 256 + 256].bitcast(F), ALU.mult, ALU.subtract, hi)
            return lo

        HH, HL = r(0, 4096), r(16, 4096)
        MH, ML = r(32, 4096), r(48, 4096)
        prep(0, 0)
        prep(0, 1)
        t_mr = norm_T(MT_, t_mem, "mem_g", MH, ML, 2, None)
        t_hr = norm_T(XT, t_x, "norm_g", HH, HL, 3, t_mr)
        H3, L3, M3, N3 = k3(HH), k3(HL), k3(MH), k3(ML)

        free = {0: None, 1: None}
        MK = f(112, 2048)
        MV = f(120, 2048)
        MV3 = MV.rearrange("p (m c) -> p m c", m=2)
        XQ = f(64, 2048)
        XA = f(132, 2048)

        def tile(ap, i, n=1):
            return ap[:, i * 256:(i + n) * 256]

        mk = []
        for i in range(8):
            b = i % 2
            drain(unit(M3, N3, b, t_mr, free[b]))
            free[b] = acopy(tile(MK, i), PS[:, b, 0:256], unit_done[0], t_hr)
            mk.append(free[b])
        vt_free = [None, None]
        b4 = [None, None]
        for i in range(8):
            b = i % 2
            drain(unit(M3, N3, b, free[b]))
            tmp = f(130 + b, 256)
            free[b] = t = acopy(tmp, PS[:, b, 0:256], unit_done[0], vt_free[b])
            for m in range(2):
                t2 = tr(PS[:, 4 + b, m * 128:m * 128 + 128], tmp[:, m * 128:m * 128 + 128], t, b4[b], sig=(m == 1))
            vt_free[b] = t2
            b4[b] = vcopy(MV3[:, :, i * 128:i * 128 + 128], PS[:, 4 + b, 0:256].rearrange("p (m c) -> p m c", m=2),
                          t2, t_hr)
        t_mv = b4[1]
        mem_pe = unit_done[0]
        xq = []
        for i in range(8):
            b = i % 2
            drain(unit(H3, L3, b, t_hr, free[b]))
            free[b] = acopy(tile(XQ, i), PS[:, b, 0:256], unit_done[0], t_hr)
            xq.append(free[b])

        def cross():
            SQ = f(80, 2048)
            RK = f(88, 1024)
            done = []
            for X, tx, gain, bank, prev in ((MK, mk[-1], "xak", 2, None), (XQ, xq[-1], "xaq", 6, None)):
                s = tt(G, SQ, X, X, ALU.mult, tx, done[-1] if done else t_hr)
                for h in range(4):
                    for i in range(2):
                        t = mm(PS[:, bank + h // 2, (h % 2) * 256:(h % 2) * 256 + 256], C("ones"), tile(SQ, 2 * h + i),
                               i == 0, i == 1, s, sig=True)
                    yield
                a = act(RK, PS[:, bank:bank + 2, :], ACT.Sqrt, t, done[-1] if done else t_hr, scale=1.0 / 256, bias=C("eps6"))
                a = recip(RK, RK, a)
                for h in range(4):
                    for i in range(2):
                        a2 = stt(tile(X, 2 * h + i), tile(X, 2 * h + i), vc(gain, i), tile(RK, h), ALU.mult, ALU.mult, a)
                done.append(a2)
                yield
            ready_ = done[-1]
            bank_free = {2: None, 3: None, 4: b4[0], 5: b4[1], 6: None, 7: None}
            p_free = [None, None]
            pt_free = [None, None]
            xa_t = []
            it = 0
            for h in range(4):
                PT = f(96 + 2 * (h % 2), 512).rearrange("p (m t) -> p m t", m=2)
                for p in range(2):
                    bk = 2 + it % 2
                    P = f(92 + it % 2, 256)
                    st = f(94 + it % 2, 8)
                    for i in range(2):
                        t = mm(PS[:, bk, 0:256], tile(XQ, 2 * h + i)[:, p * 128:p * 128 + 128], tile(MK, 2 * h + i),
                               i == 0, i == 1, ready_, bank_free[bk], sig=(i == 1))
                    mx = V.do(lambda e, st=st, bk=bk: e.tensor_reduce(st[:, 0:1], PS[:, bk, 0:256], AX.X, ALU.max, negate=True),
                              t, p_free[it % 2])
                    m2 = ts(V, st[:, 1:2], st[:, 0:1], 1.0 / 16, None, ALU.mult, None, mx)
                    ex = act(P, PS[:, bk, 0:256], ACT.Exp, m2, scale=1.0 / 16, bias=st[:, 1:2], acc=st[:, 2:3])
                    bank_free[bk] = ex
                    rc = recip(st[:, 3:4], st[:, 2:3], ex)
                    nm = ts(V, P, P, st[:, 3:4], None, ALU.mult, None, rc)
                    yield
                    b2 = 4 + it % 2
                    for m in range(2):
                        t = tr(PS[:, b2, m * 128:m * 128 + 128], P[:, m * 128:m * 128 + 128], nm, bank_free[b2], sig=(m == 1))
                    p_free[it % 2] = t
                    bank_free[b2] = cp = vcopy(PT[:, :, p * 128:p * 128 + 128],
                                               PS[:, b2, 0:256].rearrange("p (m t) -> p m t", m=2), t, pt_free[h % 2])
                    it += 1
                    yield
                for i in range(2):
                    b3 = 6 + i
                    for m in range(2):
                        t = mm(PS[:, b3, 0:256], MV3[:, m, (2 * h + i) * 128:(2 * h + i) * 128 + 128], PT[:, m, :],
                               m == 0, m == 1, cp, t_mv, bank_free[b3], sig=(m == 1))
                    bank_free[b3] = acopy(tile(XA, 2 * h + i), PS[:, b3, 0:256], t, vt_free[0], vt_free[1])
                    xa_t.append(bank_free[b3])
                pt_free[h % 2] = t
                yield
            cross_end.extend([xa_t[-1], t, bank_free[2], bank_free[3], bank_free[4], bank_free[5], bank_free[6], bank_free[7]])

        cross_end = []

        QK, VT = f(32, 6144), f(56, 6144)
        QT, KT = QK[:, 0:3072], QK[:, 3072:6144]
        SSQ = f(88, 6144)
        AB = f(112, 256)

        conv_free = [None] * 2
        cv = [0]

        def conv_tile(dst, widx, bank, done, *waits):
            i = cv[0] % 2
            cv[0] += 1
            tmp = f(128 + i, 256)
            t = ts(V, tmp, PS[:, bank, 0:256], vc("conv", widx * 4 + 3), None, ALU.mult, None, done, conv_free[i], t_hr)
            for s in (1, 2, 3):
                t = stt(tmp[:, s:256], PS[:, bank, 0:256 - s], vc("conv", widx * 4 + 3 - s), tmp[:, s:256],
                        ALU.mult, ALU.add, t)
            conv_free[i] = a = act(dst, tmp, ACT.Silu, t, *waits)
            return t, a

        qk_t = []

        def qk_units():
            for i in range(24):
                hk, isq = i // 2, i % 2
                b = i % 2
                yield from unit(H3, L3, b, free[b])
                dst = tile(QT if isq else KT, hk)
                free[b], a = conv_tile(dst, hk if isq else 12 + hk, b, unit_done[0], mem_pe)
                qk_t.append(a)

        together(cross(), qk_units())
        sq_t = []
        for c in range(6):
            sq_t.append(tt(G, SSQ[:, c * 1024:c * 1024 + 1024], QK[:, c * 1024:c * 1024 + 1024],
                           QK[:, c * 1024:c * 1024 + 1024], ALU.mult, qk_t[-1], *cross_end))

        drain(unit(H3, L3, 0, free[0]))
        free[0] = t = acopy(AB, PS[:, 0, 0:256], unit_done[0], *cross_end)
        for p in range(2):
            t = tr(PS[:, 2, p * 128:p * 128 + 128], AB[:, p * 128:p * 128 + 128], t, cross_end[2], sig=True)
        SM = f(113, 48 * 12)
        sm = lambda i, n=1: SM[:, 48 * i:48 * (i + n)]
        v2 = lambda ap: ap.rearrange("p (a h) -> p a h", a=2)
        a_ = vcopy(v2(sm(0)), PS[:, 2, 0:256].rearrange("p (a c) -> p a c", a=2)[:, :, 0:24], t, *cross_end)
        b_ = vcopy(v2(sm(1)), PS[:, 2, 0:256].rearrange("p (a c) -> p a c", a=2)[:, :, 24:48])
        x_ = tt(V, v2(sm(0)), v2(sm(0)), bc(vc("dtb", 0, 24), 2), ALU.add, a_, b_)
        n_ = ts(V, sm(2), sm(0), -1.0, None, ALU.mult, None, x_)
        n_ = tt(V, sm(2), sm(2), sm(0), ALU.min, n_)
        m_ = ts(V, sm(3), sm(0), 0.0, None, ALU.max, None, x_)
        e1 = act(sm(2), sm(2), ACT.Exp, n_)
        e2 = act(sm(4), sm(1), ACT.Exp, b_, scale=-1.0)
        e3 = act(f(116, 24), vc("alog", 0, 24), ACT.Exp, *cross_end)
        e1 = act(sm(2), sm(2), ACT.Ln, e1, bias=1.0)
        s_ = tt(V, sm(3), sm(3), sm(2), ALU.add, m_, e1)
        GG = sm(5)
        g_ = tt(V, v2(GG), v2(sm(3)), bc(f(116, 24), 2), ALU.mult, s_, e3)
        g_ = ts(V, GG, GG, -1.0, None, ALU.mult, None, g_)
        BE = sm(6)
        e2 = ts(V, BE, sm(4), 1.0, None, ALU.add, None, e2)
        be_ = recip(BE, BE, e2)
        for p in range(2):
            t = mm(PS[:, 2, p * 24:p * 24 + 24], C("tri"), GG[:, p * 24:p * 24 + 24], True, True, g_)
            t = mm(PS[:, 2, 48 + p * 24:72 + p * 24], C("blk"), GG[:, p * 24:p * 24 + 24], True, True)
            for n in range(2):
                o = 96 + (2 * p + n) * 24
                t = mm(PS[:, 2, o:o + 24], C("chunk")[:, n:n + 1].to_broadcast([128, 128]), GG[:, p * 24:p * 24 + 24],
                       True, True, sig=True)
        GC = f(117, 192)
        c_ = vcopy(GC, PS[:, 2, 0:192], t)
        KD = sm(7)
        d_ = tt(V, KD, GC[:, 48:96], GC[:, 0:48], ALU.subtract, c_)
        kd_ = act(KD, KD, ACT.Exp, d_)
        CD = f(118, 96)
        cd_ = act(CD, GC[:, 96:192], ACT.Exp, c_)
        BX = sm(8)
        bx_ = act(BX, GC[:, 0:48], ACT.Exp, c_)
        bx_ = tt(V, BX, BX, BE, ALU.mult, bx_, be_)
        small = [kd_, cd_, bx_]
        KEEP = keep[:, 0:256]
        k0 = vcopy(KEEP[:, 0:48], GG, *small)
        k0 = vcopy(KEEP[:, 48:96], BE)
        k0 = vcopy(KEEP[:, 96:144], KD)
        k0 = vcopy(KEEP[:, 144:192], BX)
        k0 = vcopy(KEEP[:, 192:240], GC[:, 0:48])
        CDK = keep[:, 256:352]
        k0 = vcopy(CDK, CD)
        GG, BE, KD, BX, GC = (KEEP[:, 48 * i:48 * i + 48] for i in range(5))
        KEEP_T = k0

        def qk_norm():
            for c in range(12):
                bk = 2 + c % 6
                t = mm(PS[:, bk, :], C("ones"), SSQ[:, c * 512:c * 512 + 512], True, True, sq_t[c // 2], k0,
                       cross_end[2], cross_end[3], cross_end[4], cross_end[5], cross_end[6], cross_end[7],
                       nb[bk], sig=True)
                nb[bk] = a = act(SSQ[:, c * 512:c * 512 + 512], PS[:, bk, :], ACT.Sqrt, t, bias=C("eps6"))
                yield
            for c in range(12):
                b = recip(SSQ[:, c * 512:c * 512 + 512], SSQ[:, c * 512:c * 512 + 512], a)
                q = QK[:, c * 512:c * 512 + 512]
                b = stt(q, q, 128.0 ** -0.5 if c < 6 else 1.0, SSQ[:, c * 512:c * 512 + 512], ALU.mult, ALU.mult, b)
                yield
            qk_n.append(b)

        nb = {i: None for i in range(2, 8)}
        qk_n = []
        v_t = []

        def v_units():
            for i in range(24):
                b = i % 2
                yield from unit(H3, L3, b, free[b])
                free[b], a = conv_tile(tile(VT, i), 24 + i, b, unit_done[0], *cross_end)
                v_t.append(a)

        together(qk_norm(), v_units())
        if stage == 1:
            tk = load(G, dbg[:, 0:12288], f(32, 12288), v_t[-1], qk_n[0], store=True)
            tk = load(G, dbg[:, 12288:14336], XA, v_t[-1], qk_n[0], store=True)
            tk = load(G, dbg[:, 14336:14336 + 240], KEEP[:, 0:240], v_t[-1], KEEP_T, store=True)
            return finish()

        ztok = {}
        gdone = []

        def ztile(i):
            if i < 8:
                return f(80 + i, 256)
            g = (i - 8) // 2
            return tile(KT if (i - 8) % 2 else QT, g)

        def z_units():
            for i in range(32):
                while i >= 8 and len(gdone) <= (i - 8) // 2:
                    yield
                b = i % 2
                yield from unit(H3, L3, b, free[b], per=6)
                w = gdone[(i - 8) // 2] if i >= 8 else qk_n[0]
                ztok[i] = free[b] = acopy(ztile(i), PS[:, b, 0:256], unit_done[0], w)

        bankfree = {i: nb[i] for i in range(2, 8)}
        slot_t = [qk_n[0], qk_n[0]]
        y_t = {}

        def group(g):
            s = g % 2
            bA, bB, bC = 2 + 3 * s, 3 + 3 * s, 4 + 3 * s
            base = 88 + 22 * s
            w = lambda kb, n=512: f(base + kb, n)
            kb, bv, kdc, dT, qd, Lb, LT, T, U, BT = (w(2 * i) for i in range(10))
            u, S = w(20, 256), w(21, 256)
            start = [slot_t[s], qk_n[0], v_t[-1], KEEP_T]
            kT, qT = tile(KT, g), tile(QT, g)
            vT = [tile(VT, 2 * g), tile(VT, 2 * g + 1)]
            col = lambda M, i: M[:, (i % 2) * 24 + 2 * g + i // 2:(i % 2) * 24 + 2 * g + i // 2 + 1]
            blk = lambda X, i: X[:, i * 128:i * 128 + 128]
            c4 = lambda X: X.rearrange("p (i c) -> p i c", i=4)
            for p in range(2):
                kp, qp = kT[:, p * 128:p * 128 + 128], qT[:, p * 128:p * 128 + 128]
                mm(PS[:, bA, p * 128:p * 128 + 128], kp, kp, True, True, *start, bankfree[bA])
                tA = mm(PS[:, bA, 256 + p * 128:384 + p * 128], kp, qp, True, True, sig=(p == 1))
            for i in range(4):
                tB = mm(PS[:, bB, i * 128:i * 128 + 128], col(GG, i).to_broadcast([128, 128]), C("tri"), True, True,
                        bankfree[bB], sig=(i == 3))
            for p in range(2):
                tr(PS[:, bC, p * 128:p * 128 + 128], kT[:, p * 128:p * 128 + 128], bankfree[bC])
            for p in range(2):
                tC = tr(PS[:, bC, 256 + p * 128:384 + p * 128], vT[0][:, p * 128:p * 128 + 128], sig=(p == 1))
            yield
            for i in range(4):
                d1 = stt(blk(dT, i), PS[:, bB, i * 128:i * 128 + 128], col(GC, i), C("mt"), ALU.subtract, ALU.add, tB,
                         *start)
            for i in range(4):
                d2 = stt(blk(Lb, i), PS[:, bB, i * 128:i * 128 + 128], col(GC, i), C("ms"), ALU.subtract, ALU.add)
            eB = act(qd, PS[:, bB, :], ACT.Exp, d2)
            eL = act(Lb, Lb, ACT.Exp, d2, scale=-1.0)
            eT = act(dT, dT, ACT.Exp, d1)
            for i in range(4):
                kpi = PS[:, bC, (i % 2) * 128:(i % 2) * 128 + 128]
                k1 = act(blk(kb, i), kpi, ACT.Copy, tC, *start, scale=col(BX, i))
                k2 = act(blk(kdc, i), kpi, ACT.Copy, scale=col(KD, i))
            for p in range(2):
                v1 = act(blk(bv, p), PS[:, bC, 256 + p * 128:384 + p * 128], ACT.Copy, scale=col(BE, p))
            for p in range(2):
                tB = tr(PS[:, bB, p * 128:p * 128 + 128], vT[1][:, p * 128:p * 128 + 128], eB, sig=(p == 1))
            yield
            for i in range(4):
                lk = stt(blk(Lb, i), blk(Lb, i), col(BE, i), PS[:, bA, (i % 2) * 128:(i % 2) * 128 + 128], ALU.mult,
                         ALU.mult, eL, tA)
            h2 = lambda X: X.rearrange("p (h c) -> p h c", h=2)
            qk = tt(V, h2(dT), h2(dT), bc(PS[:, bA, 256:512], 2), ALU.mult, eT)
            qd_ = tt(G, h2(qd), h2(qd), bc(qT, 2), ALU.mult, eB)
            for p in range(2):
                v1 = act(blk(bv, 2 + p), PS[:, bB, p * 128:p * 128 + 128], ACT.Copy, tB, scale=col(BE, 2 + p))
            for i in range(4):
                t = tr(PS[:, bA, i * 128:i * 128 + 128], blk(Lb, i), lk, qk, sig=(i == 3))
            cl = acopy(LT, PS[:, bA, :], t, *start)
            T1 = tt(V, c4(T), c4(Lb), bc(C("nm1"), 4), ALU.mult, lk)
            T1 = tt(V, c4(T), c4(T), bc(C("ident"), 4), ALU.add, T1)
            yield
            bt = tt(G, c4(BT), c4(LT), bc(C("mt2"), 4), ALU.mult, cl, *start)
            U1 = tt(G, c4(U), c4(LT), bc(C("nmt1"), 4), ALU.mult, cl)
            U1 = tt(G, c4(U), c4(U), bc(C("ident"), 4), ALU.add, U1)
            yield
            freeB, freeA, freeC = v1, cl, v1
            for s_ in LEVELS:
                for i in range(4):
                    t = mm(PS[:, bB, i * 128:i * 128 + 128], blk(BT, i), blk(T, i), True, True, bt, T1, freeB, sig=(i == 3))
                freeB = x = acopy(Lb, PS[:, bB, :], t, lk, T1)
                if s_ != 32:
                    bt = tt(G, c4(BT), c4(LT), bc(C(f"mt{2 * s_}"), 4), ALU.mult, t)
                yield
                if s_ != 32:
                    for i in range(4):
                        tA = mm(PS[:, bA, i * 128:i * 128 + 128], blk(U, i), blk(Lb, i), True, True, x, U1, freeA,
                                sig=(i == 3))
                for i in range(4):
                    tC = mm(PS[:, bC, i * 128:i * 128 + 128], blk(Lb, i), blk(U, i), True, True, x, U1, freeC,
                            sig=(i == 3))
                if s_ != 32:
                    freeA = T1 = tt(V, T, T, PS[:, bA, :], ALU.subtract, tA)
                freeC = U1 = tt(V, U, U, PS[:, bC, :], ALU.subtract, tC)
                yield
            for i in range(4):
                t = mm(PS[:, bB, i * 128:i * 128 + 128], blk(kb, i), blk(U, i), True, True, k1, U1, freeB, sig=(i == 3))
            freeB = nw = A.do(lambda e: e.mul(LT, PS[:, bB, :], -1.0), t, bt)
            yield
            St = None
            ut = None
            for n in range(4):
                p, b = n // 2, 64 * (n % 2)
                for h in range(2):
                    i = 2 * h + p
                    o = PS[b:b + 64, bA, h * 128:h * 128 + 128]
                    t = mm(o, blk(U, i)[:, b:b + 64], blk(bv, i), True, n == 0, v1, freeA, sig=(h == 1 and n == 0))
                    if n:
                        t = mm(o, blk(LT, i)[:, b:b + 64], blk(S, h), False, True, nw, St, sig=(h == 1))
                freeA = ut = acopy(u[b:b + 64, :], PS[b:b + 64, bA, 0:256], t, *start)
                yield
                for h in range(2):
                    i = 2 * h + p
                    o = PS[:, bC, h * 256 + n * 64:h * 256 + n * 64 + 64]
                    if n:
                        mm(o, blk(S, h), blk(qd, i)[:, b:b + 64], True, False, qd_, St)
                    tC = mm(o, u[b:b + 64, h * 128:h * 128 + 128], dT[b:b + 64, i * 128 + b:i * 128 + b + 64], n == 0,
                            True, ut, freeC, qk, sig=(h == 1))
                if n < 3:
                    for h in range(2):
                        i = 2 * h + p
                        t = mm(PS[:, bB, h * 128:h * 128 + 128], kdc[b:b + 64, i * 128:i * 128 + 128],
                               u[b:b + 64, h * 128:h * 128 + 128], True, True, k2, freeB, sig=(h == 1))
                    for h in range(2):
                        if n == 0:
                            St = vcopy(blk(S, h), PS[:, bB, h * 128:h * 128 + 128], t, *start)
                        else:
                            cc = CDK[:, n * 24 + 2 * g + h:n * 24 + 2 * g + h + 1]
                            St = stt(blk(S, h), blk(S, h), cc, PS[:, bB, h * 128:h * 128 + 128], ALU.mult, ALU.add, t, St)
                    freeB = St
                yield
            yt = acopy(tile(VT, 2 * g, 2), PS[:, bC, :], tC)
            y_t[g] = yt
            bankfree[bA], bankfree[bB], bankfree[bC] = freeA, freeB, yt
            slot_t[s] = yt
            gdone.append(yt)

        zu = z_units()
        live = []
        nextg = 0
        while nextg < 12 or live:
            if nextg < 12 and (len(live) < 2):
                if not live or nextg < 12:
                    live.append(group(nextg))
                    nextg += 1
                    if len(live) == 1:
                        for _ in range(6):
                            next(live[0], None)
                            next(zu, None)
            for x in list(live):
                try:
                    next(x)
                except StopIteration:
                    live.remove(x)
                next(zu, None)
        drain(zu)
        if stage == 2:
            load(G, dbg[:, 0:6144], VT, y_t[11], y_t[10], store=True)
            return finish()

        YH, YL = r(0, 8192), r(88, 8192)
        sqf = [None, None]
        bf = [bankfree[2], bankfree[3]]
        z_last = ztok[31]
        zpe = unit_done[0]
        rms_t = []
        for c in range(12):
            j = c % 2
            sq = f(120 + 2 * j, 512)
            rt = f(124 + 2 * j, 512)
            y = VT[:, c * 512:c * 512 + 512]
            s = tt(G, sq, y, y, ALU.mult, y_t[10], y_t[11], sqf[j])
            t = mm(PS[:, 2 + j, :], C("ones"), sq, True, True, s, bf[j], bankfree[5], bankfree[6], bankfree[7], sig=True)
            sqf[j] = t
            bf[j] = a = act(rt, PS[:, 2 + j, :], ACT.Sqrt, t, rms_t[-2] if c >= 2 else None, scale=1.0 / 128,
                            bias=C("eps6"))
            a = recip(rt, rt, a)
            rms_t.append(stt(y, y, vc("outg"), rt, ALU.mult, ALU.mult, a))
        xlast = cross_end[0]
        gate_t = []

        def gate(i):
            z = ztile(i)
            y = tile(VT, i) if i < 24 else tile(XA, i - 24)
            s = act(z, z, ACT.Silu, ztok[i])
            p = tt(V, z, z, y, ALU.mult, s, rms_t[-1], xlast)
            hi = acopy(tile(YH, i), z, p, zpe)
            gate_t.append(tt(V, tile(YL, i), z, tile(YH, i).bitcast(F), ALU.subtract, hi, zpe))

        for i in range(32):
            gate(i)
        X1 = f(32, 4096)
        X1H, X1L = r(48, 4096), r(64, 4096)
        t_x = load(G, X1, D["xT"], gate_t[-1])
        Y3, W3 = k3(YH), k3(YL)
        x1_t = []
        for m in range(16):
            b = m % 2
            drain(unit(Y3, W3, b, gate_t[15], free[b], stop=False))
            drain(unit(Y3[:, 16:32, :], W3[:, 16:32, :], b, gate_t[31], start=False))
            free[b] = a = tt(V, tile(X1, m), PS[:, b, 0:256], tile(X1, m), ALU.add, unit_done[0], t_x)
            hi = acopy(tile(X1H, m), tile(X1, m), a)
            x1_t.append(tt(V, tile(X1L, m), tile(X1, m), tile(X1H, m).bitcast(F), ALU.subtract, hi, a))
        if stage == 3:
            load(G, dbg[:, 0:4096], X1, x1_t[-1], store=True)
            return finish()
        wo_pe = unit_done[0]

        P3, Q3 = k3(X1H), k3(X1L)
        QI, KI, KK, QQ = f(0, 2048), f(8, 256), f(9, 2048), f(17, 2048)
        WI = f(25, 32).rearrange("p (a h) -> p a h", a=2)
        SC, WK, MM = f(26, 512), f(28, 512), f(30, 512)
        VN = f(80, 2048).rearrange("p (m c) -> p m c", m=2)
        HK = f(88, 2048).rearrange("p (h x) -> p h x", h=8)
        PT_ = f(96, 2048)
        XH2, XL2 = r(104, 4096), r(120, 4096)
        HOT, RB, BV = f(96, 384)[0:32, :], f(98, 8)[0:32, :], f(99, 384)[0:8, :]
        t1 = load(G, HOT, D["hot"], gate_t[-1], wo_pe)
        t2 = load(G, RB, D["rb"])
        t = mm(PS[0:8, 2, 0:384], RB, HOT, True, True, t1, t2, bf[0], sig=True)
        t = vcopy(BV, PS[0:8, 2, 0:384], t)
        sv = load(G, scratch["bias"], BV, t, store=True)
        hsrc = scratch["bias"]
        hank = bass.AP(hsrc.tensor, hsrc.offset, [[1, 128], [384, 8], [1, 256]])
        t_hk = load(G, HK, hank, sv, wo_pe)

        T1 = f(136, 256)
        drain(unit(P3, Q3, 0, x1_t[-1], free[0]))
        free[0] = a = vcopy(T1, PS[:, 0, 0:256], unit_done[0], wo_pe)
        t_ki = vcopy(KI[0:64, :], T1[0:64, :], a)
        t_ki2 = load(G, KI[64:128, :], T1[0:64, :], a)
        for p in range(2):
            t = tr(PS[:, 2, p * 128:p * 128 + 128], T1[:, p * 128:p * 128 + 128], a, t, sig=True)
        t_wi = ts(V, WI, PS[:, 2, 0:256].rearrange("p (a c) -> p a c", a=2)[:, :, 64:80], 1.0 / 32, None, ALU.mult,
                  None, t)
        bk = {i: t_wi for i in range(2, 8)}
        rel_free = [None] * 4
        it = 0
        sc_t = t_wi
        for i in range(8):
            b = i % 2
            drain(unit(P3, Q3, b, free[b]))
            free[b] = q_ = acopy(tile(QI, i), PS[:, b, 0:256], unit_done[0])
            for hh in (2 * i, 2 * i + 1):
                o = 64 * (hh % 2)
                for p in range(2):
                    S_ = 128 * (p + 1)
                    kb_ = 2 + it % 6
                    t = mm(PS[:, kb_, 0:S_], tile(QI, i)[o:o + 64, p * 128:p * 128 + 128], KI[o:o + 64, 0:S_], True, True,
                           q_, t_ki, t_ki2, bk[kb_], sig=True)
                    rl = f(136 + it % 4, S_)
                    bk[kb_] = a = act(rl, PS[:, kb_, 0:S_], ACT.Relu, t, rel_free[it % 4], t_wi)
                    sc = SC[:, p * 256:p * 256 + S_]
                    if hh == 0:
                        sc_t = ts(V, sc, rl, WI[:, p, hh:hh + 1], None, ALU.mult, None, a, wo_pe)
                    else:
                        sc_t = stt(sc, rl, WI[:, p, hh:hh + 1], sc, ALU.mult, ALU.add, a, sc_t)
                    rel_free[it % 4] = sc_t
                    it += 1
        mx8 = f(25.5, 8)

        def topk():
            for p in range(2):
                S_ = 128 * (p + 1)
                sc, wk, m = (X[:, p * 256:p * 256 + S_] for X in (SC, WK, MM))
                d = slice(S_ - 128, S_)
                t = tt(V, sc[:, d], sc[:, d], C("causal"), ALU.add, sc_t)
                src = sc
                for k in range(8):
                    t = V.do(lambda e, src=src: e.max(out=mx8, in_=src), t)
                    t = V.do(lambda e, src=src, wk=wk: e.match_replace(out=wk, in_to_replace=mx8, in_values=src,
                                                                       imm_value=-3e38), t)
                    src = wk
                    yield
                t = ts(V, m, wk, -2e38, -BIG, ALU.is_gt, ALU.mult, t)
                t = tt(V, m[:, d], m[:, d], C("causal"), ALU.add, t)
                m_t.append(t)
                yield

        m_t = []
        tk = topk()
        kq_t = []
        for i in range(16):
            b = i % 2
            drain(unit(P3, Q3, b, free[b]))
            if i < 8:
                free[b] = acopy(tile(KK, i), PS[:, b, 0:256], unit_done[0])
            else:
                free[b] = A.do(lambda e, i=i, b=b: e.mul(tile(QQ, i - 8), PS[:, b, 0:256], 128.0 ** -0.5), unit_done[0])
            kq_t.append(free[b])
            next(tk, None)
            next(tk, None)
        drain(tk)
        vt = [None, None]
        for i in range(8):
            b = i % 2
            drain(unit(P3, Q3, b, free[b]))
            tmp = f(136 + b, 256)
            free[b] = t = acopy(tmp, PS[:, b, 0:256], unit_done[0], vt[b], sc_t)
            for m in range(2):
                t = tr(PS[:, 2 + b, m * 128:m * 128 + 128], tmp[:, m * 128:m * 128 + 128], t, bk[2 + b], sig=(m == 1))
            vt[b] = t
            bk[2 + b] = vcopy(VN[:, :, i * 128:i * 128 + 128], PS[:, 2 + b, 0:256].rearrange("p (m c) -> p m c", m=2), t,
                              wo_pe)
        t_vn = bk[3]
        INV = f(136, 1024)
        t_inv = load(G, INV, D["inv"], vt[0], vt[1])
        x2_t = {}
        att = [None]

        def attention():
            it = 0
            pf = [None] * 2
            ptf = [None] * 2
            for h in range(8):
                PT = f(4 + 2 * (h % 2), 384)
                for p in range(2):
                    S_ = 128 * (p + 1)
                    kb_ = 2 + it % 2
                    P = f(it % 2, S_)
                    st = f(2 + it % 2, 8)
                    mm(PS[:, kb_, 0:S_], tile(QQ, h)[:, p * 128:p * 128 + 128], tile(KK, h)[:, 0:S_], True, False,
                       kq_t[-1], bk[kb_])
                    t = mm(PS[:, kb_, 0:S_], C("flip"), HK[:, h, 256 - S_:256], False, True, t_hk, sig=True)
                    bk[kb_] = a = tt(V, P, PS[:, kb_, 0:S_], MM[:, p * 256:p * 256 + S_], ALU.add, t, m_t[-1],
                                     pf[it % 2], sc_t)
                    a = V.do(lambda e, st=st, P=P: e.tensor_reduce(st[:, 0:1], P, AX.X, ALU.max, negate=True), a)
                    a = act(P, P, ACT.Exp, a, bias=st[:, 0:1], acc=st[:, 2:3])
                    a = recip(st[:, 3:4], st[:, 2:3], a)
                    a = ts(V, P, P, st[:, 3:4], None, ALU.mult, None, a)
                    yield
                    b2 = 4 + it % 2
                    for m in range(p + 1):
                        t = tr(PS[:, b2, m * 128:m * 128 + 128], P[:, m * 128:m * 128 + 128], a, bk[b2], sig=(m == p))
                    pf[it % 2] = t
                    bk[b2] = cp = vcopy(PT[:, p * 128:p * 128 + S_], PS[:, b2, 0:S_], t, ptf[h % 2])
                    it += 1
                    yield
                b3 = 6 + h % 2
                mm(PS[:, b3, 0:128], VN[:, 0, h * 128:h * 128 + 128], PT[:, 0:128], True, True, cp, t_vn, bk[b3])
                mm(PS[:, b3, 128:256], VN[:, 0, h * 128:h * 128 + 128], PT[:, 128:256], True, False)
                t = mm(PS[:, b3, 128:256], VN[:, 1, h * 128:h * 128 + 128], PT[:, 256:384], False, True, sig=True)
                ptf[h % 2] = t
                hi = acopy(tile(XH2, 8 + h), PS[:, b3, 0:256], t, wo_pe, sc_t)
                bk[b3] = lo = tt(V, tile(XL2, 8 + h), PS[:, b3, 0:256], tile(XH2, 8 + h).bitcast(F), ALU.subtract, hi)
                x2_t[8 + h] = lo
                att[0] = t
                yield

        ping = [f(26, 256), f(28, 256)]

        def pool_units():
            prev = m_t[-1]
            for c in range(8):
                b = c % 2
                yield from unit(P3, Q3, b, free[b])
                x = tile(PT_, c)
                free[b] = a = acopy(x, PS[:, b, 0:256], unit_done[0], t_hk)
                cur = x
                for k in range(c // 2 + 1):
                    st = 1 << k
                    nx = ping[k % 2]
                    a = tt(G, nx[:, st:256], cur[:, st:256], cur[:, 0:256 - st], ALU.add, a, prev)
                    a = G.do(lambda e, nx=nx, cur=cur, st=st: e.tensor_copy(nx[:, 0:st], cur[:, 0:st]), a)
                    cur = nx
                a = tt(G, cur, cur, INV[:, (c // 2) * 256:(c // 2) * 256 + 256], ALU.mult, a, t_inv)
                prev = tt(G, x, cur, x, ALU.subtract, a)
                pool_t.append(prev)

        pool_t = []
        together(attention(), pool_units())
        PW = f(88, 2048).rearrange("p (g d) -> p g d", g=8)
        t_pw = load(G, PW, D["pw"], att[0])
        for g in range(4):
            for d in range(2):
                kb_ = 2 + (2 * g + d) % 6
                for c in range(2):
                    t = mm(PS[:, kb_, 0:256], PW[:, 2 * g + c, d * 128:d * 128 + 128], tile(PT_, 2 * g + c), c == 0, c == 1,
                           t_pw, pool_t[-1], bk[kb_], sig=(c == 1))
                i = 2 * g + d
                hi = act(tile(XH2, i), PS[:, kb_, 0:256], ACT.Identity, t, scale=vc("pools", i))
                bk[kb_] = x2_t[i] = stt(tile(XL2, i), PS[:, kb_, 0:256], vc("pools", i), tile(XH2, i).bitcast(F), ALU.mult,
                                        ALU.subtract, hi)
        if stage == 4:
            load(G, dbg[:, 0:4096].bitcast(R), XH2, x2_t[7], x2_t[15], store=True)
            load(G, dbg[:, 4096:8192].bitcast(R), XL2, x2_t[7], x2_t[15], store=True)
            return finish()
        Z3, R3 = k3(XH2), k3(XL2)
        r1_t = []
        for m in range(16):
            b = m % 2
            drain(unit(Z3, R3, b, x2_t[7], x2_t[15], free[b]))
            free[b] = stt(tile(X1, m), tile(X1, m), ALPHA, PS[:, b, 0:256], ALU.mult, ALU.add, unit_done[0])
            r1_t.append(free[b])
        mix_pe = unit_done[0]

        MU, RS, SQ = f(80, 256), f(81, 256), f(104, 4096)
        for kt in range(16):
            t = mm(PS[:, 2, 0:256], C("ones"), tile(X1, kt), kt == 0, kt == 15, r1_t[kt], bk[2], sig=(kt == 15))
        a = ts(V, MU, PS[:, 2, 0:256], 1.0 / 2048, None, ALU.mult, None, t)
        sq = []
        for c in range(4):
            x = k3(X1)[:, 4 * c:4 * c + 4, :]
            a2 = tt(V, x, x, bc(MU, 4), ALU.subtract, a)
            sq.append(act(k3(SQ)[:, 4 * c:4 * c + 4, :], x, ACT.Square, a2, mix_pe))
        for kt in range(16):
            t = mm(PS[:, 3, 0:256], C("ones"), tile(SQ, kt), kt == 0, kt == 15, sq[kt // 4], bk[3], sig=(kt == 15))
        s_ = act(RS, PS[:, 3, 0:256], ACT.Sqrt, t, att[0], scale=1.0 / 2048, bias=C("eps5"))
        s_ = recip(RS, RS, s_)
        H2H, H2L = r(0, 4096), r(16, 4096)
        hh_t = []
        for c in range(4):
            x = k3(X1)[:, 4 * c:4 * c + 4, :]
            a = tt(V, x, x, bc(RS, 4), ALU.mult, s_, *sq)
            for kt in range(4 * c, 4 * c + 4):
                x1 = tile(X1, kt)
                b_ = ts(V, x1, x1, vc("ln1g", kt), vc("ln1b", kt), ALU.mult, ALU.add, a)
                hi = acopy(tile(H2H, kt), x1, b_)
                hh_t.append(tt(V, tile(H2L, kt), x1, tile(H2H, kt).bitcast(F), ALU.subtract, hi))
        E3, O3 = k3(H2H), k3(H2L)
        stg = f(104, 4096).rearrange("p (a d) -> p a d", a=2)
        bb = {i: (bk[i] if i > 3 else s_) for i in range(2, 8)}
        it = 0
        for p in range(2):
            for c in range(4):
                kb_ = 2 + it % 6
                it += 1
                for k in range(4):
                    t = tr(PS[:, kb_, k * 128:k * 128 + 128], tile(X1, 4 * c + k)[:, p * 128:p * 128 + 128], hh_t[-1], bb[kb_],
                           s_, sig=(k == 3))
                bb[kb_] = acopy(stg[:, p, c * 512:c * 512 + 512], PS[:, kb_, :], t)
        h_tr = t
        t_sc = load(G, scratch["h"], stg, bb[kb_], store=True)
        if stage == 5:
            load(G, dbg[:, 0:4096], X1, hh_t[-1], store=True)
            return finish()

        SUB = f(92, 256).rearrange("p (s k) -> p s k", s=2)
        t_sub = load(G, SUB, D["sub"], mix_pe, x2_t[7])
        QH = f(76, 4096)
        ST = f(60, 4096).rearrange("p (a s h k) -> p a s h k", a=2, s=2, h=8)
        CAND, WRK = f(32, 2048), f(40, 2048)
        VAL, IDX, IDF = f(48, 512), f(50, 512).bitcast(U32), f(52, 512)
        val = VAL.rearrange("p (q k) -> p q k", k=16)
        idx = IDX.rearrange("p (q k) -> p q k", k=16)
        idf = IDF.rearrange("p (q k) -> p q k", k=16)
        BST, POS = f(54, 128), f(54.5, 128).bitcast(U32)
        POA, POB = f(55, 128), f(55.5, 128)
        PUA = f(56, 128).bitcast(U32)
        SEL = f(56.5, 128)
        I1T, I2T, GTT = f(57, 256), f(58, 256), f(59, 256)
        sel_done = []

        def top16(vals, v16, i16, wk, *t):
            a = V.do(lambda e: e.max(out=v16[:, 0:8], in_=vals), *t)
            V.do(lambda e: e.max_index(out=i16[:, 0:8], in_max=v16[:, 0:8], in_values=vals), a)
            c = V.do(lambda e: e.match_replace(out=wk, in_to_replace=v16[:, 0:8], in_values=vals, imm_value=-3e38), a)
            d = V.do(lambda e: e.max(out=v16[:, 8:16], in_=wk), c)
            return V.do(lambda e: e.max_index(out=i16[:, 8:16], in_max=v16[:, 8:16], in_values=wk), d)

        def keys16(hs, t):
            for p in range(2):
                o = (2 * hs + p) % 16 * 128
                top_t[p] = top16(ST[:, p, hs % 2, hs // 2, :], val[:, 16 * p + hs, :], idx[:, 16 * p + hs, :],
                                 WRK[:, o:o + 128], t, h_tr, mix_pe)

        top_t = {}

        def select():
            v4 = val.rearrange("p (a q) k -> p a q k", a=2)
            i4 = idf.rearrange("p (a q) k -> p a q k", a=2)
            cand = CAND.rearrange("p (h a b) -> p h a b", h=8, a=16)
            bst = BST.rearrange("p (h k) -> p h k", k=16)
            pos = POS.rearrange("p (h k) -> p h k", k=16)
            hot = CAND.rearrange("p (k a) -> p k a", a=16)
            sel3 = SEL.rearrange("p (h k) -> p h k", k=16)
            prev = vcopy(IDF, IDX, top_t[0], top_t[1])
            for p in range(2):
                for h in range(8):
                    c = tt(V, cand[:, h, :, :], bc(v4[:, p, 2 * h, :], 16, 2), bc(v4[:, p, 2 * h + 1, :], 16), ALU.add,
                           prev)
                    if h % 4 == 3:
                        yield
                for h in range(8):
                    t = top16(CAND[:, h * 256:h * 256 + 256], bst[:, h, :], pos[:, h, :],
                              WRK[:, h * 256:h * 256 + 256], c)
                    yield
                a = ts(V, PUA, POS, 4, None, ALU.logical_shift_right, None, t)
                a = vcopy(POA, PUA, a)
                b = ts(V, PUA, POS, 15, None, ALU.bitwise_and, None, a)
                b = vcopy(POB, PUA, b)
                out_ = t
                for which, P_ in ((0, POA), (1, POB)):
                    c = tt(V, hot, bc(P_, 16, 2), bc(C("iota16"), 128), ALU.is_equal, a, b, out_)
                    yield
                    for h in range(8):
                        c2 = tt(V, hot[:, 16 * h:16 * h + 16, :], hot[:, 16 * h:16 * h + 16, :],
                                bc(i4[:, p, 2 * h + which, :], 16), ALU.mult, c)
                    yield
                    c = V.do(lambda e: e.tensor_reduce(SEL, hot, AX.X, ALU.add), c2, out_)
                    t3 = tr(PS[:, 2, which * 128:which * 128 + 128], SEL, c, bb[2], sig=True)
                    yield
                    out_ = bb[2] = vcopy((I1T, I2T)[which][:, p * 128:p * 128 + 128],
                                         PS[:, 2, which * 128:which * 128 + 128], t3)
                a = tt(V, sel3, bst, bst[:, :, 0:1].broadcast_to([128, 8, 16]), ALU.subtract, out_)
                a = act(SEL, SEL, ACT.Exp, a)
                yield
                sm_ = POA[:, 0:8]
                b = V.do(lambda e: e.tensor_reduce(sm_, sel3, AX.X, ALU.add), a)
                b = recip(sm_, sm_, b)
                b = tt(V, sel3, sel3, bc(sm_, 16, 2), ALU.mult, b)
                t3 = tr(PS[:, 2, 256:384], SEL, b, bb[2], sig=True)
                yield
                bb[2] = prev = vcopy(GTT[:, p * 128:p * 128 + 128], PS[:, 2, 256:384], t3)
            sel_done.append(prev)

        s_t = []
        for i in range(16):
            b = i % 2
            drain(unit(E3, O3, b, hh_t[-1], free[b]))
            free[b] = a = acopy(f(76 + (i % 4), 256), PS[:, b, 0:256], unit_done[0], s_t[i - 4][1] if i >= 4 else mix_pe,
                                hh_t[-1])
            kb_ = 2 + i % 2
            for p in range(2):
                t = mm(PS[:, kb_, p * 128:p * 128 + 128], f(76 + (i % 4), 256)[:, p * 128:p * 128 + 128], SUB[:, i % 2, :],
                       True, True, a, t_sub, bb[kb_], sig=(p == 1))
            bb[kb_] = a = acopy(ST[:, :, i % 2, i // 2, :], PS[:, kb_, 0:256].rearrange("p (a k) -> p a k", a=2), t, mix_pe)
            s_t.append((a, t))
            if i >= 1:
                keys16(i - 1, s_t[i - 1][0])
        keys16(15, s_t[15][0])
        qh_pe = s_t[-1][1]
        if stage == 6:
            load(G, dbg[:, 0:4096], f(60, 4096), s_t[-1][0], store=True)
            return finish()

        CC = f(76, 16384)
        C3 = CC.rearrange("p (j t) -> p j t", t=256)
        ACC = f(60, 4096)
        O1 = f(32, 2048).rearrange("p (b k i) -> p b k i", b=4, k=4)
        O2 = f(40, 1024).rearrange("p (b k i) -> p b k i", b=4, k=4)
        CTH, CTL = r(44, 512), r(46, 512)
        GT = f(48, 512)
        sel = select()
        pe_free = {"o": [None] * 4, "ct": [None, None], "gt": [None, None]}
        c_free = [t_sc, qh_pe]
        hot_t, mm_t = {}, {}
        quad_last = [None]
        gelu_last = [None]

        def gate_hots(q, half):
            ob = q % 4
            for k in range(4):
                t = 4 * q + k
                ts(V, O1[:, ob, k, :], C("iota"), I1T[:, t:t + 1], GTT[:, t:t + 1], ALU.is_equal, ALU.mult,
                   sel_done[0], pe_free["o"][ob])
                b = ts(V, O2[:, ob, k, :], C("iota")[:, 64 * half:64 * half + 64], I2T[:, t:t + 1], None, ALU.is_equal,
                       None)
            hot_t[q] = b

        def gate_mm(q):
            ob, bank = q % 4, 3 + q % 4
            for k in range(4):
                m = mm(PS[:, bank, k * 64:k * 64 + 64], O1[:, ob, k, :], O2[:, ob, k, :], True, True, hot_t[q], bb[bank],
                       sig=(k == 3))
            pe_free["o"][ob] = mm_t[q] = m

        def gate_apply(q, jdone):
            bank = 3 + q % 4
            g = PS[:, bank, 0:256].rearrange("p (t j) -> p j t", t=4)
            tcol = slice(4 * q, 4 * q + 4)
            x = mm_t[q]
            if jdone:
                x = tt(V, C3[:, 0:jdone, tcol], C3[:, 0:jdone, tcol], g[:, 0:jdone, :], ALU.mult, x, gelu_last[0])
            if jdone < 64:
                x = vcopy(C3[:, jdone:64, tcol], g[:, jdone:64, :], x, *c_free)
            bb[bank] = quad_last[0] = x

        v_evac = {}
        for half in range(2):
            hots = mms = applied = 0
            quad_last[0] = None
            gm = None
            for j in range(64):
                b = j % 2
                due = 64 if j >= 60 else (j + 2 if half else int(64 * max(0, j - 23) / 37))
                due = min(due, hots + 2, 64) if sel_done else 0
                work = [lambda q=q: gate_apply(q, j) for q in range(applied, mms)]
                work += [lambda q=q: gate_mm(q) for q in range(mms, hots)]
                work += [lambda q=q: gate_hots(q, half) for q in range(hots, due)]
                applied, mms, hots = mms, hots, max(due, hots)
                for _ in unit(E3, O3, b, free[b], per=6):
                    if half == 0 and not sel_done:
                        next(sel, None)
                    if work:
                        work.pop(0)()
                for x in work:
                    x()
                tq = 4 * applied
                gtmp = GT[:, b * 256:b * 256 + 256]
                if tq:
                    ga = free[b] = act(gtmp[:, 0:tq], PS[:, b, 0:tq], ACT.Gelu, unit_done[0], pe_free["gt"][b])
                if tq < 256:
                    free[b] = gelu_last[0] = act(C3[:, j, tq:256], PS[:, b, tq:256], ACT.Gelu, unit_done[0], *c_free)
                if tq:
                    pe_free["gt"][b] = gm = tt(G, C3[:, j, 0:tq], C3[:, j, 0:tq], gtmp[:, 0:tq], ALU.mult, ga,
                                               quad_last[0])
            while applied < 64:
                for q in range(applied, mms):
                    gate_apply(q, 64)
                for q in range(mms, hots):
                    gate_mm(q)
                for q in range(hots, min(hots + 2, 64)):
                    gate_hots(q, half)
                applied, mms, hots = mms, hots, min(hots + 2, 64)
            if stage == 7 and half == 0:
                load(G, dbg[:, 0:16384], CC, quad_last[0], gelu_last[0], gm, store=True)
                return finish()
            start_wait = [bb[i] for i in range(2, 8)] + [free[0], free[1]]
            for j in range(64):
                n = un[0]
                un[0] += 1
                c = j % 2
                ch, cl_ = CTH[:, c * 256:c * 256 + 256], CTL[:, c * 256:c * 256 + 256]
                hi = acopy(ch, C3[:, j, :], quad_last[0], gm, pe_free["ct"][c])
                lo = tt(V, cl_, C3[:, j, :], ch.bitcast(F), ALU.subtract, hi)
                for h in range(2):
                    prep_ahead(n, h)
                    kk_ = (n % 2) * 2 + h
                    for tp in range(2):
                        cth, ctl = ch[:, tp * 128:tp * 128 + 128], cl_[:, tp * 128:tp * 128 + 128]
                        for lhs, W, st_, sp_ in ((cth, WH, True, False), (cth, WL, False, False), (ctl, WH, False, True)):
                            for d in range(2):
                                m = mm(PS[:, 4 * tp + 2 * h + d, :], lhs, W[:, kk_, d * 512:d * 512 + 512],
                                       st_ and j == 0, sp_ and j == 63, lo, ready[(n, h)], *start_wait,
                                       sig=(d == 1 and sp_))
                    used[(n, h)] = m
                start_wait = []
                pe_free["ct"][c] = m
            vdone = m
            if half == 0:
                for i in range(8):
                    if i % 2:
                        e_ = acopy(ACC[:, i * 512:i * 512 + 512], PS[:, i, :], vdone, sel_done[0])
                    else:
                        e_ = vcopy(ACC[:, i * 512:i * 512 + 512], PS[:, i, :], vdone)
                    if i < 2:
                        free[i] = e_
                    else:
                        bb[i] = e_
                    v_evac[i] = e_
                c_free = [lo, hi]

        HN = f(76, 4096)
        LG, LB = f(92, 2048), f(100, 2048)
        t_h = load(G, HN, scratch["h"].rearrange("p a d -> p (a d)"), lo, hi, t_sc)
        t_g = load(G, LG, D["ln2g"])
        t_b = load(G, LB, D["ln2b"])
        t = stt(ACC, HN, ALPHA, ACC, ALU.mult, ALU.add, t_h, v_evac[7], v_evac[6])
        mu = f(108, 16)
        for p in range(2):
            X = ACC[:, p * 2048:p * 2048 + 2048]
            for d in range(4):
                t = tt(V, X[:, d * 512:d * 512 + 512], X[:, d * 512:d * 512 + 512], PS[:, 4 * p + d, :], ALU.add, t, vdone)
            o = 4 * p
            a = V.do(lambda e, X=X, o=o: e.tensor_reduce(mu[:, o:o + 1], X, AX.X, ALU.add), t)
            a = ts(V, mu[:, o:o + 1], mu[:, o:o + 1], 1.0 / 2048, None, ALU.mult, None, a)
            a = ts(V, X, X, mu[:, o:o + 1], None, ALU.subtract, None, a)
            a2 = act(HN[:, p * 2048:p * 2048 + 2048], X, ACT.Square, a, acc=mu[:, o + 1:o + 2])
            a2 = act(mu[:, o + 2:o + 3], mu[:, o + 1:o + 2], ACT.Sqrt, a2, scale=1.0 / 2048, bias=C("eps5"))
            a2 = recip(mu[:, o + 3:o + 4], mu[:, o + 2:o + 3], a2)
            a2 = stt(X, X, mu[:, o + 3:o + 4], LG, ALU.mult, ALU.mult, a2, t_g)
            a2 = tt(V, X, X, LB, ALU.add, a2, t_b)
            load(SP, out[0, p * 128:p * 128 + 128, :], X, a2, store=True)

        finish()


def layout(inputs):
    a = {k: np.asarray(v) for k, v in inputs.items()}

    def tiles(w):
        k, c = w.shape
        return np.ascontiguousarray(w.reshape(k // 2048, 16, 128, c // 128, 128).transpose(3, 0, 2, 1, 4)).reshape(
            (k // 2048) * (c // 128), 128, 2048)

    def turned(x):
        return np.ascontiguousarray(x.T.reshape(16, 128, 256).transpose(1, 0, 2)).reshape(128, 4096)

    def cols(g):
        return g.reshape(-1, 128).T

    w = a["dn_w_in"][0]
    w2 = a["w_in_2"][0]
    vec = np.concatenate([
        cols(a["norm_g"][0]), cols(a["mem_norm_g"]),
        a["dn_conv_w"][0].reshape(4, 48, 128).transpose(2, 1, 0).reshape(128, 192),
        cols(a["ln1_g_2"][0]), cols(a["ln1_b_2"][0]), cols(a["xa_q_norm_g"][0]), cols(a["xa_k_norm_g"][0]),
        cols(a["dn_out_norm_g"][0]), cols(a["pool_scale_2"][0]),
        np.broadcast_to(a["dn_a_log"], (128, 24)), np.broadcast_to(a["dn_dt_bias"], (128, 24))], axis=1)
    con, inv, hot = constants()
    return {
        "con": con, "inv": inv, "hot": hot, "vec": np.ascontiguousarray(vec),
        "xT": turned(a["x"][0]), "memT": turned(a["mem"][0]),
        "w_kv": tiles(a["mem_w_kv"][0]),
        "w_qkv": tiles(w[:, 0:6144]), "w_ab": tiles(w[:, 6144:6272]), "w_xq": tiles(w[:, 6192:7216]),
        "w_z": tiles(w[:, 7216:11312]), "w_o": tiles(a["w_out"][0]),
        "w2": tiles(w2[:, 0:5120]),
        "w2_kiwi": tiles(np.concatenate([w2[:, 5120:5200], w2[:, 5072:5120]], axis=1)),
        "rb": a["rel_bias_2"],
        "pw": np.ascontiguousarray(a["pool_w_2"][0].reshape(4, 2, 128, 256).transpose(2, 0, 1, 3)).reshape(128, 2048),
        "w_o2": tiles(a["w_out_2"][0]), "w_q2": tiles(a["peer_wq_2"][0]),
        "sub": np.ascontiguousarray(a["peer_subkeys_2"][0].transpose(2, 0, 1)),
        "pu": np.ascontiguousarray(a["peer_u_2"][0].reshape(128, 128, 16, 128).transpose(1, 3, 2, 0)).reshape(
            128, 128, 2048),
        "pv": np.ascontiguousarray(a["peer_v_2"][0]),
        "ln2g": np.ascontiguousarray(np.broadcast_to(a["ln2_g_2"], (128, 2048))),
        "ln2b": np.ascontiguousarray(np.broadcast_to(a["ln2_b_2"], (128, 2048))),
    }


def kernel(**inputs):
    import concourse.bacc as bacc
    from concourse.bass_utils import run_bass_kernel_spmd

    nc = bacc.Bacc("TRN2", target_bir_lowering=False, num_devices=1)
    arrays = layout(inputs)
    D = {k: nc.dram_tensor(f"in_{k}", v.shape, mybir.dt.from_np(v.dtype), kind="ExternalInput").ap()
         for k, v in arrays.items()}
    out = nc.dram_tensor("out_0", (1, 256, 2048), F, kind="ExternalOutput").ap()
    scratch = {"bias": nc.dram_tensor("s_bias", (8, 384), F, kind="Internal").ap(),
               "h": nc.dram_tensor("s_h", (128, 2, 2048), F, kind="Internal").ap()}
    build(nc, D, out, scratch)
    res = run_bass_kernel_spmd(nc, [{f"in_{k}": v for k, v in arrays.items()}], core_ids=[0])
    return res.results[0]["out_0"]
```

```python
import math
from contextlib import ExitStack

import numpy as np
import concourse.bass as bass
from concourse import mybir

F = mybir.dt.float32
R = mybir.dt.float32r
U32 = mybir.dt.uint32
ALU = mybir.AluOpType
ACT = mybir.ActivationFunctionType
AX = mybir.AxisListType

KB = 256
NRAW = 3
ALPHA = 2.0 ** 0.25
BIG = 1e30
SEL_RATE = 0.27
NZ0 = 2
FILL = 1.3
LEVELS = (2, 4, 8, 16, 32)

CON = {}
_off = 0
for _n, _w in (("ident", 128), ("tri", 128), ("blk", 128), ("mt", 128), ("ms", 128), ("nm1", 128),
               ("nmt1", 128), ("mt2", 128), ("mt4", 128), ("mt8", 128), ("mt16", 128), ("mt32", 128),
               ("flip", 128), ("ones", 128), ("iota", 128), ("causal", 128), ("chunk", 2), ("iota16", 16),
               ("eps6", 1), ("eps5", 1)):
    CON[_n] = (_off, _w)
    _off += _w
NCON = _off

VEC = {}
_off = 0
for _n, _w in (("norm_g", 16), ("mem_g", 16), ("conv", 192), ("ln1g", 16), ("ln1b", 16), ("xaq", 2), ("xak", 2),
               ("outg", 1), ("pools", 8), ("alog", 24), ("dtb", 24)):
    VEC[_n] = (_off, _w)
    _off += _w
NVEC = _off


def constants():
    c = np.zeros((128, NCON), np.float32)
    p = np.arange(128)[:, None]
    x = np.arange(128)[None, :]
    same = (p // 64) == (x // 64)

    def put(name, a):
        o, w = CON[name]
        c[:, o:o + w] = a

    put("ident", p == x)
    put("tri", (p <= x) & same)
    put("blk", same)
    put("mt", np.where((p <= x) & same, 0.0, -BIG))
    put("ms", np.where((x < p) & same, 0.0, BIG))

    def low(s):
        return ((p // (2 * s)) == (x // (2 * s))) & ((p // s) % 2 == 1) & ((x // s) % 2 == 0)

    put("nm1", -1.0 * low(1))
    put("nmt1", -1.0 * low(1).T)
    for s in LEVELS:
        put(f"mt{s}", low(s).T)
    put("flip", (p + x) == 127)
    put("ones", 1.0)
    put("iota", x + 0 * p)
    put("causal", np.where(x <= p, 0.0, -BIG))
    put("chunk", (p // 64) == np.arange(2)[None, :])
    put("iota16", np.arange(16)[None, :] + 0 * p)
    put("eps6", 1e-6)
    put("eps5", 1e-5)
    inv = np.stack([1.0 / np.minimum(np.arange(256) + 1, w) for w in (2, 4, 8, 16)]).astype(np.float32)
    inv = np.ascontiguousarray(np.broadcast_to(inv.reshape(1, 1024), (128, 1024)))
    dist = np.maximum(255 - np.arange(384), 0)
    d = np.maximum(dist, 1).astype(np.float32)
    large = 16 + (np.log(d / np.float32(16)) / np.float32(math.log(8.0)) * np.float32(16)).astype(np.int32)
    bucket = np.where(dist < 16, dist, np.minimum(large, 31))
    hot = (np.arange(32)[:, None] == bucket[None, :]).astype(np.float32)
    return c, inv, hot


class Queue:

    def __init__(self, sem):
        self.sem, self.items, self.n, self.seen = sem, [], 0, {}

    def wait(self, tok):
        if tok is None:
            return
        sem, value = tok
        key = sem.name
        if self.seen.get(key, 0) < value:
            self.seen[key] = value
            self.items.append(lambda e: e.wait_ge(sem, value))

    def do(self, fn, *waits, sig=True):
        for w in waits:
            self.wait(w)
        if not sig:
            self.items.append(fn)
            return None
        self.n += 1
        self.items.append(lambda e: fn(e).then_inc(self.sem, 1))
        return (self.sem, self.n)

    def dma(self, fn, sem, value, *waits):
        for w in waits:
            self.wait(w)
        self.items.append(lambda e: fn(e).then_inc(sem, 16))
        return (sem, value)


def build(nc, D, out, scratch, stage=99, dbg=None):
    ctx = ExitStack()
    with ctx:
        def sb(name, shape, dt):
            return ctx.enter_context(nc.sbuf_tensor(name, shape, dt))

        def semaphore(name):
            return ctx.enter_context(nc.semaphore(name))

        con = sb("cons", [128, NCON], F)
        vec = sb("vecs", [128, NVEC], F)
        keep = sb("keep", [128, 352], F)
        raw = sb("raw", [128, NRAW, 2048], F)
        WH = sb("WH", [128, 4, 1024], R)
        WL = sb("WL", [128, 4, 1024], R)
        PS = ctx.enter_context(nc.psum_tensor("PS", [128, 8, 512], F))

        PE = Queue(semaphore("pe"))
        V = Queue(semaphore("dve"))
        A = Queue(semaphore("act"))
        G = Queue(semaphore("pool"))
        SP = Queue(semaphore("sp"))

        views = {}

        def view(kb, n, dt):
            o = int(kb * KB)
            key = (o, n, dt)
            if key not in views:
                name = f"m{o}_{n}" + ("r" if dt == R else "")
                if o:
                    with nc.sbuf_tensor("pad_" + name, [128, o], F):
                        with nc.sbuf_tensor(name, [128, n], dt) as t:
                            pass
                else:
                    with nc.sbuf_tensor(name, [128, n], dt) as t:
                        pass
                views[key] = t[:, :]
            return views[key]

        def f(kb, n):
            return view(kb, n, F)

        def r(kb, n):
            return view(kb, n, R)

        def C(name):
            o, w = CON[name]
            return con[:, o:o + w]

        def vc(name, i=0, n=1):
            o, _ = VEC[name]
            return vec[:, o + i:o + i + n]

        def finish():
            for tok in last_store:
                SP.wait(tok)
            for tok in raw_in.values():
                SP.wait(tok)

            block = ctx.enter_context(nc.Block())

            def play(q):
                def body(e):
                    for item in q.items:
                        item(e)
                return body

            block.sync(play(SP))
            block.tensor(play(PE))
            block.vector(play(V))
            block.scalar(play(A))
            block.gpsimd(play(G))

        nload = [0]
        last_store = []

        def load(q, dst, src, *waits, store=False):
            nload[0] += 1
            s = semaphore(f"ld{nload[0]}")
            tok = q.dma(lambda e: e.dma_start(dst, src), s, 16, *waits)
            if store:
                last_store.append(tok)
            return tok

        def mm(o, l, x, start, stop, *waits, sig=False):
            return PE.do(lambda e: e.matmul(o, l, x, start=start, stop=stop), *waits, sig=sig)

        def tr(o, i, *waits, sig=False):
            return PE.do(lambda e: e.transpose(o, i, C("ident")), *waits, sig=sig)

        def tt(q, o, a, b, op, *waits):
            return q.do(lambda e: e.tensor_tensor(o, a, b, op), *waits)

        def ts(q, o, a, s1, s2, op0, op1, *waits):
            if op1 is None:
                return q.do(lambda e: e.tensor_scalar(o, a, s1, None, op0), *waits)
            return q.do(lambda e: e.tensor_scalar(o, a, s1, s2, op0, op1), *waits)

        def stt(o, a, s, b, op0, op1, *waits):
            return V.do(lambda e: e.scalar_tensor_tensor(out=o, in0=a, scalar=s, in1=b, op0=op0, op1=op1), *waits)

        def act(o, i, fn, *waits, scale=1.0, bias=0.0, acc=None):
            if acc is None:
                return A.do(lambda e: e.activation(o, i, fn, scale=scale, bias=bias), *waits)
            return A.do(lambda e: e.activation(o, i, fn, scale=scale, bias=bias, accum_out=acc), *waits)

        def acopy(o, i, *waits):
            return A.do(lambda e: e.copy(o, i), *waits)

        def vcopy(o, i, *waits):
            return V.do(lambda e: e.tensor_copy(o, i), *waits)

        def recip(o, i, *waits):
            return V.do(lambda e: e.reciprocal(o, i), *waits)

        def bc(ap, n, axis=1):
            w = ap.shape[1]
            return ap.unsqueeze(1).broadcast_to([128, n, w]) if axis == 1 else ap.unsqueeze(2).broadcast_to([128, w, n])

        units = []
        for i in range(16):
            units.append(D["w_kv"][i])
        units.append(D["w_ab"][0])
        for i in range(8):
            units.append(D["w_xq"][i])
        for i in range(12):
            units.append(D["w_qkv"][12 + i])
            units.append(D["w_qkv"][i])
        fill = [("v", i) for i in range(4)] + [("z", i) for i in range(NZ0)]
        nv, nz = 4, NZ0
        for g in range(10):
            fill += [("v", nv), ("v", nv + 1)]
            nv += 2
            for _ in range(3 if g % 3 == 0 else 2):
                if nz < 32:
                    fill.append(("z", nz))
                    nz += 1
        fill += [("z", i) for i in range(nz, 32)]
        for kind, i in fill:
            units.append(D["w_qkv"][24 + i] if kind == "v" else D["w_z"][i])
        for i in range(32):
            units.append(D["w_o"][i])
        units.append(D["w2_kiwi"][0])
        for g in (4, 2, 1, 3, 0):
            for i in range(8):
                units.append(D["w2"][8 * g + i])
        for i in range(16):
            units.append(D["w_o2"][i])
        for i in range(16):
            units.append(D["w_q2"][i])
        vv = D["pv"].rearrange("(i j) d -> j i d", j=128)
        for half in range(2):
            for j in range(64):
                units.append(D["pu"][64 * half + j])
            for j in range(64):
                units.append(vv[64 * half + j])
        raw_sem = [semaphore(f"raw{i}") for i in range(NRAW)]
        raw_in = {}
        ready = {}
        used = {}

        def issue(n, *waits):
            if n < len(units):
                raw_in[n] = SP.dma(lambda e: e.dma_start(raw[:, n % NRAW, :], units[n]),
                                   raw_sem[n % NRAW], 16 * (n // NRAW + 1), *waits)

        def prep(n, h):
            if (n, h) in ready or n >= len(units):
                return
            k = (n % 2) * 2 + h
            src = raw[:, n % NRAW, h * 1024:h * 1024 + 1024]
            free = used.get((n - 2, h))
            hi = acopy(WH[:, k, :], src, raw_in[n], free)
            lo = tt(V, WL[:, k, :], src, WH[:, k, :].bitcast(F), ALU.subtract, raw_in[n], hi, free)
            ready[(n, h)] = lo
            if h == 1:
                issue(n + NRAW, ready[(n, 0)], lo)

        def prep_ahead(n, h):
            for q in range(2 * n + h, 2 * n + h + 4):
                prep(q // 2, q % 2)

        for n in range(NRAW):
            issue(n)
        un = [0]

        def unit(XH, XL, bank, *waits, start=True, stop=True, per=12, tiles=None):
            n = un[0]
            un[0] += 1
            for h in range(2):
                prep_ahead(n, h)
                k = (n % 2) * 2 + h
                cnt = 0
                for kt in range(8):
                    x = 8 * h + kt
                    wh = WH[:, k, kt * 128:kt * 128 + 128]
                    wl = WL[:, k, kt * 128:kt * 128 + 128]
                    first = start and h == 0 and kt == 0
                    if tiles:
                        PE.wait(tiles[x])
                    last = stop and h == 1 and kt == 7
                    mm(PS[:, bank, 0:256], wh, XH[:, x, :], first, False, ready[(n, h)], *waits)
                    mm(PS[:, bank, 0:256], wh, XL[:, x, :], False, False)
                    t = mm(PS[:, bank, 0:256], wl, XH[:, x, :], False, last, sig=(kt == 7))
                    cnt += 3
                    if kt == 7:
                        used[(n, h)] = t
                    if cnt % per == 0:
                        yield t
            unit_done[0] = t

        unit_done = [None]

        def drain(g):
            for _ in g:
                pass

        def together(a, b, k=1):
            for _ in a:
                for _ in range(k):
                    next(b, None)
            drain(b)

        XT, TMP, MT_ = f(64, 4096), f(80, 4096), f(96, 4096)
        quarter = lambda X, c: X[:, c * 1024:c * 1024 + 1024]
        t_mem = [load(A, quarter(MT_, c), quarter(D["memT"], c)) for c in range(4)]
        t_con = load(A, con[:, :], D["con"])
        t_vec = load(A, vec[:, :], D["vec"])
        t_x = [load(A, quarter(XT, c), quarter(D["xT"], c)) for c in range(4)]

        def k3(ap):
            return ap.rearrange("p (k t) -> p k t", t=256)

        def norm_T(src, t_src, gain, XH, XL, bank, rt, out_, first):
            sq = []
            for c in range(4):
                sq.append(act(quarter(TMP, c), quarter(src, c), ACT.Square, t_src[c], *(out_prev if not first else ())))
                if not first:
                    yield
            if first:
                for q in (PE, V, A, G):
                    q.wait(t_con)
                    q.wait(t_vec)
            for kt in range(16):
                t = mm(PS[:, bank, 0:256], C("ones"), TMP[:, kt * 256:kt * 256 + 256], kt == 0, kt == 15,
                       sq[kt // 4], sig=(kt == 15))
                if kt % 4 == 3:
                    yield
            a = act(rt, PS[:, bank, 0:256], ACT.Sqrt, t, scale=1.0 / 2048, bias=C("eps6"))
            b = recip(rt, rt, a)
            yield
            for c in range(4):
                m = tt(V, k3(quarter(TMP, c)), k3(quarter(src, c)), bc(rt, 4), ALU.mult, b)
                for kt in range(4 * c, 4 * c + 4):
                    hi = act(tile(XH, kt), tile(TMP, kt), ACT.Identity, m, scale=vc(gain, kt))
                    lo = stt(tile(XL, kt), tile(TMP, kt), vc(gain, kt), tile(XH, kt).bitcast(F), ALU.mult,
                             ALU.subtract, hi)
                    out_.append(lo)
                    if kt % 2:
                        yield

        def tile(ap, i, n=1):
            return ap[:, i * 256:(i + n) * 256]

        HH, HL = r(0, 4096), r(16, 4096)
        MH, ML = r(32, 4096), r(48, 4096)
        prep(0, 0)
        t_mr, t_hr_ = [], []
        out_prev = t_mr
        drain(norm_T(MT_, t_mem, "mem_g", MH, ML, 2, f(128, 256), t_mr, True))
        H3, L3, M3, N3 = k3(HH), k3(HL), k3(MH), k3(ML)

        free = {0: None, 1: None}
        MK = f(112, 2048)
        MV = f(120, 2048)
        MV3 = MV.rearrange("p (m c) -> p m c", m=2)
        XQ = f(64, 2048)
        XA = f(132, 2048)
        SQ = f(80, 2048)
        mk, xq = [], []
        sqx = {}

        def mk_units():
            for i in range(8):
                b = i % 2
                yield from unit(M3, N3, b, free[b], tiles=t_mr if i == 0 else None)
                free[b] = acopy(tile(MK, i), PS[:, b, 0:256], unit_done[0])
                mk.append(free[b])

        together(norm_T(XT, t_x, "norm_g", HH, HL, 3, f(129, 256), t_hr_, False), mk_units())
        t_hr = t_hr_[-1]
        vt_free = [None, None]
        b4 = [None, None]

        def mv_units():
            pend = None
            for i in range(9):
                b = i % 2
                if i < 8:
                    yield from unit(M3, N3, b, free[b])
                    tmp = f(130 + b, 256)
                    done = free[b] = acopy(tmp, PS[:, b, 0:256], unit_done[0], vt_free[b])
                if pend is not None:
                    pb, ptmp, pt, pi = pend
                    for m in range(2):
                        t2 = tr(PS[:, 4 + pb, m * 128:m * 128 + 128], ptmp[:, m * 128:m * 128 + 128], pt, b4[pb],
                                sig=(m == 1))
                    vt_free[pb] = t2
                    b4[pb] = vcopy(MV3[:, :, pi * 128:pi * 128 + 128],
                                   PS[:, 4 + pb, 0:256].rearrange("p (m c) -> p m c", m=2), t2, t_hr)
                pend = (b, tmp, done, i)

        def head_norm(X, tx, gain, st, prev, out_):
            s = tt(G, SQ, X, X, ALU.mult, tx, t_hr, prev)
            yield
            for h in range(4):
                for p in range(2):
                    for i in range(2):
                        t = mm(PS[:, 2, 2 * h + p:2 * h + p + 1], tile(SQ, 2 * h + i)[:, p * 128:p * 128 + 128],
                               C("ones")[:, 0:1], i == 0, i == 1, s, t_hr, keep_t[0] if keep_t else None,
                               sig=(i == 1))
            a = act(st, PS[:, 2, 0:8], ACT.Sqrt, t, scale=1.0 / 256, bias=C("eps6"))
            a = recip(st, st, a)
            yield
            for h in range(4):
                for p in range(2):
                    o = 256 * (h % 2) + 128 * p
                    t = mm(PS[:, 6 + h // 2, o:o + 128], st[:, 2 * h + p:2 * h + p + 1].to_broadcast([128, 128]),
                           C("ident"), True, True, a, prev, sig=True)
            yield
            for h in range(4):
                for i in range(2):
                    o = 256 * (h % 2)
                    a = stt(tile(X, 2 * h + i), tile(X, 2 * h + i), vc(gain, i), PS[:, 6 + h // 2, o:o + 256], ALU.mult,
                            ALU.mult, t)
            out_.append(a)

        keep_t = []
        k_n, q_n = [], []
        together(head_norm(MK, mk[-1], "xak", f(94, 8), None, k_n), mv_units(), 4)
        t_mv = b4[1]
        mem_pe = unit_done[0]

        AB = f(100, 256)
        drain(unit(H3, L3, 0, free[0]))
        free[0] = t_ab = acopy(AB, PS[:, 0, 0:256], unit_done[0], t_hr)
        KEEP = keep[:, 0:256]
        CDK = keep[:, 256:352]

        def small_gates():
            for p in range(2):
                t = tr(PS[:, 2, p * 128:p * 128 + 128], AB[:, p * 128:p * 128 + 128], t_ab, t_hr, sig=True)
            yield
            SM = f(101, 48 * 12)
            sm = lambda i, n=1: SM[:, 48 * i:48 * (i + n)]
            v2 = lambda ap: ap.rearrange("p (a h) -> p a h", a=2)
            a_ = vcopy(v2(sm(0)), PS[:, 2, 0:256].rearrange("p (a c) -> p a c", a=2)[:, :, 0:24], t)
            b_ = vcopy(v2(sm(1)), PS[:, 2, 0:256].rearrange("p (a c) -> p a c", a=2)[:, :, 24:48])
            x_ = tt(V, v2(sm(0)), v2(sm(0)), bc(vc("dtb", 0, 24), 2), ALU.add, a_, b_)
            n_ = ts(V, sm(2), sm(0), -1.0, None, ALU.mult, None, x_)
            n_ = tt(V, sm(2), sm(2), sm(0), ALU.min, n_)
            m_ = ts(V, sm(3), sm(0), 0.0, None, ALU.max, None, x_)
            yield
            e1 = act(sm(2), sm(2), ACT.Exp, n_)
            e2 = act(sm(4), sm(1), ACT.Exp, b_, scale=-1.0)
            e3 = act(f(104, 24), vc("alog", 0, 24), ACT.Exp, t_ab)
            e1 = act(sm(2), sm(2), ACT.Ln, e1, bias=1.0)
            s_ = tt(V, sm(3), sm(3), sm(2), ALU.add, m_, e1)
            GG = sm(5)
            g_ = tt(V, v2(GG), v2(sm(3)), bc(f(104, 24), 2), ALU.mult, s_, e3)
            g_ = ts(V, GG, GG, -1.0, None, ALU.mult, None, g_)
            BE = sm(6)
            e2 = ts(V, BE, sm(4), 1.0, None, ALU.add, None, e2)
            be_ = recip(BE, BE, e2)
            yield
            for p in range(2):
                t = mm(PS[:, 2, p * 24:p * 24 + 24], C("tri"), GG[:, p * 24:p * 24 + 24], True, True, g_)
                t = mm(PS[:, 2, 48 + p * 24:72 + p * 24], C("blk"), GG[:, p * 24:p * 24 + 24], True, True)
                for n in range(2):
                    o = 96 + (2 * p + n) * 24
                    t = mm(PS[:, 2, o:o + 24], C("chunk")[:, n:n + 1].to_broadcast([128, 128]), GG[:, p * 24:p * 24 + 24],
                           True, True, sig=True)
            GC = f(105, 192)
            c_ = vcopy(GC, PS[:, 2, 0:192], t)
            yield
            KD = sm(7)
            d_ = tt(V, KD, GC[:, 48:96], GC[:, 0:48], ALU.subtract, c_)
            kd_ = act(KD, KD, ACT.Exp, d_)
            CD = f(106, 96)
            cd_ = act(CD, GC[:, 96:192], ACT.Exp, c_)
            BX = sm(8)
            bx_ = act(BX, GC[:, 0:48], ACT.Exp, c_)
            bx_ = tt(V, BX, BX, BE, ALU.mult, bx_, be_)
            small = [kd_, cd_, bx_]
            k0 = vcopy(KEEP[:, 0:48], GG, *small)
            k0 = vcopy(KEEP[:, 48:96], BE)
            k0 = vcopy(KEEP[:, 96:144], KD)
            k0 = vcopy(KEEP[:, 144:192], BX)
            k0 = vcopy(KEEP[:, 192:240], GC[:, 0:48])
            k0 = vcopy(CDK, CD)
            keep_t.append(k0)

        def xq_units():
            for i in range(8):
                b = (i + 1) % 2
                yield from unit(H3, L3, b, t_hr, free[b])
                free[b] = acopy(tile(XQ, i), PS[:, b, 0:256], unit_done[0], t_hr)
                xq.append(free[b])

        together(small_gates(), xq_units(), 4)

        def cross():
            yield from head_norm(XQ, xq[-1], "xaq", f(95, 8), k_n[0], q_n)
            ready_ = q_n[0]
            bank_free = {2: None, 3: None, 4: b4[0], 5: b4[1], 6: None, 7: None}
            p_free = [None, None]
            pt_free = [None, None]
            xa_t = []
            it = 0
            for h in range(4):
                PT = f(96 + 2 * (h % 2), 512).rearrange("p (m t) -> p m t", m=2)
                for p in range(2):
                    bk = 2 + it % 2
                    P = f(92 + it % 2, 256)
                    st = f(94 + it % 2, 8)
                    for i in range(2):
                        t = mm(PS[:, bk, 0:256], tile(XQ, 2 * h + i)[:, p * 128:p * 128 + 128], tile(MK, 2 * h + i),
                               i == 0, i == 1, ready_, bank_free[bk], sig=(i == 1))
                    mx = V.do(lambda e, st=st, bk=bk: e.tensor_reduce(st[:, 0:1], PS[:, bk, 0:256], AX.X, ALU.max, negate=True),
                              t, p_free[it % 2])
                    m2 = ts(V, st[:, 1:2], st[:, 0:1], 1.0 / 16, None, ALU.mult, None, mx)
                    ex = act(P, PS[:, bk, 0:256], ACT.Exp, m2, scale=1.0 / 16, bias=st[:, 1:2], acc=st[:, 2:3])
                    bank_free[bk] = ex
                    rc = recip(st[:, 3:4], st[:, 2:3], ex)
                    nm = ts(V, P, P, st[:, 3:4], None, ALU.mult, None, rc)
                    yield
                    b2 = 4 + it % 2
                    for m in range(2):
                        t = tr(PS[:, b2, m * 128:m * 128 + 128], P[:, m * 128:m * 128 + 128], nm, bank_free[b2], sig=(m == 1))
                    p_free[it % 2] = t
                    bank_free[b2] = cp = vcopy(PT[:, :, p * 128:p * 128 + 128],
                                               PS[:, b2, 0:256].rearrange("p (m t) -> p m t", m=2), t, pt_free[h % 2])
                    it += 1
                    yield
                for i in range(2):
                    b3 = 6 + i
                    for m in range(2):
                        t = mm(PS[:, b3, 0:256], MV3[:, m, (2 * h + i) * 128:(2 * h + i) * 128 + 128], PT[:, m, :],
                               m == 0, m == 1, cp, t_mv, bank_free[b3], sig=(m == 1))
                    bank_free[b3] = acopy(tile(XA, 2 * h + i), PS[:, b3, 0:256], t, vt_free[0], vt_free[1])
                    xa_t.append(bank_free[b3])
                pt_free[h % 2] = t
                yield
            cross_end.extend([xa_t[-1], t, bank_free[2], bank_free[3], bank_free[4], bank_free[5], bank_free[6], bank_free[7]])

        cross_end = []

        QK, VT = f(32, 6144), f(56, 6144)
        QT, KT = QK[:, 0:3072], QK[:, 3072:6144]
        RN = f(130, 48)
        sq_t = {}

        def sq_tile(i):
            if i < 5:
                return f(107 + i, 256)
            if i < 13:
                return f(72 + i - 5, 256)
            if i < 17:
                return f(60 + i - 13, 256)
            return f(100 + i - 17, 256)

        conv_free = [None] * 2
        cv = [0]

        def conv_tile(dst, widx, bank, done, *waits):
            i = cv[0] % 2
            cv[0] += 1
            tmp = f(128 + i, 256)
            t = ts(V, tmp, PS[:, bank, 0:256], vc("conv", widx * 4 + 3), None, ALU.mult, None, done, conv_free[i], t_hr)
            for s in (1, 2, 3):
                t = stt(tmp[:, s:256], PS[:, bank, 0:256 - s], vc("conv", widx * 4 + 3 - s), tmp[:, s:256],
                        ALU.mult, ALU.add, t)
            conv_free[i] = a = act(dst, tmp, ACT.Silu, t, *waits)
            return t, a

        qk_t = []

        def qk_units():
            for i in range(24):
                hk, isq = i // 2, i % 2
                b = i % 2
                yield from unit(H3, L3, b, free[b])
                dst = tile(QT if isq else KT, hk)
                free[b], a = conv_tile(dst, hk if isq else 12 + hk, b, unit_done[0], mem_pe)
                qk_t.append(a)
                x = sq_tile(i)
                at = hk if isq else 12 + hk
                sq_t[at] = x, tt(G, x, dst, dst, ALU.mult, a, keep_t[0] if i >= 17 else None)

        together(cross(), qk_units(), 3)
        GG, BE, KD, BX, GC = (KEEP[:, 48 * i:48 * i + 48] for i in range(5))
        KEEP_T = keep_t[0]

        def qk_norm():
            for i in range(24):
                x, tx = sq_t[i]
                for p in range(2):
                    t = mm(PS[:, 2, 2 * i + p:2 * i + p + 1], x[:, p * 128:p * 128 + 128], C("ones")[:, 0:1], True, True,
                           tx, cross_end[2], sig=True)
                if i % 6 == 5:
                    yield
            a = act(RN, PS[:, 2, 0:48], ACT.Sqrt, t, cross_end[1], bias=C("eps6"))
            a = recip(RN, RN, a)
            nb[2] = a = ts(V, RN[:, 0:24], RN[:, 0:24], 128.0 ** -0.5, None, ALU.mult, None, a)
            yield
            yield
            for c in range(12):
                bk = 2 + (c + 1) % 6
                for i in range(4):
                    o = 4 * c + i
                    t = mm(PS[:, bk, i * 128:i * 128 + 128], RN[:, o:o + 1].to_broadcast([128, 128]), C("ident"), True, True,
                           a, nb[bk], *cross_end, sig=(i == 3))
                q = QK[:, c * 512:c * 512 + 512]
                nb[bk] = b = tt(V, q, q, PS[:, bk, :], ALU.mult, t, qk_t[-1])
                yield
            qk_n.append(b)

        nb = {i: None for i in range(2, 8)}
        qk_n = []
        v_t = []

        ztok = {}
        gdone = []

        def ztile(i):
            if i < 8:
                return tile(f(80, 2048), i)
            return tile(KT if i % 2 else QT, (i - 8) // 2)

        def vz_units():
            for n, (kind, i) in enumerate(fill):
                while kind == "z" and i >= 8 and len(gdone) <= (i - 8) // 2:
                    yield
                while kind == "v" and i >= 4 and not qk_n:
                    yield
                b = n % 2
                yield from unit(H3, L3, b, free[b], per=6)
                if kind == "v":
                    free[b], a = conv_tile(tile(VT, i), 24 + i, b, unit_done[0], *cross_end)
                    v_t.append(a)
                else:
                    w = gdone[(i - 8) // 2] if i >= 8 else cross_end[1]
                    ztok[i] = free[b] = act(ztile(i), PS[:, b, 0:256], ACT.Silu, unit_done[0], w, cross_end[0])

        fz = vz_units()
        for _ in qk_norm():
            for _ in range(3):
                next(fz)
        while len(v_t) < 2:
            next(fz)

        bankfree = {i: nb[i] for i in range(2, 8)}
        slot_t = [qk_n[0], qk_n[0]]
        y_t = {}

        def group(g):
            s = g % 2
            bA, bB, bC = 2 + 3 * s, 3 + 3 * s, 4 + 3 * s
            base = 88 + 20 * s
            w = lambda kb, n=512: f(base + kb, n)
            kb, bv, kdc, dT, qd, Lb, LT, T, U, BT = (w(2 * i) for i in range(10))
            u, S = T[:, 0:256], T[:, 256:512]
            start = [slot_t[s], qk_n[0], v_t[2 * g + 1], KEEP_T]
            kT, qT = tile(KT, g), tile(QT, g)
            vT = [tile(VT, 2 * g), tile(VT, 2 * g + 1)]
            col = lambda M, i: M[:, (i % 2) * 24 + 2 * g + i // 2:(i % 2) * 24 + 2 * g + i // 2 + 1]
            blk = lambda X, i: X[:, i * 128:i * 128 + 128]
            c4 = lambda X: X.rearrange("p (i c) -> p i c", i=4)
            for p in range(2):
                kp, qp = kT[:, p * 128:p * 128 + 128], qT[:, p * 128:p * 128 + 128]
                mm(PS[:, bA, p * 128:p * 128 + 128], kp, kp, True, True, *start, bankfree[bA])
                tA = mm(PS[:, bA, 256 + p * 128:384 + p * 128], kp, qp, True, True, sig=(p == 1))
            for i in range(4):
                tB = mm(PS[:, bB, i * 128:i * 128 + 128], col(GG, i).to_broadcast([128, 128]), C("tri"), True, True,
                        bankfree[bB], sig=(i == 3))
            for p in range(2):
                tr(PS[:, bC, p * 128:p * 128 + 128], kT[:, p * 128:p * 128 + 128], bankfree[bC])
            for p in range(2):
                tC = tr(PS[:, bC, 256 + p * 128:384 + p * 128], vT[0][:, p * 128:p * 128 + 128], sig=(p == 1))
            yield
            for i in range(4):
                d1 = stt(blk(dT, i), PS[:, bB, i * 128:i * 128 + 128], col(GC, i), C("mt"), ALU.subtract, ALU.add, tB,
                         *start)
            for i in range(4):
                d2 = stt(blk(Lb, i), PS[:, bB, i * 128:i * 128 + 128], col(GC, i), C("ms"), ALU.subtract, ALU.add)
            eB = act(qd, PS[:, bB, :], ACT.Exp, d2)
            eL = act(Lb, Lb, ACT.Exp, d2, scale=-1.0)
            eT = act(dT, dT, ACT.Exp, d1)
            for i in range(4):
                kpi = PS[:, bC, (i % 2) * 128:(i % 2) * 128 + 128]
                k1 = act(blk(kb, i), kpi, ACT.Copy, tC, *start, scale=col(BX, i))
                k2 = act(blk(kdc, i), kpi, ACT.Copy, scale=col(KD, i))
            for p in range(2):
                v1 = act(blk(bv, p), PS[:, bC, 256 + p * 128:384 + p * 128], ACT.Copy, scale=col(BE, p))
            yield
            for p in range(2):
                tB = tr(PS[:, bB, p * 128:p * 128 + 128], vT[1][:, p * 128:p * 128 + 128], eB, sig=(p == 1))
            yield
            for i in range(4):
                lk = stt(blk(Lb, i), blk(Lb, i), col(BE, i), PS[:, bA, (i % 2) * 128:(i % 2) * 128 + 128], ALU.mult,
                         ALU.mult, eL, tA)
            h2 = lambda X: X.rearrange("p (h c) -> p h c", h=2)
            qk = tt(V, h2(dT), h2(dT), bc(PS[:, bA, 256:512], 2), ALU.mult, eT)
            qd_ = tt(G, h2(qd), h2(qd), bc(qT, 2), ALU.mult, eB)
            for p in range(2):
                v1 = act(blk(bv, 2 + p), PS[:, bB, p * 128:p * 128 + 128], ACT.Copy, tB, scale=col(BE, 2 + p))
            yield
            for i in range(4):
                t = tr(PS[:, bA, i * 128:i * 128 + 128], blk(Lb, i), lk, qk, sig=(i == 3))
            cl = acopy(LT, PS[:, bA, :], t, *start)
            T1 = tt(V, c4(T), c4(Lb), bc(C("nm1"), 4), ALU.mult, lk)
            T1 = tt(V, c4(T), c4(T), bc(C("ident"), 4), ALU.add, T1)
            yield
            bt = tt(G, c4(BT), c4(LT), bc(C("mt2"), 4), ALU.mult, cl, *start)
            U1 = tt(G, c4(U), c4(LT), bc(C("nmt1"), 4), ALU.mult, cl)
            U1 = tt(G, c4(U), c4(U), bc(C("ident"), 4), ALU.add, U1)
            yield
            yield
            freeB, freeA, freeC = v1, cl, v1
            for s_ in LEVELS:
                for i in range(4):
                    t = mm(PS[:, bB, i * 128:i * 128 + 128], blk(BT, i), blk(T, i), True, True, bt, T1, freeB, sig=(i == 3))
                freeB = x = acopy(Lb, PS[:, bB, :], t, lk, T1)
                if s_ != 32:
                    bt = tt(G, c4(BT), c4(LT), bc(C(f"mt{2 * s_}"), 4), ALU.mult, t)
                yield
                if s_ != 32:
                    for i in range(4):
                        tA = mm(PS[:, bA, i * 128:i * 128 + 128], blk(U, i), blk(Lb, i), True, True, x, U1, freeA,
                                sig=(i == 3))
                for i in range(4):
                    tC = mm(PS[:, bC, i * 128:i * 128 + 128], blk(Lb, i), blk(U, i), True, True, x, U1, freeC,
                            sig=(i == 3))
                if s_ != 32:
                    freeA = T1 = tt(V, T, T, PS[:, bA, :], ALU.subtract, tA)
                freeC = U1 = tt(V, U, U, PS[:, bC, :], ALU.subtract, tC)
                yield
            for i in range(4):
                t = mm(PS[:, bB, i * 128:i * 128 + 128], blk(kb, i), blk(U, i), True, True, k1, U1, freeB, sig=(i == 3))
            freeB = nw = A.do(lambda e: e.mul(LT, PS[:, bB, :], -1.0), t, bt)
            yield
            St = None
            ut = None
            for n in range(4):
                p, b = n // 2, 64 * (n % 2)
                for h in range(2):
                    i = 2 * h + p
                    o = PS[b:b + 64, bA, h * 128:h * 128 + 128]
                    t = mm(o, blk(U, i)[:, b:b + 64], blk(bv, i), True, n == 0, v1, freeA, sig=(h == 1 and n == 0))
                    if n:
                        t = mm(o, blk(LT, i)[:, b:b + 64], blk(S, h), False, True, nw, St, sig=(h == 1))
                freeA = ut = acopy(u[b:b + 64, :], PS[b:b + 64, bA, 0:256], t, *start)
                yield
                for h in range(2):
                    i = 2 * h + p
                    o = PS[:, bC, h * 256 + n * 64:h * 256 + n * 64 + 64]
                    if n:
                        mm(o, blk(S, h), blk(qd, i)[:, b:b + 64], True, False, qd_, St)
                    tC = mm(o, u[b:b + 64, h * 128:h * 128 + 128], dT[b:b + 64, i * 128 + b:i * 128 + b + 64], n == 0,
                            True, ut, freeC, qk, sig=(h == 1))
                if n < 3:
                    for h in range(2):
                        i = 2 * h + p
                        t = mm(PS[:, bB, h * 128:h * 128 + 128], kdc[b:b + 64, i * 128:i * 128 + 128],
                               u[b:b + 64, h * 128:h * 128 + 128], True, True, k2, freeB, sig=(h == 1))
                    for h in range(2):
                        if n == 0:
                            St = vcopy(blk(S, h), PS[:, bB, h * 128:h * 128 + 128], t, *start)
                        else:
                            cc = CDK[:, n * 24 + 2 * g + h:n * 24 + 2 * g + h + 1]
                            St = stt(blk(S, h), blk(S, h), cc, PS[:, bB, h * 128:h * 128 + 128], ALU.mult, ALU.add, t, St)
                    freeB = St
                yield
            y = tile(VT, 2 * g, 2)
            yt = acopy(y, PS[:, bC, :], tC)
            gdone.append(yt)
            sq = tt(G, kb, y, y, ALU.mult, yt)
            yield
            for i in range(4):
                t = mm(PS[:, bA, i:i + 1], blk(kb, i), C("ones")[:, 0:1], True, True, sq, freeA, sig=(i == 3))
            rr = S[:, 0:4]
            freeA = a = act(rr, PS[:, bA, 0:4], ACT.Sqrt, t, scale=1.0 / 128, bias=C("eps6"))
            a = recip(rr, rr, a)
            yield
            for i in range(4):
                t = mm(PS[:, bB, i * 128:i * 128 + 128], rr[:, i:i + 1].to_broadcast([128, 128]), C("ident"), True, True, a,
                       freeB, sig=(i == 3))
            yield
            yt = stt(y, y, vc("outg"), PS[:, bB, :], ALU.mult, ALU.mult, t)
            y_t[g] = yt
            bankfree[bA], bankfree[bB], bankfree[bC] = freeA, yt, sq
            slot_t[s] = yt

        def gate_tile(i):
            z = ztile(i)
            y = tile(VT, i) if i < 24 else tile(XA, i - 24)
            p_t[i] = tt(G, z, z, y, ALU.mult, ztok[i], y_t[i // 2] if i < 24 else cross_end[0])

        def gates():
            for i in range(32):
                if i not in p_t and i in ztok and (i >= 24 or i // 2 in y_t):
                    gate_tile(i)

        p_t = {}
        live = []
        nextg = 0
        credit = 0.0
        while nextg < 12 or live:
            if nextg < 12 and len(live) < 2 and len(v_t) >= 2 * nextg + 2:
                live.append(group(nextg))
                nextg += 1
                if nextg == 1:
                    for _ in range(8):
                        next(live[0], None)
                        next(fz, None)
            if not live:
                next(fz)
            for x in list(live):
                try:
                    next(x)
                except StopIteration:
                    live.remove(x)
                credit += FILL
                while credit >= 1:
                    next(fz, None)
                    credit -= 1
            gates()
        drain(fz)
        gates()
        if stage == 2:
            load(G, dbg[:, 0:6144], VT, y_t[11], y_t[10], store=True)
            return finish()

        YH, YL = r(0, 8192), r(88, 8192)
        zpe = unit_done[0]
        gate_t = []
        for c in range(8):
            src = f(80, 2048)[:, c * 1024:c * 1024 + 1024] if c < 2 else QK[:, (c - 2) * 1024:(c - 2) * 1024 + 1024]
            last = [p_t[i] for i in range(32)]
            hi = acopy(YH[:, c * 1024:c * 1024 + 1024], src, *last, zpe)
            gate_t.append(tt(V, YL[:, c * 1024:c * 1024 + 1024], src, YH[:, c * 1024:c * 1024 + 1024].bitcast(F),
                             ALU.subtract, hi, zpe, slot_t[0], slot_t[1]))
        X1 = f(32, 4096)
        X1H, X1L = r(48, 4096), r(64, 4096)
        t_x = load(G, X1, D["xT"], gate_t[-1])
        Y3, W3 = k3(YH), k3(YL)
        x1_t = []
        for m in range(16):
            b = m % 2
            drain(unit(Y3, W3, b, gate_t[3], free[b], stop=False))
            drain(unit(Y3[:, 16:32, :], W3[:, 16:32, :], b, gate_t[7], start=False))
            free[b] = a = tt(V, tile(X1, m), PS[:, b, 0:256], tile(X1, m), ALU.add, unit_done[0], t_x)
            hi = acopy(tile(X1H, m), tile(X1, m), a)
            x1_t.append(tt(V, tile(X1L, m), tile(X1, m), tile(X1H, m).bitcast(F), ALU.subtract, hi, a))
        if stage == 3:
            load(G, dbg[:, 0:4096], X1, x1_t[-1], store=True)
            return finish()
        wo_pe = unit_done[0]

        P3, Q3 = k3(X1H), k3(X1L)
        QI, KI, KK, QQ = f(0, 2048), f(8, 256), f(9, 2048), f(17, 2048)
        WI = f(25, 32).rearrange("p (a h) -> p a h", a=2)
        SC, WK, MM = f(26, 512), f(28, 512), f(30, 512)
        VN = f(80, 2048).rearrange("p (m c) -> p m c", m=2)
        HK = f(88, 2048).rearrange("p (h x) -> p h x", h=8)
        PT_ = f(96, 2048)
        XH2, XL2 = r(104, 4096), r(120, 4096)
        HOT, RB, BV = f(96, 384)[0:32, :], f(98, 8)[0:32, :], f(99, 384)[0:8, :]
        t1 = load(G, HOT, D["hot"], gate_t[-1], wo_pe)
        t2 = load(G, RB, D["rb"])
        t = mm(PS[0:8, 2, 0:384], RB, HOT, True, True, t1, t2, bankfree[2], sig=True)
        t = vcopy(BV, PS[0:8, 2, 0:384], t)
        sv = load(G, scratch["bias"], BV, t, store=True)
        hsrc = scratch["bias"]
        hank = bass.AP(hsrc.tensor, hsrc.offset, [[1, 128], [384, 8], [1, 256]])
        t_hk = load(G, HK, hank, sv, wo_pe)

        T1 = f(136, 256)
        drain(unit(P3, Q3, 0, x1_t[-1], free[0]))
        free[0] = a = vcopy(T1, PS[:, 0, 0:256], unit_done[0], wo_pe)
        t_ki = vcopy(KI[0:64, :], T1[0:64, :], a)
        t_ki2 = load(G, KI[64:128, :], T1[0:64, :], a)
        for p in range(2):
            t = tr(PS[:, 2, p * 128:p * 128 + 128], T1[:, p * 128:p * 128 + 128], a, t, sig=True)
        t_wi = ts(V, WI, PS[:, 2, 0:256].rearrange("p (a c) -> p a c", a=2)[:, :, 64:80], 1.0 / 32, None, ALU.mult,
                  None, t)
        bk = {i: t_wi for i in range(2, 8)}
        rel_free = [None] * 4
        it = 0
        sc_t = t_wi
        for i in range(8):
            b = i % 2
            drain(unit(P3, Q3, b, free[b]))
            free[b] = q_ = acopy(tile(QI, i), PS[:, b, 0:256], unit_done[0])
            for hh in (2 * i, 2 * i + 1):
                o = 64 * (hh % 2)
                for p in range(2):
                    S_ = 128 * (p + 1)
                    kb_ = 2 + it % 6
                    t = mm(PS[:, kb_, 0:S_], tile(QI, i)[o:o + 64, p * 128:p * 128 + 128], KI[o:o + 64, 0:S_], True, True,
                           q_, t_ki, t_ki2, bk[kb_], sig=True)
                    rl = f(136 + it % 4, S_)
                    bk[kb_] = a = act(rl, PS[:, kb_, 0:S_], ACT.Relu, t, rel_free[it % 4], t_wi)
                    sc = SC[:, p * 256:p * 256 + S_]
                    if hh == 0:
                        sc_t = ts(V, sc, rl, WI[:, p, hh:hh + 1], None, ALU.mult, None, a, wo_pe)
                    else:
                        sc_t = stt(sc, rl, WI[:, p, hh:hh + 1], sc, ALU.mult, ALU.add, a, sc_t)
                    rel_free[it % 4] = sc_t
                    it += 1
        mx8 = f(25.5, 8)

        def topk():
            for p in range(2):
                S_ = 128 * (p + 1)
                sc, wk, m = (X[:, p * 256:p * 256 + S_] for X in (SC, WK, MM))
                d = slice(S_ - 128, S_)
                t = tt(V, sc[:, d], sc[:, d], C("causal"), ALU.add, sc_t)
                src = sc
                for k in range(8):
                    t = V.do(lambda e, src=src: e.max(out=mx8, in_=src), t)
                    t = V.do(lambda e, src=src, wk=wk: e.match_replace(out=wk, in_to_replace=mx8, in_values=src,
                                                                       imm_value=-3e38), t)
                    src = wk
                    yield
                t = ts(V, m, wk, -2e38, -BIG, ALU.is_gt, ALU.mult, t)
                t = tt(V, m[:, d], m[:, d], C("causal"), ALU.add, t)
                m_t.append(t)
                yield

        m_t = []
        tk = topk()
        kq_t = []
        for i in range(16):
            b = i % 2
            drain(unit(P3, Q3, b, free[b]))
            if i < 8:
                free[b] = acopy(tile(KK, i), PS[:, b, 0:256], unit_done[0])
            else:
                free[b] = A.do(lambda e, i=i, b=b: e.mul(tile(QQ, i - 8), PS[:, b, 0:256], 128.0 ** -0.5), unit_done[0])
            kq_t.append(free[b])
            next(tk, None)
            next(tk, None)
        drain(tk)
        vt = [None, None]
        for i in range(8):
            b = i % 2
            drain(unit(P3, Q3, b, free[b]))
            tmp = f(136 + b, 256)
            free[b] = t = acopy(tmp, PS[:, b, 0:256], unit_done[0], vt[b], sc_t)
            for m in range(2):
                t = tr(PS[:, 2 + b, m * 128:m * 128 + 128], tmp[:, m * 128:m * 128 + 128], t, bk[2 + b], sig=(m == 1))
            vt[b] = t
            bk[2 + b] = vcopy(VN[:, :, i * 128:i * 128 + 128], PS[:, 2 + b, 0:256].rearrange("p (m c) -> p m c", m=2), t,
                              wo_pe)
        t_vn = bk[3]
        INV = f(136, 1024)
        t_inv = load(G, INV, D["inv"], vt[0], vt[1])
        x2_t = {}
        att = [None]

        def attention():
            it = 0
            pf = [None] * 2
            ptf = [None] * 2
            for h in range(8):
                PT = f(4 + 2 * (h % 2), 384)
                for p in range(2):
                    S_ = 128 * (p + 1)
                    kb_ = 2 + it % 2
                    P = f(it % 2, S_)
                    st = f(2 + it % 2, 8)
                    mm(PS[:, kb_, 0:S_], tile(QQ, h)[:, p * 128:p * 128 + 128], tile(KK, h)[:, 0:S_], True, False,
                       kq_t[-1], bk[kb_])
                    t = mm(PS[:, kb_, 0:S_], C("flip"), HK[:, h, 256 - S_:256], False, True, t_hk, sig=True)
                    bk[kb_] = a = tt(V, P, PS[:, kb_, 0:S_], MM[:, p * 256:p * 256 + S_], ALU.add, t, m_t[-1],
                                     pf[it % 2], sc_t)
                    a = V.do(lambda e, st=st, P=P: e.tensor_reduce(st[:, 0:1], P, AX.X, ALU.max, negate=True), a)
                    a = act(P, P, ACT.Exp, a, bias=st[:, 0:1], acc=st[:, 2:3])
                    a = recip(st[:, 3:4], st[:, 2:3], a)
                    a = ts(V, P, P, st[:, 3:4], None, ALU.mult, None, a)
                    yield
                    b2 = 4 + it % 2
                    for m in range(p + 1):
                        t = tr(PS[:, b2, m * 128:m * 128 + 128], P[:, m * 128:m * 128 + 128], a, bk[b2], sig=(m == p))
                    pf[it % 2] = t
                    bk[b2] = cp = vcopy(PT[:, p * 128:p * 128 + S_], PS[:, b2, 0:S_], t, ptf[h % 2])
                    it += 1
                    yield
                b3 = 6 + h % 2
                mm(PS[:, b3, 0:128], VN[:, 0, h * 128:h * 128 + 128], PT[:, 0:128], True, True, cp, t_vn, bk[b3])
                mm(PS[:, b3, 128:256], VN[:, 0, h * 128:h * 128 + 128], PT[:, 128:256], True, False)
                t = mm(PS[:, b3, 128:256], VN[:, 1, h * 128:h * 128 + 128], PT[:, 256:384], False, True, sig=True)
                ptf[h % 2] = t
                hi = acopy(tile(XH2, 8 + h), PS[:, b3, 0:256], t, wo_pe, sc_t)
                bk[b3] = lo = tt(V, tile(XL2, 8 + h), PS[:, b3, 0:256], tile(XH2, 8 + h).bitcast(F), ALU.subtract, hi)
                x2_t[8 + h] = lo
                att[0] = t
                yield

        ping = [f(26, 256), f(28, 256)]

        def pool_units():
            prev = m_t[-1]
            for c in range(8):
                b = c % 2
                yield from unit(P3, Q3, b, free[b])
                x = tile(PT_, c)
                free[b] = a = acopy(x, PS[:, b, 0:256], unit_done[0], t_hk)
                cur = x
                for k in range(c // 2 + 1):
                    st = 1 << k
                    nx = ping[k % 2]
                    a = tt(G, nx[:, st:256], cur[:, st:256], cur[:, 0:256 - st], ALU.add, a, prev)
                    a = G.do(lambda e, nx=nx, cur=cur, st=st: e.tensor_copy(nx[:, 0:st], cur[:, 0:st]), a)
                    cur = nx
                a = tt(G, cur, cur, INV[:, (c // 2) * 256:(c // 2) * 256 + 256], ALU.mult, a, t_inv)
                prev = tt(G, x, cur, x, ALU.subtract, a)
                pool_t.append(prev)

        pool_t = []
        together(attention(), pool_units())
        PW = f(88, 2048).rearrange("p (g d) -> p g d", g=8)
        t_pw = load(G, PW, D["pw"], att[0])
        for g in range(4):
            for d in range(2):
                kb_ = 2 + (2 * g + d) % 6
                for c in range(2):
                    t = mm(PS[:, kb_, 0:256], PW[:, 2 * g + c, d * 128:d * 128 + 128], tile(PT_, 2 * g + c), c == 0, c == 1,
                           t_pw, pool_t[-1], bk[kb_], sig=(c == 1))
                i = 2 * g + d
                hi = act(tile(XH2, i), PS[:, kb_, 0:256], ACT.Identity, t, scale=vc("pools", i))
                bk[kb_] = x2_t[i] = stt(tile(XL2, i), PS[:, kb_, 0:256], vc("pools", i), tile(XH2, i).bitcast(F), ALU.mult,
                                        ALU.subtract, hi)
        if stage == 4:
            load(G, dbg[:, 0:4096].bitcast(R), XH2, x2_t[7], x2_t[15], store=True)
            load(G, dbg[:, 4096:8192].bitcast(R), XL2, x2_t[7], x2_t[15], store=True)
            return finish()
        Z3, R3 = k3(XH2), k3(XL2)
        r1_t = []
        for m in range(16):
            b = m % 2
            drain(unit(Z3, R3, b, x2_t[7], x2_t[15], free[b]))
            free[b] = stt(tile(X1, m), tile(X1, m), ALPHA, PS[:, b, 0:256], ALU.mult, ALU.add, unit_done[0])
            r1_t.append(free[b])
        mix_pe = unit_done[0]

        MU, RS, SQ = f(80, 256), f(81, 256), f(104, 4096)
        for kt in range(16):
            t = mm(PS[:, 2, 0:256], C("ones"), tile(X1, kt), kt == 0, kt == 15, r1_t[kt], bk[2], sig=(kt == 15))
        a = ts(V, MU, PS[:, 2, 0:256], 1.0 / 2048, None, ALU.mult, None, t)
        sq = []
        for c in range(4):
            x = k3(X1)[:, 4 * c:4 * c + 4, :]
            a2 = tt(V, x, x, bc(MU, 4), ALU.subtract, a)
            sq.append(act(k3(SQ)[:, 4 * c:4 * c + 4, :], x, ACT.Square, a2, mix_pe))
        for kt in range(16):
            t = mm(PS[:, 3, 0:256], C("ones"), tile(SQ, kt), kt == 0, kt == 15, sq[kt // 4], bk[3], sig=(kt == 15))
        s_ = act(RS, PS[:, 3, 0:256], ACT.Sqrt, t, att[0], scale=1.0 / 2048, bias=C("eps5"))
        s_ = recip(RS, RS, s_)
        H2H, H2L = r(0, 4096), r(16, 4096)
        hh_t = []
        for c in range(4):
            x = k3(X1)[:, 4 * c:4 * c + 4, :]
            a = tt(V, x, x, bc(RS, 4), ALU.mult, s_, *sq)
            for kt in range(4 * c, 4 * c + 4):
                x1 = tile(X1, kt)
                b_ = ts(V, x1, x1, vc("ln1g", kt), vc("ln1b", kt), ALU.mult, ALU.add, a)
                hi = acopy(tile(H2H, kt), x1, b_)
                hh_t.append(tt(V, tile(H2L, kt), x1, tile(H2H, kt).bitcast(F), ALU.subtract, hi))
        E3, O3 = k3(H2H), k3(H2L)
        stg = f(104, 4096).rearrange("p (a d) -> p a d", a=2)
        bb = {i: (bk[i] if i > 3 else s_) for i in range(2, 8)}
        it = 0
        for p in range(2):
            for c in range(4):
                kb_ = 2 + it % 6
                it += 1
                for k in range(4):
                    t = tr(PS[:, kb_, k * 128:k * 128 + 128], tile(X1, 4 * c + k)[:, p * 128:p * 128 + 128], hh_t[-1], bb[kb_],
                           s_, sig=(k == 3))
                bb[kb_] = acopy(stg[:, p, c * 512:c * 512 + 512], PS[:, kb_, :], t)
        h_tr = t
        t_sc = load(G, scratch["h"], stg, bb[kb_], store=True)
        if stage == 5:
            load(G, dbg[:, 0:4096], X1, hh_t[-1], store=True)
            return finish()

        SUB = f(92, 256).rearrange("p (s k) -> p s k", s=2)
        t_sub = load(G, SUB, D["sub"], mix_pe, x2_t[7])
        QH = f(76, 4096)
        ST = f(60, 4096).rearrange("p (a s h k) -> p a s h k", a=2, s=2, h=8)
        CAND, WRK = f(32, 2048), f(40, 2048)
        VAL, IDX, IDF = f(48, 512), f(50, 512).bitcast(U32), f(52, 512)
        val = VAL.rearrange("p (q k) -> p q k", k=16)
        idx = IDX.rearrange("p (q k) -> p q k", k=16)
        idf = IDF.rearrange("p (q k) -> p q k", k=16)
        BST, POS = f(54, 128), f(54.5, 128).bitcast(U32)
        POA, POB = f(55, 128), f(55.5, 128)
        PUA = f(56, 128).bitcast(U32)
        SEL = f(56.5, 128)
        I1T, I2T, GTT = f(57, 256), f(58, 256), f(59, 256)
        sel_done = []

        def top16(vals, v16, i16, wk, *t):
            a = V.do(lambda e: e.max(out=v16[:, 0:8], in_=vals), *t)
            V.do(lambda e: e.max_index(out=i16[:, 0:8], in_max=v16[:, 0:8], in_values=vals), a)
            c = V.do(lambda e: e.match_replace(out=wk, in_to_replace=v16[:, 0:8], in_values=vals, imm_value=-3e38), a)
            d = V.do(lambda e: e.max(out=v16[:, 8:16], in_=wk), c)
            return V.do(lambda e: e.max_index(out=i16[:, 8:16], in_max=v16[:, 8:16], in_values=wk), d)

        def keys16(hs, t):
            for p in range(2):
                o = (2 * hs + p) % 16 * 128
                yield
                top_t[p] = top16(ST[:, p, hs % 2, hs // 2, :], val[:, 16 * p + hs, :], idx[:, 16 * p + hs, :],
                                 WRK[:, o:o + 128], t, h_tr, mix_pe)

        top_t = {}

        def select(last):
            yield from last
            yield from keys16(15, s_t[15][0])
            v4 = val.rearrange("p (a q) k -> p a q k", a=2)
            i4 = idf.rearrange("p (a q) k -> p a q k", a=2)
            cand = CAND.rearrange("p (h a b) -> p h a b", h=8, a=16)
            bst = BST.rearrange("p (h k) -> p h k", k=16)
            pos = POS.rearrange("p (h k) -> p h k", k=16)
            hot = CAND.rearrange("p (k a) -> p k a", a=16)
            sel3 = SEL.rearrange("p (h k) -> p h k", k=16)
            prev = vcopy(IDF, IDX, top_t[0], top_t[1])
            for p in range(2):
                for h in range(8):
                    c = tt(V, cand[:, h, :, :], bc(v4[:, p, 2 * h, :], 16, 2), bc(v4[:, p, 2 * h + 1, :], 16), ALU.add,
                           prev)
                    if h % 4 == 3:
                        yield
                for h in range(8):
                    t = top16(CAND[:, h * 256:h * 256 + 256], bst[:, h, :], pos[:, h, :],
                              WRK[:, h * 256:h * 256 + 256], c)
                    yield
                a = ts(V, PUA, POS, 4, None, ALU.logical_shift_right, None, t)
                a = vcopy(POA, PUA, a)
                b = ts(V, PUA, POS, 15, None, ALU.bitwise_and, None, a)
                b = vcopy(POB, PUA, b)
                out_ = t
                for which, P_ in ((0, POA), (1, POB)):
                    c = tt(V, hot, bc(P_, 16, 2), bc(C("iota16"), 128), ALU.is_equal, a, b, out_)
                    yield
                    for h in range(8):
                        c2 = tt(V, hot[:, 16 * h:16 * h + 16, :], hot[:, 16 * h:16 * h + 16, :],
                                bc(i4[:, p, 2 * h + which, :], 16), ALU.mult, c)
                        if h == 3:
                            yield
                    yield
                    c = V.do(lambda e: e.tensor_reduce(SEL, hot, AX.X, ALU.add), c2, out_)
                    t3 = tr(PS[:, 2, which * 128:which * 128 + 128], SEL, c, bb[2], sig=True)
                    yield
                    out_ = bb[2] = vcopy((I1T, I2T)[which][:, p * 128:p * 128 + 128],
                                         PS[:, 2, which * 128:which * 128 + 128], t3)
                a = tt(V, sel3, bst, bst[:, :, 0:1].broadcast_to([128, 8, 16]), ALU.subtract, out_)
                a = act(SEL, SEL, ACT.Exp, a)
                yield
                sm_ = POA[:, 0:8]
                b = V.do(lambda e: e.tensor_reduce(sm_, sel3, AX.X, ALU.add), a)
                b = recip(sm_, sm_, b)
                b = tt(V, sel3, sel3, bc(sm_, 16, 2), ALU.mult, b)
                t3 = tr(PS[:, 2, 256:384], SEL, b, bb[2], sig=True)
                yield
                bb[2] = prev = vcopy(GTT[:, p * 128:p * 128 + 128], PS[:, 2, 256:384], t3)
            sel_done.append(prev)

        s_t = []
        pend = iter(())
        for i in range(16):
            b = i % 2
            for _ in unit(E3, O3, b, hh_t[-1], free[b], per=24):
                next(pend, None)
            drain(pend)
            free[b] = a = acopy(f(76 + (i % 4), 256), PS[:, b, 0:256], unit_done[0], s_t[i - 4][1] if i >= 4 else mix_pe,
                                hh_t[-1])
            kb_ = 2 + i % 2
            for p in range(2):
                t = mm(PS[:, kb_, p * 128:p * 128 + 128], f(76 + (i % 4), 256)[:, p * 128:p * 128 + 128], SUB[:, i % 2, :],
                       True, True, a, t_sub, bb[kb_], sig=(p == 1))
            bb[kb_] = a = acopy(ST[:, :, i % 2, i // 2, :], PS[:, kb_, 0:256].rearrange("p (a k) -> p a k", a=2), t, mix_pe)
            s_t.append((a, t))
            if i >= 1:
                pend = keys16(i - 1, s_t[i - 1][0])

        qh_pe = s_t[-1][1]
        if stage == 6:
            load(G, dbg[:, 0:4096], f(60, 4096), s_t[-1][0], store=True)
            return finish()

        CC = f(76, 16384)
        C3 = CC.rearrange("p (j t) -> p j t", t=256)
        ACC = f(60, 4096)
        O1 = f(32, 2048).rearrange("p (b k i) -> p b k i", b=4, k=4)
        O2 = f(40, 1024).rearrange("p (b k i) -> p b k i", b=4, k=4)
        CTH, CTL = r(44, 512), r(46, 512)
        GT = f(48, 512)
        sel = select(pend)
        pe_free = {"o": [None] * 4, "ct": [None, None], "gt": [None, None]}
        c_free = [t_sc, qh_pe]
        hot_t, mm_t = {}, {}
        quad_last = [None]
        gelu_last = [None]

        def gate_hots(q, half):
            ob = q % 4
            for k in range(4):
                t = 4 * q + k
                ts(V, O1[:, ob, k, :], C("iota"), I1T[:, t:t + 1], GTT[:, t:t + 1], ALU.is_equal, ALU.mult,
                   sel_done[0], pe_free["o"][ob])
            hot_t[q] = tt(V, O2[:, ob, :, :], bc(C("iota")[:, 64 * half:64 * half + 64], 4), bc(I2T[:, 4 * q:4 * q + 4], 64, 2),
                          ALU.is_equal)

        def gate_mm(q):
            ob, bank = q % 4, 3 + q % 4
            for k in range(4):
                m = mm(PS[:, bank, k * 64:k * 64 + 64], O1[:, ob, k, :], O2[:, ob, k, :], True, True, hot_t[q], bb[bank],
                       sig=(k == 3))
            pe_free["o"][ob] = mm_t[q] = m

        def gate_apply(q, jdone):
            bank = 3 + q % 4
            g = PS[:, bank, 0:256].rearrange("p (t j) -> p j t", t=4)
            tcol = slice(4 * q, 4 * q + 4)
            x = mm_t[q]
            if jdone:
                x = tt(V, C3[:, 0:jdone, tcol], C3[:, 0:jdone, tcol], g[:, 0:jdone, :], ALU.mult, x, gelu_last[0])
            if jdone < 64:
                x = vcopy(C3[:, jdone:64, tcol], g[:, jdone:64, :], x, *c_free)
            bb[bank] = quad_last[0] = x

        v_evac = {}
        seln = 0.0
        for half in range(2):
            hots = mms = applied = 0
            quad_last[0] = None
            gm = None
            for j in range(64):
                b = j % 2
                due = 64 if j >= 60 else (j + 2 if half else int(64 * max(0, j - 25) / 35))
                due = min(due, hots + 2, 64) if sel_done else 0
                work = [lambda q=q: gate_apply(q, j) for q in range(applied, mms)]
                work += [lambda q=q: gate_mm(q) for q in range(mms, hots)]
                work += [lambda q=q: gate_hots(q, half) for q in range(hots, due)]
                applied, mms, hots = mms, hots, max(due, hots)
                for x in unit(E3, O3, b, free[b], per=6):
                    seln += SEL_RATE
                    if half == 0 and not sel_done and seln >= 1:
                        seln -= 1
                        next(sel, None)
                    if work:
                        work.pop(0)()
                for x in work:
                    x()
                tq = 4 * applied
                gtmp = GT[:, b * 256:b * 256 + 256]
                if tq:
                    ga = free[b] = act(gtmp[:, 0:tq], PS[:, b, 0:tq], ACT.Gelu, unit_done[0], pe_free["gt"][b])
                if tq < 256:
                    free[b] = gelu_last[0] = act(C3[:, j, tq:256], PS[:, b, tq:256], ACT.Gelu, unit_done[0], *c_free)
                if tq:
                    pe_free["gt"][b] = gm = tt(G, C3[:, j, 0:tq], C3[:, j, 0:tq], gtmp[:, 0:tq], ALU.mult, ga,
                                               quad_last[0])
            while applied < 64:
                for q in range(applied, mms):
                    gate_apply(q, 64)
                for q in range(mms, hots):
                    gate_mm(q)
                for q in range(hots, min(hots + 2, 64)):
                    gate_hots(q, half)
                applied, mms, hots = mms, hots, min(hots + 2, 64)
            if stage == 7 and half == 0:
                load(G, dbg[:, 0:16384], CC, quad_last[0], gelu_last[0], gm, store=True)
                return finish()
            start_wait = [bb[i] for i in range(2, 8)] + [free[0], free[1]]
            split_t = {}

            def split(j):
                c = j % 2
                ch, cl_ = CTH[:, c * 256:c * 256 + 256], CTL[:, c * 256:c * 256 + 256]
                hi = acopy(ch, C3[:, j, :], quad_last[0], gm, pe_free["ct"][c])
                split_t[j] = hi, tt(V, cl_, C3[:, j, :], ch.bitcast(F), ALU.subtract, hi)

            split(0)
            for j in range(64):
                n = un[0]
                un[0] += 1
                c = j % 2
                ch, cl_ = CTH[:, c * 256:c * 256 + 256], CTL[:, c * 256:c * 256 + 256]
                hi, lo = split_t[j]
                for h in range(2):
                    if h and j < 63:
                        split(j + 1)
                    prep_ahead(n, h)
                    kk_ = (n % 2) * 2 + h
                    for tp in range(2):
                        cth, ctl = ch[:, tp * 128:tp * 128 + 128], cl_[:, tp * 128:tp * 128 + 128]
                        for lhs, W, st_, sp_ in ((cth, WH, True, False), (cth, WL, False, False), (ctl, WH, False, True)):
                            for d in range(2):
                                m = mm(PS[:, 4 * tp + 2 * h + d, :], lhs, W[:, kk_, d * 512:d * 512 + 512],
                                       st_ and j == 0, sp_ and j == 63, lo, ready[(n, h)], *start_wait,
                                       sig=(d == 1 and sp_))
                    used[(n, h)] = m
                start_wait = []
                pe_free["ct"][c] = m
            vdone = m
            if half == 0:
                for i in range(8):
                    if i % 2:
                        e_ = acopy(ACC[:, i * 512:i * 512 + 512], PS[:, i, :], vdone, sel_done[0])
                    else:
                        e_ = vcopy(ACC[:, i * 512:i * 512 + 512], PS[:, i, :], vdone)
                    if i < 2:
                        free[i] = e_
                    else:
                        bb[i] = e_
                    v_evac[i] = e_
                c_free = [lo, hi]

        HN = f(76, 4096)
        LG, LB = f(92, 2048), f(100, 2048)
        t_h = load(G, HN, scratch["h"].rearrange("p a d -> p (a d)"), lo, hi, t_sc)
        t_g = load(G, LG, D["ln2g"])
        t_b = load(G, LB, D["ln2b"])
        t = stt(ACC, HN, ALPHA, ACC, ALU.mult, ALU.add, t_h, v_evac[7], v_evac[6])
        mu = f(108, 16)
        for p in range(2):
            X = ACC[:, p * 2048:p * 2048 + 2048]
            for d in range(4):
                t = tt(V, X[:, d * 512:d * 512 + 512], X[:, d * 512:d * 512 + 512], PS[:, 4 * p + d, :], ALU.add, t, vdone)
            o = 4 * p
            a = V.do(lambda e, X=X, o=o: e.tensor_reduce(mu[:, o:o + 1], X, AX.X, ALU.add), t)
            a = ts(V, mu[:, o:o + 1], mu[:, o:o + 1], 1.0 / 2048, None, ALU.mult, None, a)
            a = ts(V, X, X, mu[:, o:o + 1], None, ALU.subtract, None, a)
            a2 = act(HN[:, p * 2048:p * 2048 + 2048], X, ACT.Square, a, acc=mu[:, o + 1:o + 2])
            a2 = act(mu[:, o + 2:o + 3], mu[:, o + 1:o + 2], ACT.Sqrt, a2, scale=1.0 / 2048, bias=C("eps5"))
            a2 = recip(mu[:, o + 3:o + 4], mu[:, o + 2:o + 3], a2)
            a2 = stt(X, X, mu[:, o + 3:o + 4], LG, ALU.mult, ALU.mult, a2, t_g)
            a2 = tt(V, X, X, LB, ALU.add, a2, t_b)
            load(SP, out[0, p * 128:p * 128 + 128, :], X, a2, store=True)

        finish()


def layout(inputs):
    a = {k: np.asarray(v) for k, v in inputs.items()}

    def tiles(w):
        k, c = w.shape
        return np.ascontiguousarray(w.reshape(k // 2048, 16, 128, c // 128, 128).transpose(3, 0, 2, 1, 4)).reshape(
            (k // 2048) * (c // 128), 128, 2048)

    def turned(x):
        return np.ascontiguousarray(x.T.reshape(16, 128, 256).transpose(1, 0, 2)).reshape(128, 4096)

    def cols(g):
        return g.reshape(-1, 128).T

    w = a["dn_w_in"][0]
    w2 = a["w_in_2"][0]
    vec = np.concatenate([
        cols(a["norm_g"][0]), cols(a["mem_norm_g"]),
        a["dn_conv_w"][0].reshape(4, 48, 128).transpose(2, 1, 0).reshape(128, 192),
        cols(a["ln1_g_2"][0]), cols(a["ln1_b_2"][0]), cols(a["xa_q_norm_g"][0]), cols(a["xa_k_norm_g"][0]),
        cols(a["dn_out_norm_g"][0]), cols(a["pool_scale_2"][0]),
        np.broadcast_to(a["dn_a_log"], (128, 24)), np.broadcast_to(a["dn_dt_bias"], (128, 24))], axis=1)
    con, inv, hot = constants()
    order = list(range(8)) + list(range(8, 32, 2)) + list(range(9, 32, 2))
    return {
        "con": con, "inv": inv, "hot": hot, "vec": np.ascontiguousarray(vec),
        "xT": turned(a["x"][0]), "memT": turned(a["mem"][0]),
        "w_kv": tiles(a["mem_w_kv"][0]),
        "w_qkv": tiles(w[:, 0:6144]), "w_ab": tiles(w[:, 6144:6272]), "w_xq": tiles(w[:, 6192:7216]),
        "w_z": tiles(w[:, 7216:11312]),
        "w_o": tiles(a["w_out"][0].reshape(32, 128, 2048)[order].reshape(4096, 2048)),
        "w2": tiles(w2[:, 0:5120]),
        "w2_kiwi": tiles(np.concatenate([w2[:, 5120:5200], w2[:, 5072:5120]], axis=1)),
        "rb": a["rel_bias_2"],
        "pw": np.ascontiguousarray(a["pool_w_2"][0].reshape(4, 2, 128, 256).transpose(2, 0, 1, 3)).reshape(128, 2048),
        "w_o2": tiles(a["w_out_2"][0]), "w_q2": tiles(a["peer_wq_2"][0]),
        "sub": np.ascontiguousarray(a["peer_subkeys_2"][0].transpose(2, 0, 1)),
        "pu": np.ascontiguousarray(a["peer_u_2"][0].reshape(128, 128, 16, 128).transpose(1, 3, 2, 0)).reshape(
            128, 128, 2048),
        "pv": np.ascontiguousarray(a["peer_v_2"][0]),
        "ln2g": np.ascontiguousarray(np.broadcast_to(a["ln2_g_2"], (128, 2048))),
        "ln2b": np.ascontiguousarray(np.broadcast_to(a["ln2_b_2"], (128, 2048))),
    }


def kernel(**inputs):
    import concourse.bacc as bacc
    from concourse.bass_utils import run_bass_kernel_spmd

    nc = bacc.Bacc("TRN2", target_bir_lowering=False, num_devices=1)
    arrays = layout(inputs)
    D = {k: nc.dram_tensor(f"in_{k}", v.shape, mybir.dt.from_np(v.dtype), kind="ExternalInput").ap()
         for k, v in arrays.items()}
    out = nc.dram_tensor("out_0", (1, 256, 2048), F, kind="ExternalOutput").ap()
    scratch = {"bias": nc.dram_tensor("s_bias", (8, 384), F, kind="Internal").ap(),
               "h": nc.dram_tensor("s_h", (128, 2, 2048), F, kind="Internal").ap()}
    build(nc, D, out, scratch)
    res = run_bass_kernel_spmd(nc, [{f"in_{k}": v for k, v in arrays.items()}], core_ids=[0])
    return res.results[0]["out_0"]
```

```python
import math
from contextlib import ExitStack

import numpy as np
import concourse.bass as bass
from concourse import mybir

F = mybir.dt.float32
R = mybir.dt.float32r
U32 = mybir.dt.uint32
ALU = mybir.AluOpType
ACT = mybir.ActivationFunctionType
AX = mybir.AxisListType

KB = 256
NRAW = 3
ALPHA = 2.0 ** 0.25
BIG = 1e30
SEL_RATE = 0.22
NZ0 = 0
LEAD = 8
WAITS = (1, 2, 2, 1, 1)
FILL = 1.3
POOL = (6, 7, 4, 5, 2, 3, 0, 1)
LEVELS = (2, 4, 8, 16, 32)

CON = {}
_off = 0
for _n, _w in (("ident", 128), ("tri", 128), ("blk", 128), ("mt", 128), ("ms", 128), ("nm1", 128),
               ("nmt1", 128), ("mt2", 128), ("mt4", 128), ("mt8", 128), ("mt16", 128), ("mt32", 128),
               ("flip", 128), ("ones", 128), ("iota", 128), ("causal", 128), ("chunk", 2), ("iota16", 16),
               ("eps6", 1), ("eps5", 1)):
    CON[_n] = (_off, _w)
    _off += _w
NCON = _off

VEC = {}
_off = 0
for _n, _w in (("norm_g", 16), ("mem_g", 16), ("conv", 192), ("ln1g", 16), ("ln1b", 16), ("xaq", 2), ("xak", 2),
               ("outg", 1), ("pools", 8), ("alog", 24), ("dtb", 24)):
    VEC[_n] = (_off, _w)
    _off += _w
NVEC = _off


def constants():
    c = np.zeros((128, NCON), np.float32)
    p = np.arange(128)[:, None]
    x = np.arange(128)[None, :]
    same = (p // 64) == (x // 64)

    def put(name, a):
        o, w = CON[name]
        c[:, o:o + w] = a

    put("ident", p == x)
    put("tri", (p <= x) & same)
    put("blk", same)
    put("mt", np.where((p <= x) & same, 0.0, -BIG))
    put("ms", np.where((x < p) & same, 0.0, BIG))

    def low(s):
        return ((p // (2 * s)) == (x // (2 * s))) & ((p // s) % 2 == 1) & ((x // s) % 2 == 0)

    put("nm1", -1.0 * low(1))
    put("nmt1", -1.0 * low(1).T)
    for s in LEVELS:
        put(f"mt{s}", low(s).T)
    put("flip", (p + x) == 127)
    put("ones", 1.0)
    put("iota", x + 0 * p)
    put("causal", np.where(x <= p, 0.0, -BIG))
    put("chunk", (p // 64) == np.arange(2)[None, :])
    put("iota16", np.arange(16)[None, :] + 0 * p)
    put("eps6", 1e-6)
    put("eps5", 1e-5)
    inv = np.stack([1.0 / np.minimum(np.arange(256) + 1, w) for w in (2, 4, 8, 16)]).astype(np.float32)
    inv = np.ascontiguousarray(np.broadcast_to(inv.reshape(1, 1024), (128, 1024)))
    dist = np.maximum(255 - np.arange(384), 0)
    d = np.maximum(dist, 1).astype(np.float32)
    large = 16 + (np.log(d / np.float32(16)) / np.float32(math.log(8.0)) * np.float32(16)).astype(np.int32)
    bucket = np.where(dist < 16, dist, np.minimum(large, 31))
    hot = (np.arange(32)[:, None] == bucket[None, :]).astype(np.float32)
    return c, inv, hot


class Queue:

    def __init__(self, sem):
        self.sem, self.items, self.n, self.seen = sem, [], 0, {}

    def wait(self, tok):
        if tok is None:
            return
        sem, value = tok
        key = sem.name
        if self.seen.get(key, 0) < value:
            self.seen[key] = value
            self.items.append(lambda e: e.wait_ge(sem, value))

    def do(self, fn, *waits, sig=True):
        for w in waits:
            self.wait(w)
        if not sig:
            self.items.append(fn)
            return None
        self.n += 1
        self.items.append(lambda e: fn(e).then_inc(self.sem, 1))
        return (self.sem, self.n)

    def dma(self, fn, sem, value, *waits):
        for w in waits:
            self.wait(w)
        self.items.append(lambda e: fn(e).then_inc(sem, 16))
        return (sem, value)


def build(nc, D, out, scratch):
    ctx = ExitStack()
    with ctx:
        def sb(name, shape, dt):
            return ctx.enter_context(nc.sbuf_tensor(name, shape, dt))

        def semaphore(name):
            return ctx.enter_context(nc.semaphore(name))

        con = sb("cons", [128, NCON], F)
        vec = sb("vecs", [128, NVEC], F)
        keep = sb("keep", [128, 352], F)
        raw = sb("raw", [128, NRAW, 2048], F)
        WH = sb("WH", [128, 4, 1024], R)
        WL = sb("WL", [128, 4, 1024], R)
        PS = ctx.enter_context(nc.psum_tensor("PS", [128, 8, 512], F))

        PE = Queue(semaphore("pe"))
        V = Queue(semaphore("dve"))
        A = Queue(semaphore("act"))
        G = Queue(semaphore("pool"))
        SP = Queue(semaphore("sp"))

        views = {}

        def view(kb, n, dt):
            o = int(kb * KB)
            key = (o, n, dt)
            if key not in views:
                name = f"m{o}_{n}" + ("r" if dt == R else "")
                if o:
                    with nc.sbuf_tensor("pad_" + name, [128, o], F):
                        with nc.sbuf_tensor(name, [128, n], dt) as t:
                            pass
                else:
                    with nc.sbuf_tensor(name, [128, n], dt) as t:
                        pass
                views[key] = t[:, :]
            return views[key]

        def f(kb, n):
            return view(kb, n, F)

        def r(kb, n):
            return view(kb, n, R)

        def C(name):
            o, w = CON[name]
            return con[:, o:o + w]

        def vc(name, i=0, n=1):
            o, _ = VEC[name]
            return vec[:, o + i:o + i + n]

        def finish():
            for tok in last_store:
                SP.wait(tok)
            for tok in raw_in.values():
                SP.wait(tok)

            block = ctx.enter_context(nc.Block())

            def play(q):
                def body(e):
                    for item in q.items:
                        item(e)
                return body

            block.sync(play(SP))
            block.tensor(play(PE))
            block.vector(play(V))
            block.scalar(play(A))
            block.gpsimd(play(G))

        nload = [0]
        last_store = []

        def load(q, dst, src, *waits, store=False):
            nload[0] += 1
            s = semaphore(f"ld{nload[0]}")
            tok = q.dma(lambda e: e.dma_start(dst, src), s, 16, *waits)
            if store:
                last_store.append(tok)
            return tok

        def mm(o, l, x, start, stop, *waits, sig=False):
            return PE.do(lambda e: e.matmul(o, l, x, start=start, stop=stop), *waits, sig=sig)

        def tr(o, i, *waits, sig=False):
            return PE.do(lambda e: e.transpose(o, i, C("ident")), *waits, sig=sig)

        def tt(q, o, a, b, op, *waits):
            return q.do(lambda e: e.tensor_tensor(o, a, b, op), *waits)

        def ts(q, o, a, s1, s2, op0, op1, *waits):
            if op1 is None:
                return q.do(lambda e: e.tensor_scalar(o, a, s1, None, op0), *waits)
            return q.do(lambda e: e.tensor_scalar(o, a, s1, s2, op0, op1), *waits)

        def stt(o, a, s, b, op0, op1, *waits):
            return V.do(lambda e: e.scalar_tensor_tensor(out=o, in0=a, scalar=s, in1=b, op0=op0, op1=op1), *waits)

        def act(o, i, fn, *waits, scale=1.0, bias=0.0, acc=None):
            if acc is None:
                return A.do(lambda e: e.activation(o, i, fn, scale=scale, bias=bias), *waits)
            return A.do(lambda e: e.activation(o, i, fn, scale=scale, bias=bias, accum_out=acc), *waits)

        def acopy(o, i, *waits):
            return A.do(lambda e: e.copy(o, i), *waits)

        def vcopy(o, i, *waits):
            return V.do(lambda e: e.tensor_copy(o, i), *waits)

        def recip(o, i, *waits):
            return V.do(lambda e: e.reciprocal(o, i), *waits)

        def bc(ap, n, axis=1):
            w = ap.shape[1]
            return ap.unsqueeze(1).broadcast_to([128, n, w]) if axis == 1 else ap.unsqueeze(2).broadcast_to([128, w, n])

        units = []
        for i in range(16):
            units.append(D["w_kv"][i])
        units.append(D["w_ab"][0])
        for i in range(8):
            units.append(D["w_xq"][i])
        for i in range(12):
            units.append(D["w_qkv"][12 + i])
            units.append(D["w_qkv"][i])
        fill = [("v", i) for i in range(4)] + [("z", i) for i in range(NZ0)]
        nv, nz = 4, NZ0
        for g in range(10):
            fill += [("v", nv), ("v", nv + 1)]
            nv += 2
            for _ in range(3 if g % 3 == 0 else 2):
                if nz < 32:
                    fill.append(("z", nz))
                    nz += 1
        fill += [("z", i) for i in range(nz, 32)]
        for kind, i in fill:
            units.append(D["w_qkv"][24 + i] if kind == "v" else D["w_z"][i])
        for i in range(32):
            units.append(D["w_o"][i])
        units.append(D["w2_kiwi"][0])
        for g in (4, 2, 1, 3, 0):
            for i in range(8):
                units.append(D["w2"][8 * g + (i if g else POOL[i])])
        for i in range(16):
            units.append(D["w_o2"][i])
        for i in range(16):
            units.append(D["w_q2"][i])
        vv = D["pv"].rearrange("(i j) d -> j i d", j=128)
        for half in range(2):
            for j in range(64):
                units.append(D["pu"][64 * half + j])
            for j in range(64):
                units.append(vv[64 * half + j])
        raw_sem = [semaphore(f"raw{i}") for i in range(NRAW)]
        raw_in = {}
        ready = {}
        used = {}

        def issue(n, *waits):
            if n < len(units):
                raw_in[n] = SP.dma(lambda e: e.dma_start(raw[:, n % NRAW, :], units[n]),
                                   raw_sem[n % NRAW], 16 * (n // NRAW + 1), *waits)

        def prep(n, h):
            if (n, h) in ready or n >= len(units):
                return
            k = (n % 2) * 2 + h
            src = raw[:, n % NRAW, h * 1024:h * 1024 + 1024]
            free = used.get((n - 2, h))
            hi = acopy(WH[:, k, :], src, raw_in[n], free)
            lo = tt(V, WL[:, k, :], src, WH[:, k, :].bitcast(F), ALU.subtract, raw_in[n], hi, free)
            ready[(n, h)] = lo
            if h == 1:
                issue(n + NRAW, ready[(n, 0)], lo)

        def prep_ahead(n, h):
            for q in range(2 * n + h, 2 * n + h + 4):
                prep(q // 2, q % 2)

        un = [0]

        def unit(XH, XL, bank, *waits, start=True, stop=True, per=12, tiles=None):
            n = un[0]
            un[0] += 1
            for h in range(2):
                prep_ahead(n, h)
                k = (n % 2) * 2 + h
                cnt = 0
                for kt in range(8):
                    x = 8 * h + kt
                    wh = WH[:, k, kt * 128:kt * 128 + 128]
                    wl = WL[:, k, kt * 128:kt * 128 + 128]
                    first = start and h == 0 and kt == 0
                    if tiles:
                        PE.wait(tiles[x])
                    last = stop and h == 1 and kt == 7
                    mm(PS[:, bank, 0:256], wh, XH[:, x, :], first, False, ready[(n, h)], *waits)
                    mm(PS[:, bank, 0:256], wh, XL[:, x, :], False, False)
                    t = mm(PS[:, bank, 0:256], wl, XH[:, x, :], False, last, sig=(kt == 7))
                    cnt += 3
                    if kt == 7:
                        used[(n, h)] = t
                    if cnt % per == 0:
                        yield t
            unit_done[0] = t

        unit_done = [None]

        def drain(g):
            for _ in g:
                pass

        def together(a, b, k=1):
            for _ in a:
                for _ in range(k):
                    next(b, None)
            drain(b)

        XT, TMP, MT_ = f(64, 4096), f(80, 4096), f(96, 4096)
        quarter = lambda X, c: X[:, c * 1024:c * 1024 + 1024]
        t_mem = [load(SP, quarter(MT_, c), quarter(D["memT"], c)) for c in range(4)]
        for n in range(NRAW):
            issue(n)
        t_con = load(A, con[:, :], D["con"])
        t_vec = load(A, vec[:, :], D["vec"])
        t_x = [load(A, quarter(XT, c), quarter(D["xT"], c)) for c in range(4)]

        def k3(ap):
            return ap.rearrange("p (k t) -> p k t", t=256)

        def norm_T(src, t_src, gain, XH, XL, bank, rt, out_, first):
            sq = []
            for c in range(4):
                sq.append(act(quarter(TMP, c), quarter(src, c), ACT.Square, t_src[c], *(out_prev if not first else ())))
                if not first:
                    yield
            if first:
                prep(0, 0)
                prep(0, 1)
                for q in (PE, V, A, G):
                    q.wait(t_con)
                    q.wait(t_vec)
            for kt in range(16):
                t = mm(PS[:, bank, 0:256], C("ones"), TMP[:, kt * 256:kt * 256 + 256], kt == 0, kt == 15,
                       sq[kt // 4], sig=(kt == 15))
                if kt % 4 == 3:
                    yield
            a = act(rt, PS[:, bank, 0:256], ACT.Sqrt, t, scale=1.0 / 2048, bias=C("eps6"))
            b = recip(rt, rt, a)
            yield
            for c in range(4):
                m = tt(V, k3(quarter(TMP, c)), k3(quarter(src, c)), bc(rt, 4), ALU.mult, b)
                for kt in range(4 * c, 4 * c + 4):
                    hi = act(tile(XH, kt), tile(TMP, kt), ACT.Identity, m, scale=vc(gain, kt))
                    lo = stt(tile(XL, kt), tile(TMP, kt), vc(gain, kt), tile(XH, kt).bitcast(F), ALU.mult,
                             ALU.subtract, hi)
                    out_.append(lo)
                    if kt % 2:
                        yield

        def tile(ap, i, n=1):
            return ap[:, i * 256:(i + n) * 256]

        HH, HL = r(0, 4096), r(16, 4096)
        MH, ML = r(32, 4096), r(48, 4096)
        t_mr, t_hr_ = [], []
        out_prev = t_mr
        drain(norm_T(MT_, t_mem, "mem_g", MH, ML, 2, f(128, 256), t_mr, True))
        H3, L3, M3, N3 = k3(HH), k3(HL), k3(MH), k3(ML)

        free = {0: None, 1: None}
        MK = f(112, 2048)
        MV = f(120, 2048)
        MV3 = MV.rearrange("p (m c) -> p m c", m=2)
        XQ = f(64, 2048)
        XA = f(132, 2048)
        SQ = f(80, 2048)
        mk, xq = [], []
        sqx = {}

        def mk_units():
            for i in range(8):
                b = i % 2
                yield from unit(M3, N3, b, free[b], tiles=t_mr if i == 0 else None)
                free[b] = acopy(tile(MK, i), PS[:, b, 0:256], unit_done[0])
                mk.append(free[b])

        together(norm_T(XT, t_x, "norm_g", HH, HL, 3, f(129, 256), t_hr_, False), mk_units())
        t_hr = t_hr_[-1]
        vt_free = [None, None]
        b4 = [None, None]

        def mv_units():
            pend = None
            for i in range(9):
                b = i % 2
                if i < 8:
                    yield from unit(M3, N3, b, free[b])
                    tmp = f(130 + b, 256)
                    done = free[b] = acopy(tmp, PS[:, b, 0:256], unit_done[0], vt_free[b])
                if pend is not None:
                    pb, ptmp, pt, pi = pend
                    for m in range(2):
                        t2 = tr(PS[:, 4 + pb, m * 128:m * 128 + 128], ptmp[:, m * 128:m * 128 + 128], pt, b4[pb],
                                sig=(m == 1))
                    vt_free[pb] = t2
                    b4[pb] = vcopy(MV3[:, :, pi * 128:pi * 128 + 128],
                                   PS[:, 4 + pb, 0:256].rearrange("p (m c) -> p m c", m=2), t2, t_hr)
                pend = (b, tmp, done, i)

        def head_norm(X, tx, gain, st, prev, out_):
            s = tt(G, SQ, X, X, ALU.mult, tx, t_hr, prev)
            yield
            yield
            for h in range(4):
                for p in range(2):
                    for i in range(2):
                        t = mm(PS[:, 2, 2 * h + p:2 * h + p + 1], tile(SQ, 2 * h + i)[:, p * 128:p * 128 + 128],
                               C("ones")[:, 0:1], i == 0, i == 1, s, t_hr, keep_t[0] if keep_t else None,
                               sig=(i == 1))
            a = act(st, PS[:, 2, 0:8], ACT.Sqrt, t, scale=1.0 / 256, bias=C("eps6"))
            a = recip(st, st, a)
            yield
            for h in range(4):
                for p in range(2):
                    o = 256 * (h % 2) + 128 * p
                    t = mm(PS[:, 6 + h // 2, o:o + 128], st[:, 2 * h + p:2 * h + p + 1].to_broadcast([128, 128]),
                           C("ident"), True, True, a, prev, sig=True)
            yield
            for h in range(4):
                for i in range(2):
                    o = 256 * (h % 2)
                    a = stt(tile(X, 2 * h + i), tile(X, 2 * h + i), vc(gain, i), PS[:, 6 + h // 2, o:o + 256], ALU.mult,
                            ALU.mult, t)
            out_.append(a)

        keep_t = []
        k_n, q_n = [], []
        together(head_norm(MK, mk[-1], "xak", f(94, 8), None, k_n), mv_units(), 4)
        t_mv = b4[1]
        mem_pe = unit_done[0]

        AB = f(100, 256)
        drain(unit(H3, L3, 0, free[0]))
        free[0] = t_ab = acopy(AB, PS[:, 0, 0:256], unit_done[0], t_hr)
        KEEP = keep[:, 0:256]
        CDK = keep[:, 256:352]

        def small_gates():
            for p in range(2):
                t = tr(PS[:, 2, p * 128:p * 128 + 128], AB[:, p * 128:p * 128 + 128], t_ab, t_hr, sig=True)
            yield
            SM = f(101, 48 * 12)
            sm = lambda i, n=1: SM[:, 48 * i:48 * (i + n)]
            v2 = lambda ap: ap.rearrange("p (a h) -> p a h", a=2)
            a_ = vcopy(v2(sm(0)), PS[:, 2, 0:256].rearrange("p (a c) -> p a c", a=2)[:, :, 0:24], t)
            b_ = vcopy(v2(sm(1)), PS[:, 2, 0:256].rearrange("p (a c) -> p a c", a=2)[:, :, 24:48])
            x_ = tt(V, v2(sm(0)), v2(sm(0)), bc(vc("dtb", 0, 24), 2), ALU.add, a_, b_)
            n_ = ts(V, sm(2), sm(0), -1.0, None, ALU.mult, None, x_)
            n_ = tt(V, sm(2), sm(2), sm(0), ALU.min, n_)
            m_ = ts(V, sm(3), sm(0), 0.0, None, ALU.max, None, x_)
            yield
            e1 = act(sm(2), sm(2), ACT.Exp, n_)
            e2 = act(sm(4), sm(1), ACT.Exp, b_, scale=-1.0)
            e3 = act(f(104, 24), vc("alog", 0, 24), ACT.Exp, t_ab)
            e1 = act(sm(2), sm(2), ACT.Ln, e1, bias=1.0)
            s_ = tt(V, sm(3), sm(3), sm(2), ALU.add, m_, e1)
            GG = sm(5)
            g_ = tt(V, v2(GG), v2(sm(3)), bc(f(104, 24), 2), ALU.mult, s_, e3)
            g_ = ts(V, GG, GG, -1.0, None, ALU.mult, None, g_)
            BE = sm(6)
            e2 = ts(V, BE, sm(4), 1.0, None, ALU.add, None, e2)
            be_ = recip(BE, BE, e2)
            yield
            for p in range(2):
                t = mm(PS[:, 2, p * 24:p * 24 + 24], C("tri"), GG[:, p * 24:p * 24 + 24], True, True, g_)
                t = mm(PS[:, 2, 48 + p * 24:72 + p * 24], C("blk"), GG[:, p * 24:p * 24 + 24], True, True)
                for n in range(2):
                    o = 96 + (2 * p + n) * 24
                    t = mm(PS[:, 2, o:o + 24], C("chunk")[:, n:n + 1].to_broadcast([128, 128]), GG[:, p * 24:p * 24 + 24],
                           True, True, sig=True)
            GC = f(105, 192)
            c_ = vcopy(GC, PS[:, 2, 0:192], t)
            yield
            KD = sm(7)
            d_ = tt(V, KD, GC[:, 48:96], GC[:, 0:48], ALU.subtract, c_)
            kd_ = act(KD, KD, ACT.Exp, d_)
            CD = f(106, 96)
            cd_ = act(CD, GC[:, 96:192], ACT.Exp, c_)
            BX = sm(8)
            bx_ = act(BX, GC[:, 0:48], ACT.Exp, c_)
            bx_ = tt(V, BX, BX, BE, ALU.mult, bx_, be_)
            small = [kd_, cd_, bx_]
            k0 = vcopy(KEEP[:, 0:48], GG, *small)
            k0 = vcopy(KEEP[:, 48:96], BE)
            k0 = vcopy(KEEP[:, 96:144], KD)
            k0 = vcopy(KEEP[:, 144:192], BX)
            k0 = vcopy(KEEP[:, 192:240], GC[:, 0:48])
            k0 = vcopy(CDK, CD)
            keep_t.append(k0)

        def xq_units():
            for i in range(8):
                b = (i + 1) % 2
                yield from unit(H3, L3, b, t_hr, free[b])
                free[b] = acopy(tile(XQ, i), PS[:, b, 0:256], unit_done[0], t_hr)
                xq.append(free[b])

        together(small_gates(), xq_units(), 4)

        def cross():
            yield from head_norm(XQ, xq[-1], "xaq", f(95, 8), k_n[0], q_n)
            ready_ = q_n[0]
            bank_free = {2: None, 3: None, 4: b4[0], 5: b4[1], 6: None, 7: None}
            p_free = [None, None]
            pt_free = [None, None]
            xa_t = []
            it = 0
            for h in range(4):
                PT = f(96 + 2 * (h % 2), 512).rearrange("p (m t) -> p m t", m=2)
                for p in range(2):
                    bk = 2 + it % 2
                    P = f(92 + it % 2, 256)
                    st = f(94 + it % 2, 8)
                    for i in range(2):
                        t = mm(PS[:, bk, 0:256], tile(XQ, 2 * h + i)[:, p * 128:p * 128 + 128], tile(MK, 2 * h + i),
                               i == 0, i == 1, ready_, bank_free[bk], sig=(i == 1))
                    mx = V.do(lambda e, st=st, bk=bk: e.tensor_reduce(st[:, 0:1], PS[:, bk, 0:256], AX.X, ALU.max, negate=True),
                              t, p_free[it % 2])
                    m2 = ts(V, st[:, 1:2], st[:, 0:1], 1.0 / 16, None, ALU.mult, None, mx)
                    ex = act(P, PS[:, bk, 0:256], ACT.Exp, m2, scale=1.0 / 16, bias=st[:, 1:2], acc=st[:, 2:3])
                    bank_free[bk] = ex
                    rc = recip(st[:, 3:4], st[:, 2:3], ex)
                    nm = ts(V, P, P, st[:, 3:4], None, ALU.mult, None, rc)
                    yield
                    b2 = 4 + it % 2
                    for m in range(2):
                        t = tr(PS[:, b2, m * 128:m * 128 + 128], P[:, m * 128:m * 128 + 128], nm, bank_free[b2], sig=(m == 1))
                    p_free[it % 2] = t
                    bank_free[b2] = cp = vcopy(PT[:, :, p * 128:p * 128 + 128],
                                               PS[:, b2, 0:256].rearrange("p (m t) -> p m t", m=2), t, pt_free[h % 2])
                    it += 1
                    yield
                for i in range(2):
                    b3 = 6 + i
                    for m in range(2):
                        t = mm(PS[:, b3, 0:256], MV3[:, m, (2 * h + i) * 128:(2 * h + i) * 128 + 128], PT[:, m, :],
                               m == 0, m == 1, cp, t_mv, bank_free[b3], sig=(m == 1))
                    bank_free[b3] = acopy(tile(XA, 2 * h + i), PS[:, b3, 0:256], t, vt_free[0], vt_free[1])
                    xa_t.append(bank_free[b3])
                pt_free[h % 2] = t
                yield
            cross_end.extend([xa_t[-1], t, bank_free[2], bank_free[3], bank_free[4], bank_free[5], bank_free[6], bank_free[7]])

        cross_end = []

        QK, VT = f(32, 6144), f(56, 6144)
        QT, KT = QK[:, 0:3072], QK[:, 3072:6144]
        RN = f(130, 48)
        sq_t = {}

        def sq_tile(i):
            if i < 5:
                return f(107 + i, 256)
            if i < 13:
                return f(72 + i - 5, 256)
            if i < 17:
                return f(60 + i - 13, 256)
            return f(100 + i - 17, 256)

        conv_free = [None] * 2
        cv = [0]

        def conv_tile(dst, widx, bank, done, *waits):
            i = cv[0] % 2
            cv[0] += 1
            tmp = f(128 + i, 256)
            t = ts(V, tmp, PS[:, bank, 0:256], vc("conv", widx * 4 + 3), None, ALU.mult, None, done, conv_free[i], t_hr)
            for s in (1, 2, 3):
                t = stt(tmp[:, s:256], PS[:, bank, 0:256 - s], vc("conv", widx * 4 + 3 - s), tmp[:, s:256],
                        ALU.mult, ALU.add, t)
            conv_free[i] = a = act(dst, tmp, ACT.Silu, t, *waits)
            return t, a

        qk_t = []

        def qk_units():
            for i in range(24):
                hk, isq = i // 2, i % 2
                b = i % 2
                yield from unit(H3, L3, b, free[b])
                dst = tile(QT if isq else KT, hk)
                free[b], a = conv_tile(dst, hk if isq else 12 + hk, b, unit_done[0], mem_pe)
                qk_t.append(a)
                x = sq_tile(i)
                at = hk if isq else 12 + hk
                sq_t[at] = x, tt(G, x, dst, dst, ALU.mult, a, keep_t[0] if i >= 17 else None)

        together(cross(), qk_units(), 3)
        GG, BE, KD, BX, GC = (KEEP[:, 48 * i:48 * i + 48] for i in range(5))
        KEEP_T = keep_t[0]

        def qk_norm():
            for i in range(24):
                x, tx = sq_t[i]
                for p in range(2):
                    t = mm(PS[:, 2, 2 * i + p:2 * i + p + 1], x[:, p * 128:p * 128 + 128], C("ones")[:, 0:1], True, True,
                           tx, cross_end[2], sig=True)
                if i % 6 == 5:
                    yield
            a = act(RN, PS[:, 2, 0:48], ACT.Sqrt, t, cross_end[1], bias=C("eps6"))
            a = recip(RN, RN, a)
            nb[2] = a = ts(V, RN[:, 0:24], RN[:, 0:24], 128.0 ** -0.5, None, ALU.mult, None, a)
            yield
            yield
            for c in range(12):
                bk = 2 + (c + 1) % 6
                for i in range(4):
                    o = 4 * c + i
                    t = mm(PS[:, bk, i * 128:i * 128 + 128], RN[:, o:o + 1].to_broadcast([128, 128]), C("ident"), True, True,
                           a, nb[bk], *cross_end, sig=(i == 3))
                q = QK[:, c * 512:c * 512 + 512]
                nb[bk] = b = tt(V, q, q, PS[:, bk, :], ALU.mult, t, qk_t[-1])
                yield
            qk_n.append(b)

        nb = {i: None for i in range(2, 8)}
        qk_n = []
        v_t = []

        ztok = {}
        gdone = []

        def ztile(i):
            if i < 8:
                return tile(f(80, 2048), i)
            if i < 10:
                return tile(f(130, 512), i - 8)
            return tile(KT if i % 2 else QT, (i - 10) // 2)

        def vz_units():
            for n, (kind, i) in enumerate(fill):
                while kind == "z" and i >= 10 and len(gdone) <= (i - 10) // 2:
                    yield
                while kind == "v" and i >= 4 and not qk_n:
                    yield
                b = n % 2
                yield from unit(H3, L3, b, free[b], per=6)
                if kind == "v":
                    free[b], a = conv_tile(tile(VT, i), 24 + i, b, unit_done[0], *cross_end)
                    v_t.append(a)
                else:
                    w = gdone[(i - 10) // 2] if i >= 10 else qk_n[0] if i >= 8 else cross_end[1]
                    ztok[i] = free[b] = act(ztile(i), PS[:, b, 0:256], ACT.Silu, unit_done[0], w, cross_end[0])

        fz = vz_units()
        for _ in qk_norm():
            for _ in range(3):
                next(fz)
        while len(v_t) < 2:
            next(fz)

        bankfree = {i: nb[i] for i in range(2, 8)}
        slot_t = [qk_n[0], qk_n[0]]
        y_t = {}

        def group(g):
            s = g % 2
            bA, bB, bC = 2 + 3 * s, 3 + 3 * s, 4 + 3 * s
            base = 88 + 20 * s
            w = lambda kb, n=512: f(base + kb, n)
            kb, bv, kdc, dT, qd, Lb, LT, T, U, BT = (w(2 * i) for i in range(10))
            u, S = T[:, 0:256], T[:, 256:512]
            start = [slot_t[s], qk_n[0], v_t[2 * g + 1], KEEP_T]
            kT, qT = tile(KT, g), tile(QT, g)
            vT = [tile(VT, 2 * g), tile(VT, 2 * g + 1)]
            col = lambda M, i: M[:, (i % 2) * 24 + 2 * g + i // 2:(i % 2) * 24 + 2 * g + i // 2 + 1]
            blk = lambda X, i: X[:, i * 128:i * 128 + 128]
            c4 = lambda X: X.rearrange("p (i c) -> p i c", i=4)
            for p in range(2):
                kp, qp = kT[:, p * 128:p * 128 + 128], qT[:, p * 128:p * 128 + 128]
                mm(PS[:, bA, p * 128:p * 128 + 128], kp, kp, True, True, *start, bankfree[bA])
                tA = mm(PS[:, bA, 256 + p * 128:384 + p * 128], kp, qp, True, True, sig=(p == 1))
            for i in range(4):
                tB = mm(PS[:, bB, i * 128:i * 128 + 128], col(GG, i).to_broadcast([128, 128]), C("tri"), True, True,
                        bankfree[bB], sig=(i == 3))
            for p in range(2):
                tr(PS[:, bC, p * 128:p * 128 + 128], kT[:, p * 128:p * 128 + 128], bankfree[bC])
            for p in range(2):
                tC = tr(PS[:, bC, 256 + p * 128:384 + p * 128], vT[0][:, p * 128:p * 128 + 128], sig=(p == 1))
            yield
            for i in range(4):
                d1 = stt(blk(dT, i), PS[:, bB, i * 128:i * 128 + 128], col(GC, i), C("mt"), ALU.subtract, ALU.add, tB,
                         *start)
            for i in range(4):
                d2 = stt(blk(Lb, i), PS[:, bB, i * 128:i * 128 + 128], col(GC, i), C("ms"), ALU.subtract, ALU.add)
            eB = act(qd, PS[:, bB, :], ACT.Exp, d2)
            eL = act(Lb, Lb, ACT.Exp, d2, scale=-1.0)
            eT = act(dT, dT, ACT.Exp, d1)
            for i in range(4):
                kpi = PS[:, bC, (i % 2) * 128:(i % 2) * 128 + 128]
                k1 = act(blk(kb, i), kpi, ACT.Copy, tC, *start, scale=col(BX, i))
                k2 = act(blk(kdc, i), kpi, ACT.Copy, scale=col(KD, i))
            for p in range(2):
                v1 = act(blk(bv, p), PS[:, bC, 256 + p * 128:384 + p * 128], ACT.Copy, scale=col(BE, p))
            for _ in range(WAITS[0]):
                yield
            for p in range(2):
                tB = tr(PS[:, bB, p * 128:p * 128 + 128], vT[1][:, p * 128:p * 128 + 128], eB, sig=(p == 1))
            yield
            for i in range(4):
                lk = stt(blk(Lb, i), blk(Lb, i), col(BE, i), PS[:, bA, (i % 2) * 128:(i % 2) * 128 + 128], ALU.mult,
                         ALU.mult, eL, tA)
            h2 = lambda X: X.rearrange("p (h c) -> p h c", h=2)
            qk = tt(V, h2(dT), h2(dT), bc(PS[:, bA, 256:512], 2), ALU.mult, eT)
            qd_ = tt(G, h2(qd), h2(qd), bc(qT, 2), ALU.mult, eB)
            for p in range(2):
                v1 = act(blk(bv, 2 + p), PS[:, bB, p * 128:p * 128 + 128], ACT.Copy, tB, scale=col(BE, 2 + p))
            for _ in range(WAITS[1]):
                yield
            for i in range(4):
                t = tr(PS[:, bA, i * 128:i * 128 + 128], blk(Lb, i), lk, qk, sig=(i == 3))
            cl = acopy(LT, PS[:, bA, :], t, *start)
            T1 = tt(V, c4(T), c4(Lb), bc(C("nm1"), 4), ALU.mult, lk)
            T1 = tt(V, c4(T), c4(T), bc(C("ident"), 4), ALU.add, T1)
            yield
            bt = tt(G, c4(BT), c4(LT), bc(C("mt2"), 4), ALU.mult, cl, *start)
            U1 = tt(G, c4(U), c4(LT), bc(C("nmt1"), 4), ALU.mult, cl)
            U1 = tt(G, c4(U), c4(U), bc(C("ident"), 4), ALU.add, U1)
            for _ in range(WAITS[2]):
                yield
            freeB, freeA, freeC = v1, cl, v1
            for s_ in LEVELS:
                for i in range(4):
                    t = mm(PS[:, bB, i * 128:i * 128 + 128], blk(BT, i), blk(T, i), True, True, bt, T1, freeB, sig=(i == 3))
                freeB = x = acopy(Lb, PS[:, bB, :], t, lk, T1)
                if s_ != 32:
                    bt = tt(G, c4(BT), c4(LT), bc(C(f"mt{2 * s_}"), 4), ALU.mult, t)
                yield
                if s_ != 32:
                    for i in range(4):
                        tA = mm(PS[:, bA, i * 128:i * 128 + 128], blk(U, i), blk(Lb, i), True, True, x, U1, freeA,
                                sig=(i == 3))
                for i in range(4):
                    tC = mm(PS[:, bC, i * 128:i * 128 + 128], blk(Lb, i), blk(U, i), True, True, x, U1, freeC,
                            sig=(i == 3))
                if s_ != 32:
                    freeA = T1 = tt(V, T, T, PS[:, bA, :], ALU.subtract, tA)
                freeC = U1 = tt(V, U, U, PS[:, bC, :], ALU.subtract, tC)
                yield
            for i in range(4):
                t = mm(PS[:, bB, i * 128:i * 128 + 128], blk(kb, i), blk(U, i), True, True, k1, U1, freeB, sig=(i == 3))
            freeB = nw = A.do(lambda e: e.mul(LT, PS[:, bB, :], -1.0), t, bt)
            yield
            St = None
            ut = None
            for n in range(4):
                p, b = n // 2, 64 * (n % 2)
                for h in range(2):
                    i = 2 * h + p
                    o = PS[b:b + 64, bA, h * 128:h * 128 + 128]
                    t = mm(o, blk(U, i)[:, b:b + 64], blk(bv, i), True, n == 0, v1, freeA, sig=(h == 1 and n == 0))
                    if n:
                        t = mm(o, blk(LT, i)[:, b:b + 64], blk(S, h), False, True, nw, St, sig=(h == 1))
                freeA = ut = acopy(u[b:b + 64, :], PS[b:b + 64, bA, 0:256], t, *start)
                yield
                for h in range(2):
                    i = 2 * h + p
                    o = PS[:, bC, h * 256 + n * 64:h * 256 + n * 64 + 64]
                    if n:
                        mm(o, blk(S, h), blk(qd, i)[:, b:b + 64], True, False, qd_, St)
                    tC = mm(o, u[b:b + 64, h * 128:h * 128 + 128], dT[b:b + 64, i * 128 + b:i * 128 + b + 64], n == 0,
                            True, ut, freeC, qk, sig=(h == 1))
                if n < 3:
                    for h in range(2):
                        i = 2 * h + p
                        t = mm(PS[:, bB, h * 128:h * 128 + 128], kdc[b:b + 64, i * 128:i * 128 + 128],
                               u[b:b + 64, h * 128:h * 128 + 128], True, True, k2, freeB, sig=(h == 1))
                    for h in range(2):
                        if n == 0:
                            St = vcopy(blk(S, h), PS[:, bB, h * 128:h * 128 + 128], t, *start)
                        else:
                            cc = CDK[:, n * 24 + 2 * g + h:n * 24 + 2 * g + h + 1]
                            St = stt(blk(S, h), blk(S, h), cc, PS[:, bB, h * 128:h * 128 + 128], ALU.mult, ALU.add, t, St)
                    freeB = St
                yield
            y = tile(VT, 2 * g, 2)
            yt = acopy(y, PS[:, bC, :], tC)
            gdone.append(yt)
            sq = tt(G, kb, y, y, ALU.mult, yt)
            for _ in range(WAITS[3]):
                yield
            for i in range(4):
                t = mm(PS[:, bA, i:i + 1], blk(kb, i), C("ones")[:, 0:1], True, True, sq, freeA, sig=(i == 3))
            rr = S[:, 0:4]
            freeA = a = act(rr, PS[:, bA, 0:4], ACT.Sqrt, t, scale=1.0 / 128, bias=C("eps6"))
            a = recip(rr, rr, a)
            for _ in range(WAITS[4]):
                yield
            for i in range(4):
                t = mm(PS[:, bB, i * 128:i * 128 + 128], rr[:, i:i + 1].to_broadcast([128, 128]), C("ident"), True, True, a,
                       freeB, sig=(i == 3))
            yield
            yt = stt(y, y, vc("outg"), PS[:, bB, :], ALU.mult, ALU.mult, t)
            y_t[g] = yt
            bankfree[bA], bankfree[bB], bankfree[bC] = freeA, yt, sq
            slot_t[s] = yt

        def gate_tile(i):
            z = ztile(i)
            y = tile(VT, i) if i < 24 else tile(XA, i - 24)
            p_t[i] = tt(G, z, z, y, ALU.mult, ztok[i], y_t[i // 2] if i < 24 else cross_end[0])

        def gates():
            for i in range(32):
                if i not in p_t and i in ztok and (i >= 24 or i // 2 in y_t):
                    gate_tile(i)

        p_t = {}
        live = []
        nextg = 0
        credit = 0.0
        while nextg < 12 or live:
            if nextg < 12 and len(live) < 2 and len(v_t) >= 2 * nextg + 2:
                live.append(group(nextg))
                nextg += 1
                if nextg == 1:
                    for _ in range(LEAD):
                        next(live[0], None)
                        next(fz, None)
            if not live:
                next(fz)
            for x in list(live):
                try:
                    next(x)
                except StopIteration:
                    live.remove(x)
                credit += FILL
                while credit >= 1:
                    next(fz, None)
                    credit -= 1
            gates()
        drain(fz)
        gates()

        YH, YL = r(0, 8192), r(88, 8192)
        zpe = unit_done[0]
        at = 0
        mix = [None] * 32
        first, second, third = list(range(8)), list(range(10, 32, 2)), list(range(11, 32, 2))
        for src, zs in ((f(80, 2048), first[:4]), (f(80, 2048), first[4:]), (QT, second[:4]), (QT, second[4:8]),
                        (QT, second[8:]), (KT, third[:4]), (KT, third[4:8]), (KT, third[8:]), (f(130, 512), [8, 9])):
            k0 = zs[0] if zs[0] < 8 else 0 if zs[0] == 8 else (zs[0] - 10) // 2
            n = len(zs)
            x, yh, yl = tile(src, k0, n), tile(YH, at, n), tile(YL, at, n)
            hi = acopy(yh, x, *[p_t[i] for i in zs], zpe)
            lo = tt(V, yl, x, yh.bitcast(F), ALU.subtract, hi, zpe, slot_t[0], slot_t[1])
            mix[at:at + n] = [lo] * n
            at += n
        X1 = f(32, 4096)
        X1H, X1L = r(48, 4096), r(64, 4096)
        t_x = load(G, X1, D["xT"], mix[-1])
        Y3, W3 = k3(YH), k3(YL)
        x1_t = []
        for m in range(16):
            b = m % 2
            drain(unit(Y3, W3, b, free[b], stop=False, tiles=None if m else mix))
            drain(unit(Y3[:, 16:32, :], W3[:, 16:32, :], b, start=False, tiles=None if m else mix[16:]))
            free[b] = a = tt(V, tile(X1, m), PS[:, b, 0:256], tile(X1, m), ALU.add, unit_done[0], t_x)
            hi = acopy(tile(X1H, m), tile(X1, m), a)
            x1_t.append(tt(V, tile(X1L, m), tile(X1, m), tile(X1H, m).bitcast(F), ALU.subtract, hi, a))
        wo_pe = unit_done[0]

        P3, Q3 = k3(X1H), k3(X1L)
        QI, KI, KK, QQ = f(0, 2048), f(8, 256), f(9, 2048), f(17, 2048)
        WI = f(25, 32).rearrange("p (a h) -> p a h", a=2)
        SC, WK, MM = f(26, 512), f(28, 512), f(30, 512)
        VN = f(80, 2048).rearrange("p (m c) -> p m c", m=2)
        HK = f(88, 2048).rearrange("p (h x) -> p h x", h=8)
        PT_ = f(96, 2048)
        XH2, XL2 = r(104, 4096), r(120, 4096)
        HOT, RB, BV = f(96, 384)[0:32, :], f(98, 8)[0:32, :], f(99, 384)[0:8, :]
        t1 = load(G, HOT, D["hot"], mix[-1], wo_pe)
        t2 = load(G, RB, D["rb"])
        t = mm(PS[0:8, 2, 0:384], RB, HOT, True, True, t1, t2, bankfree[2], sig=True)
        t = vcopy(BV, PS[0:8, 2, 0:384], t)
        sv = load(G, scratch["bias"], BV, t, store=True)
        hsrc = scratch["bias"]
        hank = bass.AP(hsrc.tensor, hsrc.offset, [[1, 128], [384, 8], [1, 256]])
        t_hk = load(G, HK, hank, sv, wo_pe)

        T1 = f(136, 256)
        drain(unit(P3, Q3, 0, x1_t[-1], free[0]))
        free[0] = a = vcopy(T1, PS[:, 0, 0:256], unit_done[0], wo_pe)
        t_ki = vcopy(KI[0:64, :], T1[0:64, :], a)
        t_ki2 = load(G, KI[64:128, :], T1[0:64, :], a)
        for p in range(2):
            t = tr(PS[:, 2, p * 128:p * 128 + 128], T1[:, p * 128:p * 128 + 128], a, t, sig=True)
        t_wi = ts(V, WI, PS[:, 2, 0:256].rearrange("p (a c) -> p a c", a=2)[:, :, 64:80], 1.0 / 32, None, ALU.mult,
                  None, t)
        bk = {i: t_wi for i in range(2, 8)}
        rel_free = [None] * 4
        it = 0
        sc_t = t_wi
        for i in range(8):
            b = i % 2
            drain(unit(P3, Q3, b, free[b]))
            free[b] = q_ = acopy(tile(QI, i), PS[:, b, 0:256], unit_done[0])
            for hh in (2 * i, 2 * i + 1):
                o = 64 * (hh % 2)
                for p in range(2):
                    S_ = 128 * (p + 1)
                    kb_ = 2 + it % 6
                    t = mm(PS[:, kb_, 0:S_], tile(QI, i)[o:o + 64, p * 128:p * 128 + 128], KI[o:o + 64, 0:S_], True, True,
                           q_, t_ki, t_ki2, bk[kb_], sig=True)
                    rl = f(136 + it % 4, S_)
                    bk[kb_] = a = act(rl, PS[:, kb_, 0:S_], ACT.Relu, t, rel_free[it % 4], t_wi)
                    sc = SC[:, p * 256:p * 256 + S_]
                    if hh == 0:
                        sc_t = ts(V, sc, rl, WI[:, p, hh:hh + 1], None, ALU.mult, None, a, wo_pe)
                    else:
                        sc_t = stt(sc, rl, WI[:, p, hh:hh + 1], sc, ALU.mult, ALU.add, a, sc_t)
                    rel_free[it % 4] = sc_t
                    it += 1
        mx8 = f(25.5, 8)

        def topk():
            for p in range(2):
                S_ = 128 * (p + 1)
                sc, wk, m = (X[:, p * 256:p * 256 + S_] for X in (SC, WK, MM))
                d = slice(S_ - 128, S_)
                t = tt(V, sc[:, d], sc[:, d], C("causal"), ALU.add, sc_t)
                src = sc
                for k in range(8):
                    t = V.do(lambda e, src=src: e.max(out=mx8, in_=src), t)
                    t = V.do(lambda e, src=src, wk=wk: e.match_replace(out=wk, in_to_replace=mx8, in_values=src,
                                                                       imm_value=-3e38), t)
                    src = wk
                    yield
                t = ts(V, m, wk, -2e38, -BIG, ALU.is_gt, ALU.mult, t)
                t = tt(V, m[:, d], m[:, d], C("causal"), ALU.add, t)
                m_t.append(t)
                yield

        m_t = []
        tk = topk()
        kq_t = []
        for i in range(16):
            b = i % 2
            drain(unit(P3, Q3, b, free[b]))
            if i < 8:
                free[b] = acopy(tile(KK, i), PS[:, b, 0:256], unit_done[0])
            else:
                free[b] = A.do(lambda e, i=i, b=b: e.mul(tile(QQ, i - 8), PS[:, b, 0:256], 128.0 ** -0.5), unit_done[0])
            kq_t.append(free[b])
            next(tk, None)
            next(tk, None)
        drain(tk)
        vt = [None, None]
        x2_t = {}
        att = [None]
        pt_t = {}

        def pt_tile(h):
            return f(120 + 1.5 * h, 384) if h < 5 else f(104 + 1.5 * (h - 5), 384)

        def v2_units():
            pend = None
            for i in range(9):
                if i < 8:
                    b = i % 2
                    yield from unit(P3, Q3, b, free[b])
                    tmp = f(136 + b, 256)
                    done = free[b] = acopy(tmp, PS[:, b, 0:256], unit_done[0], vt[b], sc_t)
                if pend:
                    pb, ptmp, pt, pi = pend
                    for m in range(2):
                        t = tr(PS[:, 6 + pb, m * 128:m * 128 + 128], ptmp[:, m * 128:m * 128 + 128], pt, bk[6 + pb],
                               sig=(m == 1))
                    vt[pb] = t
                    bk[6 + pb] = vcopy(VN[:, :, pi * 128:pi * 128 + 128],
                                       PS[:, 6 + pb, 0:256].rearrange("p (m c) -> p m c", m=2), t, wo_pe)
                pend = (b, tmp, done, i)

        def weights():
            pf = [None] * 2
            pend = None
            for it in range(17):
                if it < 16:
                    h, p = it // 2, it % 2
                    S_ = 128 * (p + 1)
                    kb_ = 2 + it % 2
                    P = f(it % 2, S_)
                    st = f(2 + it % 2, 8)
                    mm(PS[:, kb_, 0:S_], tile(QQ, h)[:, p * 128:p * 128 + 128], tile(KK, h)[:, 0:S_], True, False,
                       kq_t[-1], bk[kb_])
                    t = mm(PS[:, kb_, 0:S_], C("flip"), HK[:, h, 256 - S_:256], False, True, t_hk, sig=True)
                    bk[kb_] = a = tt(V, P, PS[:, kb_, 0:S_], MM[:, p * 256:p * 256 + S_], ALU.add, t, m_t[-1],
                                     pf[it % 2], sc_t)
                    a = V.do(lambda e, st=st, P=P: e.tensor_reduce(st[:, 0:1], P, AX.X, ALU.max, negate=True), a)
                    a = act(P, P, ACT.Exp, a, bias=st[:, 0:1], acc=st[:, 2:3])
                    yield
                if pend:
                    a1, P1, st1, h1, p1, it1 = pend
                    a1 = recip(st1[:, 3:4], st1[:, 2:3], a1)
                    a1 = ts(V, P1, P1, st1[:, 3:4], None, ALU.mult, None, a1)
                    yield
                    b2 = 4 + it1 % 2
                    for m in range(p1 + 1):
                        t = tr(PS[:, b2, m * 128:m * 128 + 128], P1[:, m * 128:m * 128 + 128], a1, bk[b2], sig=(m == p1))
                    pf[it1 % 2] = t
                    bk[b2] = pt_t[h1] = vcopy(pt_tile(h1)[:, p1 * 128:p1 * 128 + 128 * (p1 + 1)],
                                              PS[:, b2, 0:128 * (p1 + 1)], t, wo_pe)
                if it < 16:
                    pend = (a, P, st, h, p, it)

        def values():
            for h in range(8):
                PT = pt_tile(h)
                b3 = 6 + h % 2
                mm(PS[:, b3, 0:128], VN[:, 0, h * 128:h * 128 + 128], PT[:, 0:128], True, True, pt_t[h], t_vn, bk[b3])
                mm(PS[:, b3, 128:256], VN[:, 0, h * 128:h * 128 + 128], PT[:, 128:256], True, False)
                t = mm(PS[:, b3, 128:256], VN[:, 1, h * 128:h * 128 + 128], PT[:, 256:384], False, True, sig=True)
                hi = acopy(tile(XH2, 8 + h), PS[:, b3, 0:256], t, wo_pe, sc_t)
                bk[b3] = lo = tt(V, tile(XL2, 8 + h), PS[:, b3, 0:256], tile(XH2, 8 + h).bitcast(F), ALU.subtract, hi)
                x2_t[8 + h] = lo
                att[0] = t
                yield
                yield

        together(weights(), v2_units())
        t_vn = bk[7]
        INV = f(136, 1024)
        t_inv = load(G, INV, D["inv"], vt[0], vt[1])

        ping = [f(26, 256), f(28, 256)]

        def pool_units():
            prev = m_t[-1]
            for n, c in enumerate(POOL):
                b = n % 2
                yield from unit(P3, Q3, b, free[b])
                x = tile(PT_, c)
                free[b] = a = acopy(x, PS[:, b, 0:256], unit_done[0], t_hk)
                cur = x
                for k in range(c // 2 + 1):
                    st = 1 << k
                    nx = ping[k % 2]
                    a = tt(G, nx[:, st:256], cur[:, st:256], cur[:, 0:256 - st], ALU.add, a, prev)
                    a = G.do(lambda e, nx=nx, cur=cur, st=st: e.tensor_copy(nx[:, 0:st], cur[:, 0:st]), a)
                    cur = nx
                a = tt(G, cur, cur, INV[:, (c // 2) * 256:(c // 2) * 256 + 256], ALU.mult, a, t_inv)
                prev = tt(G, x, cur, x, ALU.subtract, a)
                pool_t[c] = prev

        pool_t = {}
        PW = f(88, 2048).rearrange("p (g d) -> p g d", g=8)
        t_pw = load(G, PW, D["pw"], pt_t[7])
        together(values(), pool_units())
        for g in (3, 2, 1, 0):
            for d in range(2):
                kb_ = 2 + (2 * g + d) % 6
                for c in range(2):
                    t = mm(PS[:, kb_, 0:256], PW[:, 2 * g + c, d * 128:d * 128 + 128], tile(PT_, 2 * g + c), c == 0, c == 1,
                           t_pw, pool_t[2 * g], pool_t[2 * g + 1], bk[kb_], sig=(c == 1))
                i = 2 * g + d
                hi = act(tile(XH2, i), PS[:, kb_, 0:256], ACT.Identity, t, att[0], scale=vc("pools", i))
                bk[kb_] = x2_t[i] = stt(tile(XL2, i), PS[:, kb_, 0:256], vc("pools", i), tile(XH2, i).bitcast(F), ALU.mult,
                                        ALU.subtract, hi)
        Z3, R3 = k3(XH2), k3(XL2)
        r1_t = []
        CM, MU, RS, MR = f(80, 256), f(81, 256), f(82, 256), f(83, 256)
        dev = {}
        stat = [None]
        start_sq = [None] * 4

        def mean_part(m):
            stat[0] = mm(PS[:, 2, 0:256], C("ones"), tile(X1, m), m == 0, m == 5, r1_t[m], bk[2], bk[3], sig=(m == 5))
            if m == 5:
                dev["c"] = ts(V, CM, PS[:, 2, 0:256], 1.0 / 768, None, ALU.mult, None, stat[0], att[0])

        def deviate(m):
            dev[m] = tt(V, tile(X1, m), tile(X1, m), CM, ALU.subtract, r1_t[m], dev["c"])
            dev["s", m] = act(f(84 + m % 4, 256), tile(X1, m), ACT.Square, dev[m], start_sq[m % 4], att[0])

        def add_part(m):
            mm(PS[:, 2, 0:256], C("ones"), tile(X1, m), m == 0, m == 15, dev[m], sig=True)
            start_sq[m % 4] = stat[0] = mm(PS[:, 3, 0:256], C("ones"), f(84 + m % 4, 256), m == 0, m == 15, dev["s", m],
                                           sig=True)

        def statistics():
            for m in range(6):
                while len(r1_t) <= m:
                    yield
                yield
                mean_part(m)
            yield
            for m in range(17):
                while m < 16 and len(r1_t) <= m:
                    yield
                if m < 16:
                    deviate(m)
                yield
                if m:
                    add_part(m - 1)

        st_ = statistics()
        for m in range(16):
            b = m % 2
            for _ in unit(Z3, R3, b, x2_t[15], free[b], tiles=x2_t if m == 0 else None):
                next(st_, None)
            free[b] = stt(tile(X1, m), tile(X1, m), ALPHA, PS[:, b, 0:256], ALU.mult, ALU.add, unit_done[0])
            r1_t.append(free[b])
        drain(st_)
        mix_pe = unit_done[0]

        t = stat[0]
        a = act(MU, PS[:, 2, 0:256], ACT.Copy, t, att[0], scale=1.0 / 2048)
        b_ = tt(V, RS, MU, MU, ALU.mult, a)
        b_ = stt(RS, PS[:, 3, 0:256], 1.0 / 2048, RS, ALU.mult, ALU.subtract, t, b_)
        b_ = ts(V, RS, RS, 0.0, None, ALU.max, None, b_)
        s_ = act(RS, RS, ACT.Sqrt, b_, bias=C("eps5"))
        s_ = recip(RS, RS, s_)
        mr = tt(V, MR, MU, RS, ALU.mult, s_)
        H2H, H2L = r(0, 4096), r(16, 4096)
        hh_t = []
        his = []
        for c in range(9):
            if c < 8:
                x = k3(X1)[:, 2 * c:2 * c + 2, :]
                a = tt(V, x, x, bc(RS, 2), ALU.mult, s_)
                a = tt(V, x, x, bc(MR, 2), ALU.subtract, a, mr)
            if c:
                o = slice(512 * c - 512, 512 * c)
                hh_t += 2 * [tt(V, H2L[:, o], X1[:, o], H2H[:, o].bitcast(F), ALU.subtract, his[-1])]
            if c < 8:
                for kt in range(2 * c, 2 * c + 2):
                    b_ = act(tile(X1, kt), tile(X1, kt), ACT.Identity, a, scale=vc("ln1g", kt), bias=vc("ln1b", kt))
                his.append(acopy(tile(H2H, 2 * c, 2), tile(X1, 2 * c, 2), b_))
        E3, O3 = k3(H2H), k3(H2L)
        stg = f(104, 4096).rearrange("p (a d) -> p a d", a=2)
        bb = {i: (bk[i] if i > 3 else s_) for i in range(2, 8)}

        def h_out():
            it = 0
            for p in range(2):
                for c in range(4):
                    kb_ = 4 + it % 4
                    it += 1
                    for k in range(4):
                        t = tr(PS[:, kb_, k * 128:k * 128 + 128], tile(X1, 4 * c + k)[:, p * 128:p * 128 + 128], hh_t[-1],
                               bb[kb_], sig=(k == 3))
                    yield
                    bb[kb_] = acopy(stg[:, p, c * 512:c * 512 + 512], PS[:, kb_, :], t, mix_pe)
            h_tr.append(t)
            t_sc_.append(load(G, scratch["h"], stg, bb[kb_], store=True))

        h_tr, t_sc_ = [], []
        ho = h_out()
        SUB = f(92, 256).rearrange("p (s k) -> p s k", s=2)
        t_sub = load(G, SUB, D["sub"], mix_pe, x2_t[7])
        QH = f(76, 4096)
        ST = f(60, 4096).rearrange("p (a s h k) -> p a s h k", a=2, s=2, h=8)
        CAND, WRK = f(32, 2048), f(40, 2048)
        VAL, IDX, IDF = f(48, 512), f(50, 512).bitcast(U32), f(52, 512)
        val = VAL.rearrange("p (q k) -> p q k", k=16)
        idx = IDX.rearrange("p (q k) -> p q k", k=16)
        idf = IDF.rearrange("p (q k) -> p q k", k=16)
        BST, POS = f(54, 128), f(54.5, 128).bitcast(U32)
        POA, POB = f(55, 128), f(55.5, 128)
        PUA = f(56, 128).bitcast(U32)
        SEL = f(56.5, 128)
        I1T, I2T, GTT = f(57, 256), f(58, 256), f(59, 256)
        sel_done = []

        def top16(vals, v16, i16, wk, *t):
            a = V.do(lambda e: e.max(out=v16[:, 0:8], in_=vals), *t)
            V.do(lambda e: e.max_index(out=i16[:, 0:8], in_max=v16[:, 0:8], in_values=vals), a)
            c = V.do(lambda e: e.match_replace(out=wk, in_to_replace=v16[:, 0:8], in_values=vals, imm_value=-3e38), a)
            d = V.do(lambda e: e.max(out=v16[:, 8:16], in_=wk), c)
            return V.do(lambda e: e.max_index(out=i16[:, 8:16], in_max=v16[:, 8:16], in_values=wk), d)

        def key_steps():
            for hs in range(16):
                while len(s_t) <= hs:
                    yield
                for p in range(2):
                    o = (2 * hs + p) % 16 * 128
                    top_t[p] = top16(ST[:, p, hs % 2, hs // 2, :], val[:, 16 * p + hs, :], idx[:, 16 * p + hs, :],
                                     WRK[:, o:o + 128], s_t[hs][0], h_tr[0], mix_pe)
                    yield

        top_t = {}

        def select(last):
            yield from last
            v4 = val.rearrange("p (a q) k -> p a q k", a=2)
            i4 = idf.rearrange("p (a q) k -> p a q k", a=2)
            cand = CAND.rearrange("p (h a b) -> p h a b", h=8, a=16)
            bst = BST.rearrange("p (h k) -> p h k", k=16)
            pos = POS.rearrange("p (h k) -> p h k", k=16)
            hot = CAND.rearrange("p (k a) -> p k a", a=16)
            sel3 = SEL.rearrange("p (h k) -> p h k", k=16)
            prev = vcopy(IDF, IDX, top_t[0], top_t[1])
            for p in range(2):
                for h in range(8):
                    c = tt(V, cand[:, h, :, :], bc(v4[:, p, 2 * h, :], 16, 2), bc(v4[:, p, 2 * h + 1, :], 16), ALU.add,
                           prev)
                    if h % 4 == 3:
                        yield
                for h in range(8):
                    t = top16(CAND[:, h * 256:h * 256 + 256], bst[:, h, :], pos[:, h, :],
                              WRK[:, h * 256:h * 256 + 256], c)
                    yield
                a = ts(V, PUA, POS, 4, None, ALU.logical_shift_right, None, t)
                a = vcopy(POA, PUA, a)
                b = ts(V, PUA, POS, 15, None, ALU.bitwise_and, None, a)
                b = vcopy(POB, PUA, b)
                out_ = t
                for which, P_ in ((0, POA), (1, POB)):
                    c = tt(V, hot, bc(P_, 16, 2), bc(C("iota16"), 128), ALU.is_equal, a, b, out_)
                    yield
                    yield
                    for h in range(8):
                        c2 = tt(V, hot[:, 16 * h:16 * h + 16, :], hot[:, 16 * h:16 * h + 16, :],
                                bc(i4[:, p, 2 * h + which, :], 16), ALU.mult, c)
                        if h == 3:
                            yield
                    yield
                    c = V.do(lambda e: e.tensor_reduce(SEL, hot, AX.X, ALU.add), c2, out_)
                    yield
                    yield
                    t3 = tr(PS[:, 2, which * 128:which * 128 + 128], SEL, c, bb[2], sig=True)
                    yield
                    out_ = bb[2] = vcopy((I1T, I2T)[which][:, p * 128:p * 128 + 128],
                                         PS[:, 2, which * 128:which * 128 + 128], t3)
                a = tt(V, sel3, bst, bst[:, :, 0:1].broadcast_to([128, 8, 16]), ALU.subtract, out_)
                a = act(SEL, SEL, ACT.Exp, a)
                yield
                sm_ = POA[:, 0:8]
                b = V.do(lambda e: e.tensor_reduce(sm_, sel3, AX.X, ALU.add), a)
                b = recip(sm_, sm_, b)
                b = tt(V, sel3, sel3, bc(sm_, 16, 2), ALU.mult, b)
                t3 = tr(PS[:, 2, 256:384], SEL, b, bb[2], sig=True)
                yield
                bb[2] = prev = vcopy(GTT[:, p * 128:p * 128 + 128], PS[:, 2, 256:384], t3)
            sel_done.append(prev)

        s_t = []
        pend = key_steps()
        for i in range(16):
            b = i % 2
            n_ = 0
            for _ in unit(E3, O3, b, free[b], tiles=hh_t if i == 0 else None):
                n_ += 1
                if 1 <= i < 5 and n_ % 2:
                    next(ho, None)
                if i >= 5 and n_ < 4:
                    next(pend)
            if i == 4:
                drain(ho)
            free[b] = a = acopy(f(76 + (i % 4), 256), PS[:, b, 0:256], unit_done[0], s_t[i - 4][1] if i >= 4 else mix_pe,
                                hh_t[-1])
            kb_ = 2 + i % 2
            for p in range(2):
                t = mm(PS[:, kb_, p * 128:p * 128 + 128], f(76 + (i % 4), 256)[:, p * 128:p * 128 + 128], SUB[:, i % 2, :],
                       True, True, a, t_sub, bb[kb_], sig=(p == 1))
            bb[kb_] = a = acopy(ST[:, :, i % 2, i // 2, :], PS[:, kb_, 0:256].rearrange("p (a k) -> p a k", a=2), t, mix_pe)
            s_t.append((a, t))

        qh_pe = s_t[-1][1]

        CC = f(76, 16384)
        C3 = CC.rearrange("p (j t) -> p j t", t=256)
        ACC = f(60, 4096)
        O1 = f(32, 2048).rearrange("p (b k i) -> p b k i", b=4, k=4)
        O2 = f(40, 1024).rearrange("p (b k i) -> p b k i", b=4, k=4)
        CTH, CTL = r(44, 512), r(46, 512)
        GT = f(48, 512)
        sel = select(pend)
        pe_free = {"o": [None] * 4, "ct": [None, None], "gt": [None, None]}
        c_free = [t_sc_[0], qh_pe]
        hot_t, mm_t = {}, {}
        quad_last = [None]
        gelu_last = [None]

        def gate_hots(q, half):
            ob = q % 4
            for k in range(4):
                t = 4 * q + k
                ts(V, O1[:, ob, k, :], C("iota"), I1T[:, t:t + 1], GTT[:, t:t + 1], ALU.is_equal, ALU.mult,
                   sel_done[0], pe_free["o"][ob])
            hot_t[q] = tt(V, O2[:, ob, :, :], bc(C("iota")[:, 64 * half:64 * half + 64], 4), bc(I2T[:, 4 * q:4 * q + 4], 64, 2),
                          ALU.is_equal)

        def gate_mm(q):
            ob, bank = q % 4, 3 + q % 4
            for k in range(4):
                m = mm(PS[:, bank, k * 64:k * 64 + 64], O1[:, ob, k, :], O2[:, ob, k, :], True, True, hot_t[q], bb[bank],
                       sig=(k == 3))
            pe_free["o"][ob] = mm_t[q] = m

        def gate_apply(q, jdone):
            bank = 3 + q % 4
            g = PS[:, bank, 0:256].rearrange("p (t j) -> p j t", t=4)
            tcol = slice(4 * q, 4 * q + 4)
            x = mm_t[q]
            if jdone:
                x = tt(V, C3[:, 0:jdone, tcol], C3[:, 0:jdone, tcol], g[:, 0:jdone, :], ALU.mult, x, gelu_last[0])
            if jdone < 64:
                x = vcopy(C3[:, jdone:64, tcol], g[:, jdone:64, :], x, *c_free)
            bb[bank] = quad_last[0] = x

        v_evac = {}
        seln = 0.0
        for half in range(2):
            hots = mms = applied = 0
            quad_last[0] = None
            gm = None
            for j in range(64):
                b = j % 2
                due = 64 if j >= 60 else (j + 2 if half else int(64 * max(0, j - 25) / 35))
                due = min(due, hots + 2, 64) if sel_done else 0
                work = [lambda q=q: gate_apply(q, j) for q in range(applied, mms)]
                work += [lambda q=q: gate_mm(q) for q in range(mms, hots)]
                work += [lambda q=q: gate_hots(q, half) for q in range(hots, due)]
                applied, mms, hots = mms, hots, max(due, hots)
                for x in unit(E3, O3, b, free[b], per=6):
                    seln += SEL_RATE
                    if half == 0 and not sel_done and seln >= 1:
                        seln -= 1
                        next(sel, None)
                    if work:
                        work.pop(0)()
                for x in work:
                    x()
                tq = 4 * applied
                gtmp = GT[:, b * 256:b * 256 + 256]
                if tq:
                    ga = free[b] = act(gtmp[:, 0:tq], PS[:, b, 0:tq], ACT.Gelu, unit_done[0], pe_free["gt"][b])
                if tq < 256:
                    free[b] = gelu_last[0] = act(C3[:, j, tq:256], PS[:, b, tq:256], ACT.Gelu, unit_done[0], *c_free)
                if tq:
                    pe_free["gt"][b] = gm = tt(G, C3[:, j, 0:tq], C3[:, j, 0:tq], gtmp[:, 0:tq], ALU.mult, ga,
                                               quad_last[0])
            while applied < 64:
                for q in range(applied, mms):
                    gate_apply(q, 64)
                for q in range(mms, hots):
                    gate_mm(q)
                for q in range(hots, min(hots + 2, 64)):
                    gate_hots(q, half)
                applied, mms, hots = mms, hots, min(hots + 2, 64)
            start_wait = [bb[i] for i in range(2, 8)] + [free[0], free[1]]
            if half:
                HN, LG, LB = f(0, 4096), f(16, 2048), f(24, 2048)
                t_h = load(G, HN, scratch["h"].rearrange("p a d -> p (a d)"), unit_done[0], t_sc_[0])
                t_g = load(G, LG, D["ln2g"], unit_done[0])
                t_b = load(G, LB, D["ln2b"])
            split_t = {}

            def split(j):
                c = j % 2
                ch, cl_ = CTH[:, c * 256:c * 256 + 256], CTL[:, c * 256:c * 256 + 256]
                hi = acopy(ch, C3[:, j, :], quad_last[0], gm, pe_free["ct"][c])
                split_t[j] = hi, tt(V, cl_, C3[:, j, :], ch.bitcast(F), ALU.subtract, hi)

            split(0)
            for j in range(64):
                if half and j >= 8 and j % 8 == 0 and j < 40:
                    x = quarter(ACC, j // 8 - 1)
                    t_res = stt(x, quarter(HN, j // 8 - 1), ALPHA, x, ALU.mult, ALU.add, t_h, v_evac[7], v_evac[6])
                n = un[0]
                un[0] += 1
                c = j % 2
                ch, cl_ = CTH[:, c * 256:c * 256 + 256], CTL[:, c * 256:c * 256 + 256]
                hi, lo = split_t[j]
                for h in range(2):
                    if h and j < 63:
                        split(j + 1)
                    prep_ahead(n, h)
                    kk_ = (n % 2) * 2 + h
                    for tp in range(2):
                        cth, ctl = ch[:, tp * 128:tp * 128 + 128], cl_[:, tp * 128:tp * 128 + 128]
                        for lhs, W, st_, sp_ in ((cth, WH, True, False), (cth, WL, False, False), (ctl, WH, False, True)):
                            for d in range(2):
                                m = mm(PS[:, 4 * tp + 2 * h + d, :], lhs, W[:, kk_, d * 512:d * 512 + 512],
                                       st_ and j == 0, sp_ and j == 63, lo, ready[(n, h)], *start_wait,
                                       sig=(d == 1 and sp_))
                    used[(n, h)] = m
                start_wait = []
                pe_free["ct"][c] = m
            vdone = m
            if half == 0:
                for i in range(8):
                    if i % 2:
                        e_ = acopy(ACC[:, i * 512:i * 512 + 512], PS[:, i, :], vdone, sel_done[0])
                    else:
                        e_ = vcopy(ACC[:, i * 512:i * 512 + 512], PS[:, i, :], vdone)
                    if i < 2:
                        free[i] = e_
                    else:
                        bb[i] = e_
                    v_evac[i] = e_
                c_free = [lo, hi]

        mu = f(50, 32)
        col = lambda i: mu[:, i:i + 1]
        X = [ACC[:, p * 2048:p * 2048 + 2048] for p in range(2)]
        t = t_res
        for p in range(2):
            for d in range(4):
                x = X[p][:, d * 512:d * 512 + 512]
                t = tt(V, x, x, PS[:, 4 * p + d, :], ALU.add, t, vdone, gm)
                a = act(HN[:, p * 2048 + d * 512:p * 2048 + d * 512 + 512], x, ACT.Identity, t, t_res, acc=col(4 * p + d))
            t = V.do(lambda e, p=p: e.tensor_reduce(col(8 + p), mu[:, 4 * p:4 * p + 4], AX.X, ALU.add), a)
            m_ = ts(V, col(10 + p), col(8 + p), -1.0 / 2048, None, ALU.mult, None, t)
            a = act(HN[:, p * 2048:p * 2048 + 2048], X[p], ACT.Square, m_, bias=col(10 + p), acc=col(12 + p))
            t = m_
        a = act(mu[:, 14:16], mu[:, 12:14], ACT.Sqrt, a, scale=1.0 / 2048, bias=C("eps5"))
        rs = recip(mu[:, 16:18], mu[:, 14:16], a)
        for p in range(2):
            for c in range(2):
                o = slice(1024 * c, 1024 * c + 1024)
                x = X[p][:, o]
                a = stt(x, x, col(10 + p), LG[:, o], ALU.add, ALU.mult, rs, t_g)
                a = stt(x, x, col(16 + p), LB[:, o], ALU.mult, ALU.add, a, t_b)
                load(SP if c else A, out[0, p * 128:p * 128 + 128, o], x, a, store=True)

        finish()


def layout(inputs):
    a = {k: np.asarray(v) for k, v in inputs.items()}

    def tiles(w):
        k, c = w.shape
        return np.ascontiguousarray(w.reshape(k // 2048, 16, 128, c // 128, 128).transpose(3, 0, 2, 1, 4)).reshape(
            (k // 2048) * (c // 128), 128, 2048)

    def turned(x):
        return np.ascontiguousarray(x.T.reshape(16, 128, 256).transpose(1, 0, 2)).reshape(128, 4096)

    def cols(g):
        return g.reshape(-1, 128).T

    w = a["dn_w_in"][0]
    w2 = a["w_in_2"][0]
    vec = np.concatenate([
        cols(a["norm_g"][0]), cols(a["mem_norm_g"]),
        a["dn_conv_w"][0].reshape(4, 48, 128).transpose(2, 1, 0).reshape(128, 192),
        cols(a["ln1_g_2"][0]), cols(a["ln1_b_2"][0]), cols(a["xa_q_norm_g"][0]), cols(a["xa_k_norm_g"][0]),
        cols(a["dn_out_norm_g"][0]), cols(a["pool_scale_2"][0]),
        np.broadcast_to(a["dn_a_log"], (128, 24)), np.broadcast_to(a["dn_dt_bias"], (128, 24))], axis=1)
    con, inv, hot = constants()
    order = list(range(8)) + list(range(10, 32, 2)) + list(range(11, 32, 2)) + [8, 9]
    return {
        "con": con, "inv": inv, "hot": hot, "vec": np.ascontiguousarray(vec),
        "xT": turned(a["x"][0]), "memT": turned(a["mem"][0]),
        "w_kv": tiles(a["mem_w_kv"][0]),
        "w_qkv": tiles(w[:, 0:6144]), "w_ab": tiles(w[:, 6144:6272]), "w_xq": tiles(w[:, 6192:7216]),
        "w_z": tiles(w[:, 7216:11312]),
        "w_o": tiles(a["w_out"][0].reshape(32, 128, 2048)[order].reshape(4096, 2048)),
        "w2": tiles(w2[:, 0:5120]),
        "w2_kiwi": tiles(np.concatenate([w2[:, 5120:5200], w2[:, 5072:5120]], axis=1)),
        "rb": a["rel_bias_2"],
        "pw": np.ascontiguousarray(a["pool_w_2"][0].reshape(4, 2, 128, 256).transpose(2, 0, 1, 3)).reshape(128, 2048),
        "w_o2": tiles(a["w_out_2"][0]), "w_q2": tiles(a["peer_wq_2"][0]),
        "sub": np.ascontiguousarray(a["peer_subkeys_2"][0].transpose(2, 0, 1)),
        "pu": np.ascontiguousarray(a["peer_u_2"][0].reshape(128, 128, 16, 128).transpose(1, 3, 2, 0)).reshape(
            128, 128, 2048),
        "pv": np.ascontiguousarray(a["peer_v_2"][0]),
        "ln2g": np.ascontiguousarray(np.broadcast_to(a["ln2_g_2"], (128, 2048))),
        "ln2b": np.ascontiguousarray(np.broadcast_to(a["ln2_b_2"], (128, 2048))),
    }


def kernel(**inputs):
    import concourse.bacc as bacc
    from concourse.bass_utils import run_bass_kernel_spmd

    nc = bacc.Bacc("TRN2", target_bir_lowering=False, num_devices=1)
    arrays = layout(inputs)
    D = {k: nc.dram_tensor(f"in_{k}", v.shape, mybir.dt.from_np(v.dtype), kind="ExternalInput").ap()
         for k, v in arrays.items()}
    out = nc.dram_tensor("out_0", (1, 256, 2048), F, kind="ExternalOutput").ap()
    scratch = {"bias": nc.dram_tensor("s_bias", (8, 384), F, kind="Internal").ap(),
               "h": nc.dram_tensor("s_h", (128, 2, 2048), F, kind="Internal").ap()}
    build(nc, D, out, scratch)
    res = run_bass_kernel_spmd(nc, [{f"in_{k}": v for k, v in arrays.items()}], core_ids=[0])
    return res.results[0]["out_0"]
```
